# Optimizing a Trainium2 kernel written in Bass

```python
import math
import jax, jax.numpy as jnp
from jax import lax
import numpy as np

D_MODEL = 1024
BATCH = 1
SEQ = 1024
DEPTH = 1

HEAD_DIM = 64
A_Q_HEADS = 8
A_KV_HEADS = 2
A_WIDTH = A_Q_HEADS * HEAD_DIM
A_KV_WIDTH = A_KV_HEADS * HEAD_DIM
WINDOW = 128
BLOCK = 128
B_WIDTH = 256
B_BLOCKS = 4
B_BLOCK_DIM = B_WIDTH // B_BLOCKS
CONV_WIDTH = 4
LRU_C = 8.0
C_HEADS = 4
C_WIDTH = C_HEADS * HEAD_DIM
DECAY_RANK = 32
AICL_RANK = 32
VRES_RANK = 16
C_SHIFT_WIDTH = 3 * C_WIDTH + DECAY_RANK + AICL_RANK
GN_EPS = 64e-5

D_MIX = A_WIDTH + B_WIDTH + C_WIDTH
SPLIT_SIZES = (A_WIDTH, A_KV_WIDTH, A_KV_WIDTH, A_WIDTH,
               B_WIDTH, B_WIDTH,
               C_SHIFT_WIDTH, C_WIDTH)
D_IN = sum(SPLIT_SIZES)
LN_EPS = 1e-5
ALPHA = (2 * DEPTH) ** 0.25
BETA = (8 * DEPTH) ** -0.25


def _layer_norm(x, g, b):
    xf = x.astype(jnp.float32)
    mu = jnp.mean(xf, axis=-1, keepdims=True)
    var = jnp.mean(jnp.square(xf - mu), axis=-1, keepdims=True)
    return (xf - mu) * lax.rsqrt(var + LN_EPS) * g + b

def _swa_sinks(q, k, v, sinks):
    bsz, seq = q.shape[0], q.shape[1]
    nb = seq // BLOCK
    grp = A_Q_HEADS // A_KV_HEADS
    qb = q.astype(jnp.float32).reshape(bsz, nb, BLOCK, A_KV_HEADS, grp, HEAD_DIM) * (HEAD_DIM ** -0.5)

    def band(t):
        t = t.astype(jnp.float32).reshape(bsz, seq, A_KV_HEADS, HEAD_DIM)
        prev = jnp.pad(t, ((0, 0), (BLOCK, 0), (0, 0), (0, 0)))[:, :seq]
        prev = prev.reshape(bsz, nb, BLOCK, A_KV_HEADS, HEAD_DIM)
        cur = t.reshape(bsz, nb, BLOCK, A_KV_HEADS, HEAD_DIM)
        return jnp.concatenate([prev, cur], axis=2)

    kb, vb = band(k), band(v)
    s = jnp.einsum("bnqhgd,bnkhd->bnhgqk", qb, kb)
    qi = jnp.arange(BLOCK)[:, None]
    kj = jnp.arange(2 * BLOCK)[None, :]
    diff = qi + BLOCK - kj
    band_mask = (diff >= 0) & (diff < WINDOW)
    key_pos = jnp.arange(nb)[:, None] * BLOCK - BLOCK + jnp.arange(2 * BLOCK)[None, :]
    mask = band_mask[None] & (key_pos >= 0)[:, None, :]
    s = jnp.where(mask[None, :, None, None], s, -jnp.inf)
    sink = sinks.astype(jnp.float32).reshape(A_KV_HEADS, grp)[None, None, :, :, None, None]
    m = jnp.maximum(jnp.max(s, axis=-1, keepdims=True), sink)
    p = jnp.exp(s - m)
    denom = jnp.sum(p, axis=-1, keepdims=True) + jnp.exp(sink - m)
    o = jnp.einsum("bnhgqk,bnkhd->bnqhgd", p / denom, vb)
    return o.reshape(bsz, seq, A_WIDTH)

def _rg_lru(xb, conv_w, conv_b, wa, ba, wx, bx, lam):
    bsz, seq = xb.shape[0], xb.shape[1]
    xf = xb.astype(jnp.float32)
    xc = lax.conv_general_dilated(
        xf, conv_w.astype(jnp.float32).reshape(CONV_WIDTH, 1, B_WIDTH),
        window_strides=(1,), padding=[(CONV_WIDTH - 1, 0)],
        dimension_numbers=("NWC", "WIO", "NWC"), feature_group_count=B_WIDTH) + conv_b
    xh = xc.reshape(bsz, seq, B_BLOCKS, B_BLOCK_DIM)
    r = jax.nn.sigmoid(jnp.einsum("bsnd,nde->bsne", xh, wa).reshape(bsz, seq, B_WIDTH) + ba)
    i = jax.nn.sigmoid(jnp.einsum("bsnd,nde->bsne", xh, wx).reshape(bsz, seq, B_WIDTH) + bx)
    log_a = -LRU_C * r * jax.nn.softplus(-lam.astype(jnp.float32))
    a = jnp.exp(log_a)
    u = jnp.sqrt(-jnp.expm1(2.0 * log_a)) * (i * xc)

    def combine(e1, e2):
        a1, b1 = e1
        a2, b2 = e2
        return a1 * a2, a2 * b1 + b2

    _, h = lax.associative_scan(combine, (a, u), axis=1)
    return h

def _rwkv7(cs, mu, w0, w2, a0, a2, k_k, k_a, r_k, gn_w, gn_b, vres):
    bsz, seq = cs.shape[0], cs.shape[1]
    cs = cs.astype(jnp.float32)
    prev = jnp.pad(cs, ((0, 0), (1, 0), (0, 0)))[:, :seq]
    xs = cs + (prev - cs) * mu
    r, k, v, wl, al = jnp.split(xs, [C_WIDTH, 2 * C_WIDTH, 3 * C_WIDTH, 3 * C_WIDTH + DECAY_RANK], axis=-1)
    logw = -jax.nn.softplus(-(w0 + jnp.tanh(wl) @ w2)) - 0.5
    decay = jnp.exp(-jnp.exp(logw))
    a = jax.nn.sigmoid(a0 + al @ a2)
    v_own = v
    if vres is not None:
        v_first, v0, v1, v2 = vres
        v = v + (v_first - v) * jax.nn.sigmoid(v0 + (v @ v1) @ v2)

    def heads(t):
        return t.reshape(bsz, seq, C_HEADS, HEAD_DIM)

    kk = heads(k * k_k)
    kk = kk * lax.rsqrt(jnp.sum(jnp.square(kk), axis=-1, keepdims=True) + 1e-12)
    k = k * (1.0 + (a - 1.0) * k_a)
    rh, wh, kh, vh, ah = heads(r), heads(decay), heads(k), heads(v), heads(a)
    bh = kk * ah

    def step(state, inp):
        r_t, w_t, k_t, v_t, kk_t, b_t = inp
        sa = jnp.einsum("bhvk,bhk->bhv", state, -kk_t)
        state = (state * w_t[:, :, None, :] + sa[..., None] * b_t[:, :, None, :]
                 + v_t[..., None] * k_t[:, :, None, :])
        y_t = jnp.einsum("bhvk,bhk->bhv", state, r_t)
        return state, y_t

    tm = lambda t: jnp.swapaxes(t, 0, 1)
    s0 = jnp.zeros((bsz, C_HEADS, HEAD_DIM, HEAD_DIM), jnp.float32)
    _, y = lax.scan(step, s0, (tm(rh), tm(wh), tm(kh), tm(vh), tm(kk), tm(bh)))
    y = tm(y)
    ym = jnp.mean(y, axis=-1, keepdims=True)
    yv = jnp.mean(jnp.square(y - ym), axis=-1, keepdims=True)
    y = (y - ym) * lax.rsqrt(yv + GN_EPS) * gn_w.reshape(C_HEADS, HEAD_DIM) + gn_b.reshape(C_HEADS, HEAD_DIM)
    bonus = jnp.sum(rh * kh * r_k, axis=-1, keepdims=True) * vh
    return (y + bonus).reshape(bsz, seq, C_WIDTH), v_own

def first_inputs(seed: int = 0) -> dict:
    key = jax.random.key(seed)
    ks = jax.random.split(key, 32)
    n = lambda i, shape: jax.random.normal(ks[i], shape, jnp.float32)
    u_lru = jax.random.uniform(ks[11], (DEPTH, B_WIDTH), jnp.float32, 0.9, 0.999)
    a_base = u_lru ** (1.0 / LRU_C)
    w0_base = jnp.linspace(-6.0, -1.0, C_WIDTH, dtype=jnp.float32)[None, :]
    return {
        "x": n(0, (BATCH, SEQ, D_MODEL)),
        "w_in": n(1, (DEPTH, D_MODEL, D_IN)) * D_MODEL ** -0.5,
        "w_out": n(2, (DEPTH, D_MIX, D_MODEL)) * (D_MIX ** -0.5) * BETA,
        "ln_g": 1.0 + 0.02 * n(3, (DEPTH, D_MODEL)),
        "ln_b": 0.02 * n(4, (DEPTH, D_MODEL)),
        "attn_sinks": 0.5 * n(5, (DEPTH, A_Q_HEADS)),
        "conv_w": n(6, (DEPTH, CONV_WIDTH, B_WIDTH)) * CONV_WIDTH ** -0.5,
        "conv_b": 0.02 * n(7, (DEPTH, B_WIDTH)),
        "lru_wa": n(8, (DEPTH, B_BLOCKS, B_BLOCK_DIM, B_BLOCK_DIM)) * B_BLOCK_DIM ** -0.5,
        "lru_ba": 0.02 * n(9, (DEPTH, B_WIDTH)),
        "lru_wx": n(10, (DEPTH, B_BLOCKS, B_BLOCK_DIM, B_BLOCK_DIM)) * B_BLOCK_DIM ** -0.5,
        "lru_bx": 0.02 * n(12, (DEPTH, B_WIDTH)),
        "lru_lambda": jnp.log(a_base) - jnp.log1p(-a_base),
        "rwkv_mu": jax.random.uniform(ks[13], (DEPTH, C_SHIFT_WIDTH), jnp.float32),
        "rwkv_w0": w0_base + 0.1 * n(14, (DEPTH, C_WIDTH)),
        "rwkv_w2": 0.1 * n(15, (DEPTH, DECAY_RANK, C_WIDTH)),
        "rwkv_a0": 0.1 * n(16, (DEPTH, C_WIDTH)),
        "rwkv_a2": 0.1 * n(17, (DEPTH, AICL_RANK, C_WIDTH)),
        "rwkv_kk": 0.85 + 0.02 * n(18, (DEPTH, C_WIDTH)),
        "rwkv_ka": 1.0 + 0.02 * n(19, (DEPTH, C_WIDTH)),
        "rwkv_rk": -0.04 + 0.02 * n(20, (DEPTH, C_HEADS, HEAD_DIM)),
        "rwkv_gn_w": 1.0 + 0.02 * n(21, (DEPTH, C_WIDTH)),
        "rwkv_gn_b": 0.02 * n(22, (DEPTH, C_WIDTH)),
        "rwkv_v0": 1.0 + 0.1 * n(23, (DEPTH - 1, C_WIDTH)),
        "rwkv_v1": n(24, (DEPTH - 1, C_WIDTH, VRES_RANK)) * C_WIDTH ** -0.5,
        "rwkv_v2": 0.1 * n(25, (DEPTH - 1, VRES_RANK, C_WIDTH)),
    }

def first_block(x, w_in, w_out, ln_g, ln_b, attn_sinks, conv_w, conv_b, lru_wa, lru_ba,
              lru_wx, lru_bx, lru_lambda, rwkv_mu, rwkv_w0, rwkv_w2, rwkv_a0, rwkv_a2,
              rwkv_kk, rwkv_ka, rwkv_rk, rwkv_gn_w, rwkv_gn_b, rwkv_v0, rwkv_v1, rwkv_v2):
    split_idx = [int(c) for c in np.cumsum(SPLIT_SIZES)[:-1]]
    v_first = None
    for l in range(DEPTH):
        proj = jnp.einsum("bsd,de->bse", x, w_in[l])
        q, k, v, g_a, x_b, g_b, c_cols, g_c = jnp.split(proj, split_idx, axis=-1)
        y_a = _swa_sinks(q, k, v, attn_sinks[l])
        y_b = _rg_lru(x_b, conv_w[l], conv_b[l], lru_wa[l], lru_ba[l], lru_wx[l], lru_bx[l], lru_lambda[l])
        vres = None if l == 0 else (v_first, rwkv_v0[l - 1], rwkv_v1[l - 1], rwkv_v2[l - 1])
        y_c, v_own = _rwkv7(c_cols, rwkv_mu[l], rwkv_w0[l], rwkv_w2[l], rwkv_a0[l], rwkv_a2[l],
                            rwkv_kk[l], rwkv_ka[l], rwkv_rk[l], rwkv_gn_w[l], rwkv_gn_b[l], vres)
        if l == 0:
            v_first = v_own
        silu = lambda t: jax.nn.silu(t.astype(jnp.float32))
        y = jnp.concatenate([y_a * silu(g_a), y_b * silu(g_b), y_c * silu(g_c)], axis=-1)
        out = jnp.einsum("bse,ed->bsd", y, w_out[l])
        x = _layer_norm(ALPHA * x.astype(jnp.float32) + out, ln_g[l], ln_b[l]).astype(x.dtype)
    return x


_first_inputs = first_inputs


def first_inputs(seed=0):
    import zlib

    import numpy as np

    out = dict(_first_inputs(seed))
    spreads = {}
    factors = {'ln_g': 3.001,
     'ln_b': 2.876,
     'attn_sinks': 8.0,
     'conv_b': 3.874,
     'lru_ba': 8.0,
     'lru_bx': 8.0,
     'rwkv_w2': 8.0,
     'rwkv_a0': 8.0,
     'rwkv_kk': 8.0,
     'rwkv_ka': 8.0,
     'rwkv_rk': 8.0,
     'rwkv_gn_w': 8.0,
     'rwkv_gn_b': 8.0}
    for name, (base, spread) in spreads.items():
        noise = np.random.default_rng([zlib.crc32(name.encode()), seed]).standard_normal(out[name].shape)
        drawn = base * np.exp(spread * noise) if base else spread * noise
        out[name] = __import__('jax').numpy.asarray(drawn.astype(out[name].dtype))
    for name, factor in factors.items():
        out[name] = (out[name] * factor).astype(out[name].dtype)
    return out


_narrow_inputs = first_inputs


def first_inputs(seed=0):

    out = dict(_narrow_inputs(seed))
    wider = {'ln_g': 3.38,
     'ln_b': 3.38,
     'attn_sinks': 9.41,
     'lru_ba': 12.0,
     'lru_bx': 12.0,
     'rwkv_kk': 10.69,
     'rwkv_ka': 3.1,
     'rwkv_gn_w': 4.38,
     'rwkv_gn_b': 4.66}
    for name, times in wider.items():
        mean = out[name].mean()
        out[name] = (mean + times * (out[name] - mean)).astype(out[name].dtype)
    return out


DEPTH_2 = 2

N_META = 16
N_A_LAYERS = DEPTH_2 // 2
N_B_LAYERS = DEPTH_2 - N_A_LAYERS
CONV_W = 3
N_HEADS = 8
QK_NOPE_DIM = 128
QK_ROPE_DIM = 64
V_DIM = 128
Q_RANK = 384
KV_RANK = 256
ROPE_THETA = 10000.0
Q_BLOCK = 128
N_GROUPS = 8
EXPERTS_PER_GROUP = 8
N_EXPERTS = N_GROUPS * EXPERTS_PER_GROUP
TOP_K_IN_GROUP = 2
D_EXPERT = 256
EXPERT_BLOCK = 128
NORM_EPS = 1e-6


def rmsnorm(x, g):
    xf = x.astype(jnp.float32)
    y = xf * lax.rsqrt(jnp.mean(xf * xf, axis=-1, keepdims=True) + NORM_EPS)
    return (y * g.astype(jnp.float32)).astype(x.dtype)

def rope_tables(t):
    inv = ROPE_THETA ** (-jnp.arange(0, QK_ROPE_DIM, 2, dtype=jnp.float32) / QK_ROPE_DIM)
    ang = jnp.arange(t, dtype=jnp.float32)[:, None] * inv[None, :]
    return jnp.cos(ang), jnp.sin(ang)

def apply_rope(x, cos, sin):
    half = x.shape[-1] // 2
    x1, x2 = x[..., :half], x[..., half:]
    cos = cos.astype(x.dtype)
    sin = sin.astype(x.dtype)
    return jnp.concatenate([x1 * cos - x2 * sin, x1 * sin + x2 * cos], axis=-1)

def short_conv_mixer(hn, w_in, conv_w, w_out):
    bcu = hn @ w_in
    b, c, u = jnp.split(bcu, 3, axis=-1)
    z = c * u
    z = lax.conv_general_dilated(z, conv_w.astype(z.dtype), window_strides=(1,),
                                 padding=((CONV_W - 1, 0),),
                                 dimension_numbers=('NWC', 'WIO', 'NWC'),
                                 feature_group_count=z.shape[-1])
    return (b * z) @ w_out

def shared_kv_side(h, kv_g, w_dkv, ckv_g, w_ukv, cos, sin):
    bsz, t, _ = h.shape
    a = rmsnorm(h, kv_g) @ w_dkv
    c_kv = rmsnorm(a[..., :KV_RANK], ckv_g)
    k_rope = apply_rope(a[..., KV_RANK:], cos, sin)
    kv = (c_kv @ w_ukv).reshape(bsz, t, N_HEADS, QK_NOPE_DIM + V_DIM)
    return kv[..., :QK_NOPE_DIM], k_rope, kv[..., QK_NOPE_DIM:]

def causal_block_attention(q_nope, q_rope, k_nope, k_rope, v):
    bsz, t, nh, _ = q_nope.shape
    nqb = -(-t // Q_BLOCK)
    pad = nqb * Q_BLOCK - t
    def blocks(q):
        q = jnp.pad(q, ((0, 0), (0, pad), (0, 0), (0, 0)))
        return q.reshape(bsz, nqb, Q_BLOCK, nh, q.shape[-1]).transpose(1, 0, 2, 3, 4)
    qn, qr = blocks(q_nope), blocks(q_rope)
    kpos = jnp.arange(t)
    scale = (QK_NOPE_DIM + QK_ROPE_DIM) ** -0.5
    def one_block(args):
        qn_b, qr_b, j = args
        qpos = j * Q_BLOCK + jnp.arange(Q_BLOCK)
        s = (jnp.einsum('bqhd,bkhd->bhqk', qn_b, k_nope)
             + jnp.einsum('bqhd,bkd->bhqk', qr_b, k_rope)).astype(jnp.float32) * scale
        s = jnp.where(kpos[None, :] <= qpos[:, None], s, -jnp.inf)
        p = jax.nn.softmax(s, axis=-1).astype(v.dtype)
        return jnp.einsum('bhqk,bkhd->bqhd', p, v)
    o = lax.map(one_block, (qn, qr, jnp.arange(nqb, dtype=jnp.int32)))
    o = o.transpose(1, 0, 2, 3, 4).reshape(bsz, nqb * Q_BLOCK, nh * v.shape[-1])
    return o[:, :t]

def mla_mixer(hn, w_dq, cq_g, w_uq, w_o, k_nope, k_rope, v, cos, sin):
    bsz, t, _ = hn.shape
    cq = rmsnorm(hn @ w_dq, cq_g)
    q = (cq @ w_uq).reshape(bsz, t, N_HEADS, QK_NOPE_DIM + QK_ROPE_DIM)
    q_nope = q[..., :QK_NOPE_DIM]
    q_rope = apply_rope(q[..., QK_NOPE_DIM:], cos[:, None, :], sin[:, None, :])
    o = causal_block_attention(q_nope, q_rope, k_nope, k_rope, v)
    return o @ w_o

def hier_moe(hn, w_grp, w_exp, w_gate, w_up, w_down):
    bsz, t, d = hn.shape
    n = bsz * t
    xf = hn.reshape(n, d)
    g_logits = (xf @ w_grp).astype(jnp.float32)
    p_grp = jax.nn.softmax(g_logits, axis=-1)
    grp = jnp.argmax(g_logits, axis=-1).astype(jnp.int32)
    p_g = jnp.max(p_grp, axis=-1, keepdims=True)
    e_logits = (xf @ w_exp).astype(jnp.float32).reshape(n, N_GROUPS, EXPERTS_PER_GROUP)
    e_in = jnp.einsum('ng,nge->ne', jax.nn.one_hot(grp, N_GROUPS, dtype=jnp.float32), e_logits)
    top_p, top_i = lax.top_k(jax.nn.softmax(e_in, axis=-1), TOP_K_IN_GROUP)
    gate = p_g * top_p / jnp.sum(top_p, axis=-1, keepdims=True)
    expert = grp[:, None] * EXPERTS_PER_GROUP + top_i.astype(jnp.int32)
    a = n * TOP_K_IN_GROUP
    e_a = expert.reshape(a)
    w_a = gate.reshape(a).astype(hn.dtype)
    tok_a = jnp.repeat(jnp.arange(n, dtype=jnp.int32), TOP_K_IN_GROUP)
    counts = jax.ops.segment_sum(jnp.ones((a,), jnp.int32), e_a, num_segments=N_EXPERTS)
    padded = ((counts + EXPERT_BLOCK - 1) // EXPERT_BLOCK) * EXPERT_BLOCK
    pad_end = jnp.cumsum(padded)
    pad_start = pad_end - padded
    start = jnp.cumsum(counts) - counts
    order = jnp.argsort(e_a)
    e_s = e_a[order]
    dest = pad_start[e_s] + jnp.arange(a, dtype=jnp.int32) - start[e_s]
    n_blocks = (a + N_EXPERTS * (EXPERT_BLOCK - 1) + EXPERT_BLOCK - 1) // EXPERT_BLOCK
    p_slots = n_blocks * EXPERT_BLOCK
    slot_tok = jnp.full((p_slots,), n, jnp.int32).at[dest].set(tok_a[order])
    slot_w = jnp.zeros((p_slots,), hn.dtype).at[dest].set(w_a[order])
    blk_expert = jnp.minimum(jnp.searchsorted(pad_end, jnp.arange(n_blocks, dtype=jnp.int32) * EXPERT_BLOCK,
                                              side='right'), N_EXPERTS - 1).astype(jnp.int32)
    x_pad = jnp.concatenate([xf, jnp.zeros((1, d), xf.dtype)], axis=0)
    xs = x_pad[slot_tok].reshape(n_blocks, EXPERT_BLOCK, d)
    def expert_block(args):
        xb, e = args
        hh = jax.nn.silu(xb @ w_gate[e]) * (xb @ w_up[e])
        return hh @ w_down[e]
    ys = lax.map(expert_block, (xs, blk_expert)).reshape(p_slots, d)
    y = jnp.zeros((n + 1, d), ys.dtype).at[slot_tok].add(ys * slot_w[:, None])[:n]
    return y.reshape(bsz, t, d)

def second_inputs(seed: int = 0) -> dict:
    key = jax.random.key(seed)
    ks = jax.random.split(key, 21)
    def nrm(k, shape, scale):
        return jax.random.normal(k, shape, jnp.float32) * scale
    d = D_MODEL
    return {
        'x': nrm(ks[0], (BATCH, SEQ, d), 1.0),
        'meta_tokens': nrm(ks[1], (N_META, d), 1.0),
        'norm_mix_g': 1.0 + nrm(ks[2], (DEPTH_2, d), 0.02),
        'norm_ffn_g': 1.0 + nrm(ks[3], (DEPTH_2, d), 0.02),
        'conv_w_in': nrm(ks[4], (N_A_LAYERS, d, 3 * d), d ** -0.5),
        'conv_w': nrm(ks[5], (N_A_LAYERS, CONV_W, 1, d), CONV_W ** -0.5),
        'conv_w_out': nrm(ks[6], (N_A_LAYERS, d, d), d ** -0.5),
        'kv_norm_g': 1.0 + nrm(ks[7], (d,), 0.02),
        'w_dkv': nrm(ks[8], (d, KV_RANK + QK_ROPE_DIM), d ** -0.5),
        'ckv_norm_g': 1.0 + nrm(ks[9], (KV_RANK,), 0.02),
        'w_ukv': nrm(ks[10], (KV_RANK, N_HEADS * (QK_NOPE_DIM + V_DIM)), KV_RANK ** -0.5),
        'w_dq': nrm(ks[11], (N_B_LAYERS, d, Q_RANK), d ** -0.5),
        'cq_norm_g': 1.0 + nrm(ks[12], (N_B_LAYERS, Q_RANK), 0.02),
        'w_uq': nrm(ks[13], (N_B_LAYERS, Q_RANK, N_HEADS * (QK_NOPE_DIM + QK_ROPE_DIM)), Q_RANK ** -0.5),
        'w_o': nrm(ks[14], (N_B_LAYERS, N_HEADS * V_DIM, d), (N_HEADS * V_DIM) ** -0.5),
        'w_grp': nrm(ks[15], (DEPTH_2, d, N_GROUPS), d ** -0.5),
        'w_exp': nrm(ks[16], (DEPTH_2, d, N_EXPERTS), d ** -0.5),
        'w_gate': nrm(ks[17], (DEPTH_2, N_EXPERTS, d, D_EXPERT), d ** -0.5),
        'w_up': nrm(ks[18], (DEPTH_2, N_EXPERTS, d, D_EXPERT), d ** -0.5),
        'w_down': nrm(ks[19], (DEPTH_2, N_EXPERTS, D_EXPERT, d), D_EXPERT ** -0.5),
        'final_norm_g': 1.0 + nrm(ks[20], (d,), 0.02),
    }

def second_block(x, meta_tokens, norm_mix_g, norm_ffn_g, conv_w_in, conv_w, conv_w_out,
              kv_norm_g, w_dkv, ckv_norm_g, w_ukv, w_dq, cq_norm_g, w_uq, w_o,
              w_grp, w_exp, w_gate, w_up, w_down, final_norm_g):
    bsz = x.shape[0]
    meta = jnp.broadcast_to(meta_tokens[None].astype(x.dtype), (bsz, N_META, x.shape[-1]))
    h = jnp.concatenate([meta, x], axis=1)
    cos, sin = rope_tables(h.shape[1])
    shared = None
    for i in range(DEPTH_2):
        if i < N_A_LAYERS:
            h = h + short_conv_mixer(rmsnorm(h, norm_mix_g[i]), conv_w_in[i], conv_w[i], conv_w_out[i])
        else:
            if shared is None:
                shared = shared_kv_side(h, kv_norm_g, w_dkv, ckv_norm_g, w_ukv, cos, sin)
            j = i - N_A_LAYERS
            k_nope, k_rope, v = shared
            h = h + mla_mixer(rmsnorm(h, norm_mix_g[i]), w_dq[j], cq_norm_g[j], w_uq[j], w_o[j],
                              k_nope, k_rope, v, cos, sin)
        h = h + hier_moe(rmsnorm(h, norm_ffn_g[i]), w_grp[i], w_exp[i], w_gate[i], w_up[i], w_down[i])
    return rmsnorm(h, final_norm_g)[:, N_META:]


def setup_inputs(seed=0):
    out = dict(first_inputs(seed))
    for name, value in second_inputs(seed + 1).items():
        if name != "x":
            out[name + "_2"] = value
    return out


def reference(
    x, w_in, w_out, ln_g, ln_b, attn_sinks, conv_w, conv_b, lru_wa, lru_ba, lru_wx, lru_bx,
    lru_lambda, rwkv_mu, rwkv_w0, rwkv_w2, rwkv_a0, rwkv_a2, rwkv_kk, rwkv_ka, rwkv_rk,
    rwkv_gn_w, rwkv_gn_b, rwkv_v0, rwkv_v1, rwkv_v2, meta_tokens_2, norm_mix_g_2, norm_ffn_g_2,
    conv_w_in_2, conv_w_2, conv_w_out_2, kv_norm_g_2, w_dkv_2, ckv_norm_g_2, w_ukv_2, w_dq_2,
    cq_norm_g_2, w_uq_2, w_o_2, w_grp_2, w_exp_2, w_gate_2, w_up_2, w_down_2, final_norm_g_2,
):
    x = first_block(
        x, w_in, w_out, ln_g, ln_b, attn_sinks, conv_w, conv_b, lru_wa, lru_ba, lru_wx, lru_bx,
        lru_lambda, rwkv_mu, rwkv_w0, rwkv_w2, rwkv_a0, rwkv_a2, rwkv_kk, rwkv_ka, rwkv_rk,
        rwkv_gn_w, rwkv_gn_b, rwkv_v0, rwkv_v1, rwkv_v2,
    )
    return second_block(
        x, meta_tokens_2, norm_mix_g_2, norm_ffn_g_2, conv_w_in_2, conv_w_2, conv_w_out_2,
        kv_norm_g_2, w_dkv_2, ckv_norm_g_2, w_ukv_2, w_dq_2, cq_norm_g_2, w_uq_2, w_o_2,
        w_grp_2, w_exp_2, w_gate_2, w_up_2, w_down_2, final_norm_g_2,
    )


_drawn_inputs = setup_inputs


def setup_inputs(seed=0):
    import zlib

    import numpy as np

    out = dict(_drawn_inputs(seed))
    spreads = {}
    factors = {'attn_sinks': 3.372,
     'meta_tokens_2': 3.008,
     'norm_mix_g_2': 4.156,
     'norm_ffn_g_2': 5.323,
     'kv_norm_g_2': 8.0,
     'ckv_norm_g_2': 25.189,
     'cq_norm_g_2': 8.0,
     'final_norm_g_2': 7.955}
    for name, (base, spread) in spreads.items():
        noise = np.random.default_rng([zlib.crc32(name.encode()), seed]).standard_normal(out[name].shape)
        drawn = base * np.exp(spread * noise) if base else spread * noise
        out[name] = __import__('jax').numpy.asarray(drawn.astype(out[name].dtype))
    for name, factor in factors.items():
        out[name] = (out[name] * factor).astype(out[name].dtype)
    return out
```

```python
import numpy as np
import concourse.bass as bass
from concourse import mybir
from contextlib import ExitStack

F32 = mybir.dt.float32
I32 = mybir.dt.int32
U32 = mybir.dt.uint32
ALU = mybir.AluOpType
ACT = mybir.ActivationFunctionType
AX = mybir.AxisListType
P = 128
HALF = 64

SEQ = 1024
DM = 1024
KT = DM // P
NB = SEQ // P
PAIRS = 4
KV = 2
G_T, Q_T, K_T, KS_T, XB_T, R_T, CK_T, CV_T, WA_T = 0, 8, 12, 13, 14, 16, 18, 20, 22
PROJ_TILES = 23
GATE_TILES = 8
HEAD_SCALE = 64.0 ** -0.5
MASKED = -1.0e30
CHUNK = 64
NCH = SEQ // CHUNK
LN_EPS = 1e-5
GN_EPS = 64e-5
ALPHA = 2.0 ** 0.25
DECAY_HALF = float(np.exp(-0.5))
RANK = 32


class Chain:

    def __init__(self, eng, sem):
        self.eng, self.sem, self.n = eng, sem, 0

    def __call__(self, ins):
        self.n += 1
        ins.then_inc(self.sem, 1)
        self.eng.wait_ge(self.sem, self.n)

    def hold(self, ins):
        self.n += 1
        ins.then_inc(self.sem, 1)

    def wait(self):
        self.eng.wait_ge(self.sem, self.n)

    def restart(self):
        if self.n:
            self.eng.sem_clear(self.sem)
        self.n = 0


class Phase:

    seen = {}

    def __init__(self, nc, name):
        again = Phase.seen[name] = Phase.seen.get(name, -1) + 1
        self.nc, self.name, self.ctx, self.sems = nc, f"{name}{again}", ExitStack(), []

    def __enter__(self):
        return self

    def __exit__(self, kind, *rest):
        self.ctx.close()
        if kind is None and self.sems:
            self.nc.clear_and_free_semaphores(self.sems)
            self.nc.all_engine_barrier()

    def sb(self, name, shape, dt=F32):
        return self.ctx.enter_context(self.nc.sbuf_tensor(f"{self.name}__{name}", shape, dt))

    def ps(self, name, shape, dt=F32):
        return self.ctx.enter_context(self.nc.psum_tensor(f"{self.name}__{name}", shape, dt))

    def sem(self, name):
        self.sems.append(self.nc.alloc_semaphore(f"{self.name}__{name}"))
        return self.sems[-1]


def col(v):
    return v.rearrange("(p a) -> p a", a=1)


def project(nc, D, proj, vpad):
    with Phase(nc, "prj") as ph:
        xT = ph.sb("xT", [P, KT, SEQ])
        wbuf = ph.sb("w", [P, 2, KT, P])
        wv = ph.sb("wv", [P, KT, P])
        acc = ph.ps("acc", [P, 2, 2, 512])
        vacc = ph.ps("vacc", [P, 2, 512])
        x_loaded, wv_loaded = ph.sem("x_loaded"), ph.sem("wv_loaded")
        w_loaded = [ph.sem("w0_loaded"), ph.sem("w1_loaded")]
        w_used = [ph.sem("w0_used"), ph.sem("w1_used")]
        done = [ph.sem("acc0_done"), ph.sem("acc1_done")]
        freed = [ph.sem("acc0_freed"), ph.sem("acc1_freed")]
        v_done, v_zeroed = ph.sem("v_done"), ph.sem("v_zeroed")
        w_dram = D["w_in_t"]
        with nc.Block() as block:

            @block.sync
            def _(sp):
                for b in range(2):
                    sp.dma_start(wbuf[:, b], w_dram[b]).then_inc(w_loaded[b], 16)
                    for k in range(b, KT, 2):
                        sp.dma_start(xT[:, k], D["xT"][:, k]).then_inc(x_loaded, 16)
                with sp.Fori(0, PROJ_TILES // 2) as i:
                    for b in range(2):
                        sp.wait_ge(w_used[b], i + 1)
                        if b == 0:
                            sp.dma_start(wbuf[:, b], w_dram[bass.ds(2 * i + 2, 1)].rearrange(
                                "a p k c -> (a p) k c")).then_inc(w_loaded[b], 16)
                        else:
                            sp.dma_start(wbuf[:, b], w_dram[bass.ds(2 * i + 3, 1)].rearrange(
                                "a p k c -> (a p) k c")).then_inc(w_loaded[b], 16)
                sp.wait_ge(w_loaded[1], 16 * (PROJ_TILES // 2 + 1))

            def tile(pe, b, count):
                pe.wait_ge(w_loaded[b], 16 * count)
                pe.wait_ge(freed[b], 2 * count)
                for c in range(2):
                    for k in range(KT):
                        last = nc.tensor.matmul(acc[:, b, c], wbuf[:, b, k], xT[:, k, 512 * c:512 * c + 512],
                                                start=(k == 0), stop=(k == KT - 1))
                last.then_inc(done[b], 1)
                pe.wait_ge(done[b], count)
                pe.sem_inc(w_used[b], 1)

            @block.tensor
            def _(pe):
                pe.wait_ge(x_loaded, 16 * KT)
                with pe.Fori(0, PROJ_TILES // 2) as i:
                    for b in range(2):
                        tile(pe, b, i + 1)
                tile(pe, 0, PROJ_TILES // 2 + 1)
                pe.wait_ge(wv_loaded, 16)
                for t in range(NB):
                    for k in range(KT):
                        last = nc.tensor.matmul(vacc[:, t // 4, P * (t % 4):P * (t % 4) + P],
                                                xT[:, k, P * t:P * t + P], wv[:, k],
                                                start=(k == 0), stop=(k == KT - 1))
                last.then_inc(v_done, 1)

            @block.scalar
            def _(act):
                act.dma_start(wv[:], D["w_v_t"]).then_inc(wv_loaded, 16)
                with act.Fori(0, PROJ_TILES // 2) as i:
                    for b in range(2):
                        act.wait_ge(done[b], i + 1)
                        nc.scalar.copy(proj[:, bass.ds(2 * i + b, 1), 0:512].rearrange("p a t -> p (a t)"),
                                       acc[:, b, 0]).then_inc(freed[b], 1)
                act.wait_ge(done[0], PROJ_TILES // 2 + 1)
                nc.scalar.copy(proj[:, PROJ_TILES - 1, 0:512], acc[:, 0, 0]).then_inc(freed[0], 1)

            @block.vector
            def _(dve):
                for b in range(2):
                    dve.sem_inc(freed[b], 2)
                nc.vector.memset(vpad[:], 0.0).then_inc(v_zeroed, 1)
                with dve.Fori(0, PROJ_TILES // 2) as i:
                    for b in range(2):
                        dve.wait_ge(done[b], i + 1)
                        nc.vector.tensor_copy(proj[:, bass.ds(2 * i + b, 1), 512:1024].rearrange("p a t -> p (a t)"),
                                              acc[:, b, 1]).then_inc(freed[b], 1)
                dve.wait_ge(done[0], PROJ_TILES // 2 + 1)
                nc.vector.tensor_copy(proj[:, PROJ_TILES - 1, 512:1024], acc[:, 0, 1]).then_inc(freed[0], 1)
                dve.wait_ge(v_done, 1)
                dve.wait_ge(v_zeroed, 1)
                for g in range(KV):
                    nc.vector.tensor_copy(
                        vpad[:, 1:NB + 1, g, HALF:2 * HALF],
                        vacc[:].rearrange("p a (b c) -> p (a b) c", c=P)[:, :, HALF * g:HALF * g + HALF])


def gates(nc, D, proj):
    with Phase(nc, "gat") as ph:
        with nc.Block() as block:

            @block.scalar
            def _(act):
                for j in range(GATE_TILES):
                    nc.scalar.activation(proj[:, G_T + j], proj[:, G_T + j], ACT.Silu)


def window_attention(nc, D, proj, vpad):
    with Phase(nc, "swa") as ph:
        kd = ph.sb("kd", [P, KV, 2, SEQ + P])
        mask = ph.sb("mask", [P, NB, 2 * P])
        ident = ph.sb("ident", [P, P])
        qs = ph.sb("qs", [P, PAIRS, P])
        vs = ph.sb("vs", [P, 2, KV, 3 * HALF])
        sinks = ph.sb("sinks", [P, 2 * PAIRS])
        nsinks = ph.sb("nsinks", [P, 2 * PAIRS])
        sc = ph.sb("sc", [P, PAIRS, 2, 2 * P])
        mx = ph.sb("mx", [P, PAIRS, 2])
        nm = ph.sb("nm", [P, PAIRS, 2])
        ls = ph.sb("ls", [P, PAIRS, 2])
        es = ph.sb("es", [P, PAIRS, 2])
        den = ph.sb("den", [P, PAIRS, 2])
        rd = ph.sb("rd", [P, PAIRS, 2])
        pT = ph.sb("pT", [P, 2, 4, P])
        s_ps = ph.ps("s", [P, PAIRS, 512])
        t_ps = ph.ps("t", [P, 2, 512])
        o_ps = ph.ps("o", [P, 2, 512])
        const_done, sinks_loaded = ph.sem("const_done"), ph.sem("sinks_loaded")
        mask_done, v_own, a_own = ph.sem("mask_done"), ph.sem("v_own"), ph.sem("a_own")
        staged = ph.sem("staged")
        scored = ph.sem("scored")
        maxed = ph.sem("maxed")
        exped = ph.sem("exped")
        normed = ph.sem("normed")
        turned = ph.sem("turned")
        turned_out = ph.sem("turned_out")
        mixed = ph.sem("mixed")
        gated = ph.sem("gated")
        with nc.Block() as block:

            @block.sync
            def _(sp):
                sp.dma_start(sinks[:], D["attn_sinks"].partition_broadcast(P)).then_inc(sinks_loaded, 16)

            @block.gpsimd
            def _(pool):
                nc.gpsimd.memset(mask[:], 0.0).then_inc(mask_done, 1)
                nc.gpsimd.memset(ident[:], 0.0).then_inc(mask_done, 1)
                pool.wait_ge(mask_done, 2)
                nc.gpsimd.affine_select(out=mask[:, :, 0:P], in_=mask[:, :, 0:P], compare_op=ALU.is_gt,
                                        fill=MASKED, base=0, pattern=[[0, NB], [1, P]],
                                        channel_multiplier=-1).then_inc(mask_done, 1)
                nc.gpsimd.affine_select(out=mask[:, :, P:2 * P], in_=mask[:, :, P:2 * P], compare_op=ALU.is_ge,
                                        fill=MASKED, base=0, pattern=[[0, NB], [-1, P]],
                                        channel_multiplier=1).then_inc(mask_done, 1)
                nc.gpsimd.affine_select(out=ident[:], in_=ident[:], compare_op=ALU.not_equal, fill=1.0,
                                        base=0, pattern=[[-1, P]], channel_multiplier=1).then_inc(mask_done, 1)
                pool.wait_ge(mask_done, 5)
                nc.gpsimd.memset(mask[:, 0, 0:P], MASKED).then_inc(mask_done, 1)

            @block.tensor
            def _(pe):
                pe.wait_ge(mask_done, 6)
                with pe.Fori(0, NB) as i:
                    pe.wait_ge(staged, i + 1)
                    for j in range(PAIRS):
                        g = j // 2
                        nc.tensor.matmul(s_ps[:, j].rearrange("p (a b) -> p a b", a=2), qs[:, j],
                                         kd[:, g, :, bass.ds(i * P, 2 * P)],
                                         start=True, stop=True).then_inc(scored, 1)
                    for j in range(PAIRS):
                        g = j // 2
                        pe.wait_ge(normed, i * PAIRS + j + 1)
                        pe.wait_ge(turned_out, i * PAIRS + j + 1)
                        for c in range(4):
                            last = nc.tensor.transpose(t_ps[:, j % 2, P * c:P * c + P],
                                                       sc[:, j, c // 2, P * (c % 2):P * (c % 2) + P], ident[:])
                        last.then_inc(turned, 1)
                        pe.wait_ge(turned_out, i * PAIRS + j + 3)
                        pe.wait_ge(gated, i * PAIRS + j + 1)
                        for c in range(4):
                            h, b = c // 2, c % 2
                            last = nc.tensor.matmul(o_ps[:, j % 2, 0:P],
                                                    vs[:, b, g, HALF - HALF * h:3 * HALF - HALF * h],
                                                    pT[:, j % 2, c], start=(c == 0), stop=(c == 3))
                        last.then_inc(mixed, 1)

            @block.scalar
            def _(act):
                act.sem_inc(turned_out, 2)
                act.wait_ge(sinks_loaded, 16)
                with act.Fori(0, NB) as i:
                    for j in range(PAIRS):
                        act.wait_ge(maxed, i * PAIRS + j + 1)
                        for h in range(2):
                            nc.scalar.activation(sc[:, j, h], sc[:, j, h], ACT.Exp, bias=nm[:, j, h:h + 1],
                                                 accum_out=ls[:, j, h:h + 1])
                        for h in range(2):
                            last = nc.scalar.activation(es[:, j, h:h + 1], sinks[:, 2 * j + h:2 * j + h + 1], ACT.Exp,
                                                        bias=nm[:, j, h:h + 1])
                        last.then_inc(exped, 1)
                    for j in range(PAIRS):
                        act.wait_ge(turned, i * PAIRS + j + 1)
                        if j >= 2:
                            act.wait_ge(mixed, i * PAIRS + j - 1)
                        nc.scalar.copy(pT[:, j % 2], t_ps[:, j % 2].rearrange("p (c q) -> p c q", c=4)).then_inc(turned_out, 1)

            @block.vector
            def _(dve):
                v = Chain(dve, v_own)
                dve.sem_inc(gated, 2)
                v.hold(nc.vector.memset(kd[:], 0.0))
                dve.wait_ge(sinks_loaded, 16)
                v(nc.vector.tensor_scalar(nsinks[:], sinks[:], -1.0, None, ALU.mult))
                for src in range(2):
                    for h in range(2):
                        g = h if src == 0 else 1 - h
                        v.hold(nc.vector.tensor_copy(kd[HALF * h:HALF * h + HALF, g, h, P:],
                                                     proj[HALF * h:HALF * h + HALF, K_T + src]))
                v.wait()
                dve.wait_ge(mask_done, 6)
                with dve.Fori(0, NB) as i:
                    v.restart()
                    v.hold(nc.vector.tensor_copy(qs[:], proj[:, Q_T:Q_T + PAIRS, bass.ds(i * P, P)]))
                    v(nc.vector.tensor_copy(vs[:], vpad[:, bass.ds(i, 2)]))
                    dve.sem_inc(staged, 1)
                    for j in range(PAIRS):
                        dve.wait_ge(scored, i * PAIRS + j + 1)
                        v(nc.vector.scalar_tensor_tensor(
                            out=sc[:, j], in0=s_ps[:, j].rearrange("p (a b) -> p a b", a=2), scalar=HEAD_SCALE,
                            in1=mask[:, bass.ds(i, 1)].to_broadcast([P, 2, 2 * P]), op0=ALU.mult, op1=ALU.add))
                        v(nc.vector.tensor_reduce(mx[:, j], sc[:, j], AX.X, ALU.max))
                        nc.vector.scalar_tensor_tensor(out=nm[:, j], in0=mx[:, j], scalar=-1.0,
                                                       in1=nsinks[:, 2 * j:2 * j + 2], op0=ALU.mult,
                                                       op1=ALU.min).then_inc(maxed, 1)
                    for j in range(PAIRS):
                        dve.wait_ge(exped, i * PAIRS + j + 1)
                        v(nc.vector.tensor_tensor(den[:, j], ls[:, j], es[:, j], ALU.add))
                        v(nc.vector.reciprocal(rd[:, j], den[:, j]))
                        nc.vector.tensor_tensor(sc[:, j], sc[:, j],
                                                rd[:, j].unsqueeze(2).to_broadcast([P, 2, 2 * P]),
                                                ALU.mult).then_inc(normed, 1)
                    for j in range(PAIRS):
                        dve.wait_ge(mixed, i * PAIRS + j + 1)
                        out = proj[:, G_T + j, bass.ds(i * P, P)]
                        nc.vector.tensor_tensor(out, o_ps[:, j % 2, 0:P], out, ALU.mult).then_inc(gated, 1)
                dve.wait_ge(gated, NB * PAIRS + 2)


def lru(nc, D, proj):
    with Phase(nc, "lru") as ph:
        TL = 2
        xpad = ph.sb("xpad", [P, TL, SEQ + 3])
        xc = ph.sb("xc", [P, TL, SEQ])
        rg = ph.sb("rg", [P, TL, SEQ])
        ig = ph.sb("ig", [P, TL, SEQ])
        av = ph.sb("av", [P, TL, SEQ])
        uv = ph.sb("uv", [P, TL, SEQ])
        wa = ph.sb("wa", [P, TL, P])
        wx = ph.sb("wx", [P, TL, P])
        vec = ph.sb("vec", [P, TL, 8])
        sp8 = ph.sb("sp8", [P, TL, 3])
        r_ps = ph.ps("r", [P, TL, 2, 512])
        i_ps = ph.ps("i", [P, TL, 2, 512])
        loaded, zeroed, conv_done, gates_done, sig_done, v_own, a_own = (
            ph.sem(n) for n in ("loaded", "zeroed", "conv_done", "gates_done", "sig_done", "v_own", "a_own"))
        decay_done, tanh_done, root_done, root_in = (ph.sem(n) for n in ("decay_done", "tanh_done", "root_done", "root_in"))
        with nc.Block() as block:

            @block.sync
            def _(sp):
                sp.dma_start(vec[:], D["lru_vec"]).then_inc(loaded, 16)
                sp.wait_ge(zeroed, 1)
                for w, name in ((wa, "lru_wa"), (wx, "lru_wx")):
                    for n in range(4):
                        h = n % 2
                        sp.dma_start(w[HALF * h:HALF * h + HALF, n // 2, HALF * h:HALF * h + HALF],
                                     D[name][n]).then_inc(loaded, 16)

            @block.vector
            def _(dve):
                v = Chain(dve, v_own)
                v.hold(nc.vector.memset(wa[:], 0.0))
                v(nc.vector.memset(wx[:], 0.0))
                dve.sem_inc(zeroed, 1)
                v.hold(nc.vector.memset(xpad[:, :, 0:3], 0.0))
                v(nc.vector.tensor_copy(xpad[:, :, 3:], proj[:, XB_T:XB_T + TL]))
                dve.wait_ge(loaded, 16 * 9)
                for t in range(TL):
                    v.hold(nc.vector.tensor_scalar(xc[:, t], xpad[:, t, 0:SEQ], vec[:, t, 0:1], vec[:, t, 4:5],
                                                   ALU.mult, ALU.add))
                v.wait()
                for c in range(1, 4):
                    for t in range(TL):
                        v.hold(nc.vector.scalar_tensor_tensor(out=xc[:, t], in0=xpad[:, t, c:c + SEQ],
                                                              scalar=vec[:, t, c:c + 1], in1=xc[:, t],
                                                              op0=ALU.mult, op1=ALU.add))
                    v.wait()
                dve.sem_inc(conv_done, 1)
                dve.wait_ge(sig_done, 1)
                for t in range(TL):
                    v.hold(nc.vector.tensor_scalar(rg[:, t], rg[:, t], sp8[:, t, 1:2], -8.0, ALU.mult, ALU.mult))
                    v.hold(nc.vector.tensor_tensor(ig[:, t], ig[:, t], xc[:, t], ALU.mult))
                v.wait()
                dve.sem_inc(decay_done, 1)
                dve.wait_ge(tanh_done, 1)
                v(nc.vector.tensor_tensor(xc[:], av[:], av[:], ALU.mult))
                v(nc.vector.tensor_scalar(xc[:], xc[:], 1.0, -1.0, ALU.add, ALU.mult))
                v(nc.vector.tensor_tensor(uv[:], uv[:], xc[:], ALU.mult))
                dve.sem_inc(root_in, 1)
                dve.wait_ge(root_done, 1)
                v(nc.vector.tensor_tensor(uv[:], uv[:], ig[:], ALU.mult))
                for t in range(TL):
                    v.hold(nc.vector.tensor_tensor_scan(xc[:, t], av[:, t], uv[:, t], 0.0, ALU.mult, ALU.add))
                v.wait()
                v(nc.vector.tensor_tensor(proj[:, G_T + 4:G_T + 6], proj[:, G_T + 4:G_T + 6], xc[:], ALU.mult))

            @block.tensor
            def _(pe):
                pe.wait_ge(conv_done, 1)
                pe.wait_ge(loaded, 16 * 9)
                for w, acc in ((wa, r_ps), (wx, i_ps)):
                    for t in range(TL):
                        for c in range(2):
                            last = nc.tensor.matmul(acc[:, t, c], w[:, t], xc[:, t, 512 * c:512 * c + 512],
                                                    start=True, stop=True)
                last.then_inc(gates_done, 1)

            @block.scalar
            def _(act):
                a = Chain(act, a_own)
                act.wait_ge(loaded, 16 * 9)
                a(nc.scalar.activation(sp8[:, :, 0:1], vec[:, :, 7:8], ACT.Exp, scale=-1.0))
                a(nc.scalar.activation(sp8[:, :, 1:2], sp8[:, :, 0:1], ACT.Ln, bias=1.0))
                act.wait_ge(gates_done, 1)
                for t in range(TL):
                    a.hold(nc.scalar.activation(rg[:, t], r_ps[:, t].rearrange("p a b -> p (a b)"), ACT.Sigmoid,
                                                bias=vec[:, t, 5:6]))
                    a.hold(nc.scalar.activation(ig[:, t], i_ps[:, t].rearrange("p a b -> p (a b)"), ACT.Sigmoid,
                                                bias=vec[:, t, 6:7]))
                a.wait()
                act.sem_inc(sig_done, 1)
                act.wait_ge(decay_done, 1)
                a.hold(nc.scalar.activation(av[:], rg[:], ACT.Exp))
                a.hold(nc.scalar.activation(uv[:], rg[:], ACT.Tanh))
                a.wait()
                act.sem_inc(tanh_done, 1)
                act.wait_ge(root_in, 1)
                a(nc.scalar.activation(uv[:], uv[:], ACT.Sqrt))
                act.sem_inc(root_done, 1)


def rwkv(nc, D, proj):
    TL = 2
    with Phase(nc, "rwk") as ph:
        k2 = ph.sb("k2", [P, TL, SEQ])
        kkb = ph.sb("kkb", [P, TL, SEQ])
        bb = ph.sb("bb", [P, TL, SEQ])
        rr = ph.sb("rr", [P, TL, SEQ])
        vv = ph.sb("vv", [P, TL, SEQ])
        bonus = ph.sb("bonus", [P, TL, SEQ])
        wc = ph.sb("wc", [P, TL, NCH])
        vec = ph.sb("vec", [P, TL, 10])
        ones2 = ph.sb("ones2", [P, P])
        with Phase(nc, "rwp") as p2:
            xs = p2.sb("xs", [P, TL, SEQ])
            dlt = p2.sb("dlt", [P, TL, SEQ])
            lo = p2.sb("lo", [HALF, SEQ])
            lod = p2.sb("lod", [HALF, SEQ])
            muwa = p2.sb("muwa", [HALF, 1])
            w2a2 = p2.sb("w2a2", [HALF, TL * P])
            aa = p2.sb("aa", [P, TL, SEQ])
            lw = p2.sb("lw", [P, TL, SEQ])
            cum = p2.sb("cum", [P, TL, SEQ])
            keep = p2.sb("keep", [P, SEQ])
            z_ps = p2.ps("z", [P, TL, 2, 512])
            a_ps = p2.ps("a", [P, TL, 2, 512])
            loaded, v_own, a_own = p2.sem("loaded"), p2.sem("v_own"), p2.sem("a_own")
            low_ready, tanh_done, low_done, sig_done = (p2.sem(n) for n in ("low_ready", "tanh_done", "low_done", "sig_done"))
            sq_ready, sq_done, root_done, bonus_in, bonus_done, bonus_out = (
                p2.sem(n) for n in ("sq_ready", "sq_done", "root_done", "bonus_in", "bonus_done", "bonus_out"))
            cum_done, exp_done, next_exp, norm_read = (p2.sem(n) for n in ("cum_done", "exp_done", "next_exp", "norm_read"))
            with nc.Block() as block:

                @block.sync
                def _(sp):
                    sp.dma_start(vec[:], D["rwkv_vec"]).then_inc(loaded, 16)
                    sp.dma_start(muwa[:], D["rwkv_mu_lo"]).then_inc(loaded, 16)
                    sp.dma_start(w2a2[0:RANK], D["rwkv_w2"]).then_inc(loaded, 16)
                    sp.dma_start(w2a2[RANK:2 * RANK], D["rwkv_a2"]).then_inc(loaded, 16)

                @block.vector
                def _(dve):
                    v = Chain(dve, v_own)
                    v.hold(nc.vector.memset(ones2[:], 0.0))
                    v(nc.vector.memset(keep[:], 1.0))
                    v.hold(nc.vector.memset(keep[:].rearrange("p (n c) -> p n c", c=CHUNK)[:, :, 0:1], 0.0))
                    for h in range(2):
                        v.hold(nc.vector.memset(ones2[HALF * h:HALF * h + HALF, HALF * h:HALF * h + HALF], 1.0))
                    dve.wait_ge(loaded, 64)

                    def shift(out, delta, src, mu):
                        v.hold(nc.vector.tensor_scalar(delta[:, 0:1], src[:, 0:1], -1.0, None, ALU.mult))
                        v(nc.vector.tensor_tensor(delta[:, 1:SEQ], src[:, 0:SEQ - 1], src[:, 1:SEQ], ALU.subtract))
                        v(nc.vector.scalar_tensor_tensor(out=out, in0=delta, scalar=mu, in1=src,
                                                         op0=ALU.mult, op1=ALU.add))

                    shift(lo[:], lod[:], proj[0:HALF, WA_T], muwa[:, 0:1])
                    dve.sem_inc(low_ready, 1)
                    for t in range(TL):
                        shift(rr[:, t], dlt[:, t], proj[:, R_T + t], vec[:, t, 0:1])
                        shift(xs[:, t], dlt[:, t], proj[:, CK_T + t], vec[:, t, 1:2])
                        shift(vv[:, t], dlt[:, t], proj[:, CV_T + t], vec[:, t, 2:3])
                        v(nc.vector.tensor_scalar(kkb[:, t], xs[:, t], vec[:, t, 5:6], None, ALU.mult))
                        v(nc.vector.tensor_tensor(dlt[:, t], kkb[:, t], kkb[:, t], ALU.mult))
                    dve.sem_inc(sq_ready, 1)
                    dve.wait_ge(sig_done, 1)
                    for t in range(TL):
                        v(nc.vector.tensor_scalar(k2[:, t], aa[:, t], -1.0, vec[:, t, 6:7], ALU.add, ALU.mult))
                        v(nc.vector.scalar_tensor_tensor(out=k2[:, t], in0=k2[:, t], scalar=1.0, in1=xs[:, t],
                                                         op0=ALU.add, op1=ALU.mult))
                    v(nc.vector.tensor_scalar(lw[:], lw[:], -DECAY_HALF, None, ALU.mult))
                    for t in range(TL):
                        v.hold(nc.vector.tensor_tensor_scan(cum[:, t], keep[:], lw[:, t], 0.0, ALU.mult, ALU.add))
                    v.wait()
                    v(nc.vector.tensor_tensor(lw[:], cum[:], lw[:], ALU.subtract))
                    dve.sem_inc(cum_done, 1)
                    dve.wait_ge(root_done, 1)
                    v(nc.vector.reciprocal(dlt[:], dlt[:]))
                    v(nc.vector.tensor_tensor(kkb[:], kkb[:], dlt[:], ALU.mult))
                    v(nc.vector.tensor_tensor(bb[:], kkb[:], aa[:], ALU.mult))
                    for t in range(TL):
                        v(nc.vector.scalar_tensor_tensor(out=dlt[:, t], in0=rr[:, t], scalar=vec[:, t, 7:8],
                                                         in1=k2[:, t], op0=ALU.mult, op1=ALU.mult))
                    dve.sem_inc(bonus_in, 1)
                    dve.wait_ge(bonus_done, 1)
                    v(nc.vector.tensor_tensor(bonus[:], z_ps[:].rearrange("p t a b -> p t (a b)"), vv[:], ALU.mult))
                    dve.wait_ge(exp_done, 1)
                    v.hold(nc.vector.tensor_copy(wc[:], aa[:].rearrange("p t (n c) -> p t n c", c=CHUNK)[:, :, :, CHUNK - 1]))
                    v.hold(nc.vector.tensor_tensor(rr[:], rr[:], aa[:], ALU.mult))
                    v.hold(nc.vector.scalar_tensor_tensor(out=kkb[:], in0=kkb[:], scalar=-1.0, in1=lw[:],
                                                          op0=ALU.mult, op1=ALU.mult))
                    v.hold(nc.vector.tensor_tensor(bb[:], bb[:], cum[:], ALU.mult))
                    v.hold(nc.vector.tensor_tensor(k2[:], k2[:], cum[:], ALU.mult))
                    v.wait()

                @block.tensor
                def _(pe):
                    pe.wait_ge(tanh_done, 1)
                    for acc, r0 in ((z_ps, 0), (a_ps, RANK)):
                        for t in range(TL):
                            for c in range(2):
                                last = nc.tensor.matmul(acc[:, t, c], w2a2[r0:r0 + RANK, P * t:P * t + P],
                                                        lo[r0:r0 + RANK, 512 * c:512 * c + 512], start=True, stop=True)
                    last.then_inc(low_done, 1)

                    def head_sums(acc):
                        for t in range(TL):
                            for c in range(2):
                                last = nc.tensor.matmul(acc[:, t, c], ones2[:], dlt[:, t, 512 * c:512 * c + 512],
                                                        start=True, stop=True)
                        return last

                    pe.wait_ge(sq_ready, 1)
                    pe.wait_ge(sig_done, 1)
                    head_sums(a_ps).then_inc(sq_done, 1)
                    pe.wait_ge(bonus_in, 1)
                    head_sums(z_ps).then_inc(bonus_done, 1)

                @block.scalar
                def _(act):
                    a = Chain(act, a_own)
                    act.wait_ge(low_ready, 1)
                    a(nc.scalar.activation(lo[0:RANK], lo[0:RANK], ACT.Tanh))
                    act.sem_inc(tanh_done, 1)
                    act.wait_ge(low_done, 1)
                    for t in range(TL):
                        a.hold(nc.scalar.activation(lw[:, t], z_ps[:, t].rearrange("p a b -> p (a b)"), ACT.Sigmoid,
                                                    bias=vec[:, t, 3:4]))
                        a.hold(nc.scalar.activation(aa[:, t], a_ps[:, t].rearrange("p a b -> p (a b)"), ACT.Sigmoid,
                                                    bias=vec[:, t, 4:5]))
                    a.wait()
                    act.sem_inc(sig_done, 1)
                    act.wait_ge(sq_done, 1)
                    eps = p2.sb("eps", [P, 1])
                    a(nc.scalar.activation(eps[:], vec[:, 0, 0:1], ACT.Copy, scale=0.0, bias=1e-12))
                    a(nc.scalar.activation(dlt[:], a_ps[:].rearrange("p t a b -> p t (a b)"), ACT.Sqrt, bias=eps[:]))
                    act.sem_inc(root_done, 1)
                    act.wait_ge(cum_done, 1)
                    act.wait_ge(bonus_in, 1)
                    a.hold(nc.scalar.activation(aa[:], cum[:], ACT.Exp))
                    a.hold(nc.scalar.activation(lw[:], lw[:], ACT.Exp))
                    a.wait()
                    a(nc.scalar.activation(cum[:], cum[:], ACT.Exp, scale=-1.0))
                    act.sem_inc(exp_done, 1)

        with Phase(nc, "rwc") as p3:
            dg = p3.sb("dg", [P, TL, 5, P])
            A_, R_, B_, K_, V_ = range(5)
            tokm = p3.sb("tokm", [P, TL, 3, P])
            vt = p3.sb("vt", [P, TL, HALF])
            up = p3.sb("up", [P, P])
            upi = p3.sb("upi", [P, P])
            lowm = p3.sb("lowm", [P, P])
            ident = p3.sb("ident", [P, P])
            idh = p3.sb("idh", [P, HALF])
            pw = p3.sb("pw", [P, TL, 2, P])
            inv = p3.sb("inv", [P, TL, P])
            mt = p3.sb("mt", [P, TL, P])
            n1 = p3.sb("n1", [P, TL, P])
            n2 = p3.sb("n2", [P, TL, P])
            us = p3.sb("us", [P, TL, HALF])
            sa = p3.sb("sa", [P, TL, HALF])
            z = p3.sb("z", [P, TL, HALF])
            st = p3.sb("st", [P, TL, 6])
            mv = p3.sb("mv", [P, TL, 2])
            rs = p3.sb("rs", [P, TL, 1])
            eps = p3.sb("eps", [P, 1])
            ydg = p3.sb("ydg", [P, TL, P])
            yo = p3.sb("yo", [P, TL, CHUNK])
            g_ps = [[p3.ps(f"g{t}{n}", [P, 512]) for n in range(4)] for t in range(TL)]
            masks = p3.sem("masks")
            v_own = p3.sem("v_own")
            staged, crossed, masked, squared, powered, solved_in, u_done, u_out, sa_done, sa_out, y_done, rooted, root_in, y_in, y_turned, tok_out, next_ok = (
                p3.sem(n) for n in ("staged", "crossed", "masked", "squared", "powered", "solved_in", "u_done", "u_out",
                                    "sa_done", "sa_out", "y_done", "rooted", "root_in", "y_in", "y_turned", "tok_out",
                                    "next_ok"))
            POW = 5
            with nc.Block() as block:

                @block.gpsimd
                def _(pool):
                    for n, m in enumerate((up, upi, lowm)):
                        nc.gpsimd.memset(m[:], 1.0).then_inc(masks, 1)
                    nc.gpsimd.memset(ident[:], 0.0).then_inc(masks, 1)
                    nc.gpsimd.memset(idh[:], 0.0).then_inc(masks, 1)
                    pool.wait_ge(masks, 5)
                    def sel(m, op, mult, step, fill=0.0, base=0):
                        nc.gpsimd.affine_select(out=m, in_=m, compare_op=op, fill=fill, base=base,
                                                pattern=[[step, m.shape[1]]], channel_multiplier=mult).then_inc(masks, 1)
                    sel(up[:], ALU.is_gt, -1, 1)
                    sel(upi[:], ALU.is_ge, -1, 1)
                    sel(lowm[:], ALU.is_gt, 1, -1)
                    sel(ident[:], ALU.not_equal, 1, -1, 1.0)
                    sel(idh[:], ALU.not_equal, 1, -1, 1.0)
                    pool.wait_ge(masks, 10)
                    sel(idh[:], ALU.not_equal, 1, -1, 1.0, -HALF)

                @block.vector
                def _(dve):
                    v = Chain(dve, v_own)
                    for b in (dg, z, ydg):
                        v.hold(nc.vector.memset(b[:], 0.0))
                    v(nc.vector.memset(eps[:], GN_EPS))
                    dve.wait_ge(masks, 11)
                    with dve.Fori(0, NCH) as i:
                        v.restart()
                        now = bass.ds(i * CHUNK, CHUNK)
                        for h in range(2):
                            hp = slice(HALF * h, HALF * h + HALF)
                            for n, src in ((A_, kkb), (R_, rr), (B_, bb), (K_, k2), (V_, vv)):
                                v.hold(nc.vector.tensor_copy(dg[hp, :, n, hp], src[hp, :, now]))
                        v.wait()
                        dve.sem_inc(staged, 1)
                        dve.wait_ge(crossed, i + 1)
                        for t in range(TL):
                            g0, g1, g2, g3 = g_ps[t]
                            v.hold(nc.vector.tensor_tensor(pw[:, t, 1], g0[:, 0:P], up[:], ALU.mult))
                            v.hold(nc.vector.tensor_tensor(n1[:, t], g0[:, P:2 * P], upi[:], ALU.mult))
                            v.hold(nc.vector.tensor_tensor(mt[:, t], g0[:, 2 * P:3 * P], up[:], ALU.mult))
                            v.hold(nc.vector.tensor_tensor(n2[:, t], g0[:, 3 * P:4 * P], upi[:], ALU.mult))
                            v.hold(nc.vector.tensor_tensor(pw[:, t, 0], g1[:, 0:P], lowm[:], ALU.mult))
                            v.hold(nc.vector.tensor_copy(tokm[:, t].rearrange("p a b -> p (a b)"), g1[:, P:4 * P]))
                        v.wait()
                        for t in range(TL):
                            v.hold(nc.vector.tensor_tensor(inv[:, t], pw[:, t, 1], ident[:], ALU.add))
                            v.hold(nc.vector.tensor_tensor(vt[:, t], tokm[:, t, 2, 0:HALF], tokm[:, t, 2, HALF:P], ALU.add))
                        v.wait()
                        dve.sem_inc(masked, 1)
                        for n in range(POW):
                            dve.wait_ge(squared, i * POW + n + 1)
                            for t in range(TL):
                                v.hold(nc.vector.tensor_copy(pw[:, t].rearrange("p a b -> p (a b)"), g_ps[t][2][:, 0:2 * P]))
                            v.wait()
                            dve.sem_inc(powered, 1)
                            dve.wait_ge(solved_in, i * POW + n + 1)
                            for t in range(TL):
                                v.hold(nc.vector.tensor_tensor(inv[:, t], inv[:, t], g_ps[t][3][:, 0:P], ALU.add))
                            v.wait()
                        dve.sem_inc(tok_out, 1)
                        dve.wait_ge(u_done, i + 1)
                        for t in range(TL):
                            v.hold(nc.vector.tensor_copy(us[:, t], g_ps[t][3][:, P:P + HALF]))
                        v.wait()
                        dve.sem_inc(u_out, 1)
                        dve.wait_ge(sa_done, i + 1)
                        for t in range(TL):
                            v.hold(nc.vector.tensor_copy(sa[:, t], g_ps[t][3][:, 2 * P:2 * P + HALF]))
                        v.wait()
                        dve.sem_inc(sa_out, 1)
                        dve.wait_ge(y_done, i + 1)
                        for t in range(TL):
                            v.hold(nc.vector.tensor_tensor(z[:, t], z[:, t], g_ps[t][3][:, 3 * P:3 * P + HALF], ALU.add))
                            v.hold(nc.vector.bn_stats(st[:, t], g_ps[t][2][:, 0:HALF]))
                        v.wait()
                        for t in range(TL):
                            v.hold(nc.vector.tensor_tensor(z[:, t], z[:, t],
                                                           wc[:, t, bass.ds(i, 1)].to_broadcast([P, HALF]), ALU.mult))
                            v.hold(nc.vector.bn_aggr(mv[:, t], st[:, t]))
                        v.wait()
                        dve.sem_inc(root_in, 1)
                        dve.wait_ge(rooted, i + 1)
                        v(nc.vector.reciprocal(rs[:], rs[:]))
                        for t in range(TL):
                            for h in range(2):
                                hp = slice(HALF * h, HALF * h + HALF)
                                v.hold(nc.vector.tensor_scalar(ydg[hp, t, hp], g_ps[t][2][hp, 0:HALF], mv[hp, t, 0:1],
                                                               rs[hp, t], ALU.subtract, ALU.mult))
                        v.wait()
                        dve.sem_inc(y_in, 1)
                        dve.wait_ge(y_turned, i + 1)
                        for t in range(TL):
                            v.hold(nc.vector.tensor_scalar(yo[:, t], g_ps[t][1][:, 0:HALF], vec[:, t, 8:9],
                                                           vec[:, t, 9:10], ALU.mult, ALU.add))
                        v.wait()
                        v(nc.vector.tensor_tensor(yo[:], yo[:], bonus[:, :, now], ALU.add))
                        out = proj[:, G_T + 6:G_T + 8, now]
                        v(nc.vector.tensor_tensor(out, out, yo[:], ALU.mult))

                @block.scalar
                def _(act):
                    with act.Fori(0, NCH) as i:
                        act.wait_ge(root_in, i + 1)
                        nc.scalar.activation(rs[:, :, 0], mv[:, :, 1], ACT.Sqrt, bias=eps[:]).then_inc(rooted, 1)

                @block.tensor
                def _(pe):
                    mm = nc.tensor.matmul
                    with pe.Fori(0, NCH) as i:
                        pe.wait_ge(staged, i + 1)
                        for t in range(TL):
                            g0, g1, g2, g3 = g_ps[t]
                            ar = dg[:, t, 0:2].rearrange("p a b -> p (a b)")
                            mm(g0[:, 0:2 * P], dg[:, t, B_], ar, start=True, stop=True)
                            mm(g0[:, 2 * P:4 * P], dg[:, t, K_], ar, start=True, stop=True)
                            mm(g1[:, 0:P], dg[:, t, A_], dg[:, t, B_], start=True, stop=True)
                            for n, src in enumerate((B_, K_, V_)):
                                last = nc.tensor.transpose(g1[:, P + P * n:2 * P + P * n], dg[:, t, src], ident[:])
                        last.then_inc(crossed, 1)
                        pe.wait_ge(masked, i + 1)
                        for n in range(POW):
                            for t in range(TL):
                                g2 = g_ps[t][2]
                                mm(g2[:, 0:P], pw[:, t, 1], pw[:, t, 0], start=True, stop=True)
                                last = mm(g2[:, P:2 * P], pw[:, t, 0], pw[:, t, 1], start=True, stop=True)
                            last.then_inc(squared, 1)
                            pe.wait_ge(powered, i * POW + n + 1)
                            for t in range(TL):
                                last = mm(g_ps[t][3][:, 0:P], pw[:, t, 0], inv[:, t], start=True, stop=True)
                            last.then_inc(solved_in, 1)
                            if n < POW - 1:
                                pass
                        pe.wait_ge(tok_out, i + 1)
                        for t in range(TL):
                            mm(g_ps[t][3][:, P:P + HALF], dg[:, t, A_], z[:, t], start=True, stop=False)
                            last = mm(g_ps[t][3][:, P:P + HALF], mt[:, t], vt[:, t], start=False, stop=True)
                        last.then_inc(u_done, 1)
                        pe.wait_ge(u_out, i + 1)
                        for t in range(TL):
                            last = mm(g_ps[t][3][:, 2 * P:2 * P + HALF], inv[:, t], us[:, t], start=True, stop=True)
                        last.then_inc(sa_done, 1)
                        pe.wait_ge(sa_out, i + 1)
                        for t in range(TL):
                            mm(g_ps[t][3][:, 3 * P:3 * P + HALF], tokm[:, t, 0], sa[:, t], start=True, stop=False)
                            mm(g_ps[t][3][:, 3 * P:3 * P + HALF], tokm[:, t, 1], vt[:, t], start=False, stop=True)
                            y = g_ps[t][2][:, 0:HALF]
                            mm(y, dg[:, t, R_], z[:, t], start=True, stop=False)
                            mm(y, n1[:, t], sa[:, t], start=False, stop=False)
                            last = mm(y, n2[:, t], vt[:, t], start=False, stop=True)
                        last.then_inc(y_done, 1)
                        pe.wait_ge(y_in, i + 1)
                        for t in range(TL):
                            last = mm(g_ps[t][1][:, 0:HALF], ydg[:, t], idh[:], start=True, stop=True)
                        last.then_inc(y_turned, 1)


def first_out(nc, D, proj):
    META = 16
    with Phase(nc, "fo") as ph:
        wo = ph.sb("wo", [P, KT, DM])
        xb = ph.sb("xb", [P, 2, DM])
        hb = ph.sb("hb", [P, 2, DM])
        gb = ph.sb("gb", [P, 2, DM])
        st = ph.sb("st", [P, 2, 6])
        mv = ph.sb("mv", [P, 2])
        rs = ph.sb("rs", [P, 1])
        eps = ph.sb("eps", [P, 1])
        meta = ph.sb("meta", [META, DM])
        zpad = ph.sb("zpad", [P - META, DM])
        acc = ph.ps("acc", [P, 2, 2, 512])
        w_loaded, gb_loaded, v_own, h_ready, meta_in, pad_ready, padded = (
            ph.sem(n) for n in ("w_loaded", "gb_loaded", "v_own", "h_ready", "meta_in", "pad_ready", "padded"))
        stored = [ph.sem("h0_stored"), ph.sem("h1_stored")]
        x_loaded = [ph.sem("x0_loaded"), ph.sem("x1_loaded")]
        done, var_ready, rooted = ph.sem("done"), ph.sem("var_ready"), ph.sem("rooted")
        h = D["h0"]
        with nc.Block() as block:

            @block.sync
            def _(sp):
                for k in range(KT):
                    sp.dma_start(wo[:, k], D["w_out"][P * k:P * k + P]).then_inc(w_loaded, 16)
                sp.dma_start(gb[:, 0], D["ln_g"].partition_broadcast(P)).then_inc(gb_loaded, 16)
                sp.dma_start(gb[:, 1], D["ln_b"].partition_broadcast(P)).then_inc(gb_loaded, 16)
                sp.dma_start(meta[:], D["meta_tokens_2"]).then_inc(meta_in, 16)
                for t in range(2):
                    sp.dma_start(xb[:, t], D["x"][P * t:P * t + P]).then_inc(x_loaded[t], 16)
                for t in range(NB):
                    sp.wait_ge(h_ready, t + 1)
                    sp.dma_start(h[META + P * t:META + P * t + P], hb[:, t % 2]).then_inc(stored[t % 2], 16)
                    if t + 2 < NB:
                        sp.dma_start(xb[:, t % 2], D["x"][P * (t + 2):P * (t + 3)]).then_inc(x_loaded[t % 2], 16)
                sp.wait_ge(meta_in, 16)
                sp.dma_start(h[0:META], meta[:]).then_inc(padded, 16)
                sp.wait_ge(pad_ready, 1)
                sp.dma_start(h[META + SEQ:], zpad[:]).then_inc(padded, 16)
                sp.wait_ge(padded, 32)
                for b in range(2):
                    sp.wait_ge(stored[b], 16 * (NB // 2))

            @block.tensor
            def _(pe):
                pe.wait_ge(w_loaded, 16 * KT)
                for t in range(NB):
                    if t >= 2:
                        pe.wait_ge(var_ready, t - 1)
                    for c in range(2):
                        for k in range(KT):
                            last = nc.tensor.matmul(acc[:, t % 2, c], proj[:, G_T + k, P * t:P * t + P],
                                                    wo[:, k, 512 * c:512 * c + 512], start=(k == 0), stop=(k == KT - 1))
                    last.then_inc(done, 1)

            @block.vector
            def _(dve):
                v = Chain(dve, v_own)
                nc.vector.memset(zpad[:], 0.0).then_inc(pad_ready, 1)
                v(nc.vector.memset(eps[:], LN_EPS))
                dve.wait_ge(gb_loaded, 32)
                for t in range(NB):
                    b = t % 2
                    dve.wait_ge(done, t + 1)
                    dve.wait_ge(x_loaded[b], 16 * (t // 2 + 1))
                    if t >= 2:
                        dve.wait_ge(stored[b], 16 * (t // 2))
                    v(nc.vector.scalar_tensor_tensor(out=hb[:, b], in0=xb[:, b], scalar=ALPHA,
                                                     in1=acc[:, b].rearrange("p a b -> p (a b)"),
                                                     op0=ALU.mult, op1=ALU.add))
                    for c in range(2):
                        v.hold(nc.vector.bn_stats(st[:, c], hb[:, b, 512 * c:512 * c + 512]))
                    v.wait()
                    v(nc.vector.bn_aggr(mv[:], st[:].rearrange("p a b -> p (a b)")))
                    dve.sem_inc(var_ready, 1)
                    dve.wait_ge(rooted, t + 1)
                    v(nc.vector.reciprocal(rs[:], rs[:]))
                    v(nc.vector.tensor_scalar(hb[:, b], hb[:, b], mv[:, 0:1], rs[:], ALU.subtract, ALU.mult))
                    v(nc.vector.tensor_tensor(hb[:, b], hb[:, b], gb[:, 0], ALU.mult))
                    v(nc.vector.tensor_tensor(hb[:, b], hb[:, b], gb[:, 1], ALU.add))
                    dve.sem_inc(h_ready, 1)

            @block.scalar
            def _(act):
                for t in range(NB):
                    act.wait_ge(var_ready, t + 1)
                    nc.scalar.activation(rs[:], mv[:, 1:2], ACT.Sqrt, bias=eps[:]).then_inc(rooted, 1)


def first(nc, D):
    with Phase(nc, "A") as ph:
        proj = ph.sb("proj", [P, PROJ_TILES, SEQ])
        with Phase(nc, "V") as pv:
            vpad = pv.sb("vpad", [P, NB + 1, KV, 3 * HALF])
            project(nc, D, proj, vpad)
            gates(nc, D, proj)
            window_attention(nc, D, proj, vpad)
        lru(nc, D, proj)
        rwkv(nc, D, proj)
        if "dbg" in D:
            with Phase(nc, "dbg") as p2:
                s = p2.sem("s")
                with nc.Block() as block:
                    @block.sync
                    def _(sp):
                        sp.dma_start(D["dbg"], proj[:, 0:8]).then_inc(s, 16)
                        sp.wait_ge(s, 16)
        first_out(nc, D, proj)

META = 16
T = META + SEQ
TT = -(-T // P)
TP = TT * P
LAST = T - (TT - 1) * P
NORM_EPS = 1e-6
CUTS = [(0, 352), (352, 352), (704, T - 704)]
GROUPS = 8
PER_GROUP = 8
EXPERTS = GROUPS * PER_GROUP
DE = 256
CAP = 64
MAIN_SLOTS = EXPERTS * CAP
SPILL_BLOCKS = 2 * T // CAP
SPILL_BLOCKS += SPILL_BLOCKS % 2
PER_EXPERT_SPILL = (T - 1) // CAP
SLOTS = MAIN_SLOTS + SPILL_BLOCKS * CAP
PAIRS_M = EXPERTS // 2
HEADS = 8
NOPE = 128
ROPE = 64
QR = 384
KVR = 256
VD = 128
ATT_SCALE = float(NOPE + ROPE) ** -0.5


def rows_of(t):
    return P if t < TT - 1 else LAST


def make_identity(nc, pool, ident, sem):
    nc.gpsimd.memset(ident[:], 0.0).then_inc(sem, 1)
    pool.wait_ge(sem, 1)
    nc.gpsimd.affine_select(out=ident[:], in_=ident[:], compare_op=ALU.not_equal, fill=1.0,
                            base=0, pattern=[[-1, P]], channel_multiplier=1).then_inc(sem, 1)


def norm_transpose(nc, h, outs, gains):
    with Phase(nc, "nt") as ph:
        NBUF = 3
        hb = ph.sb("hb", [P, NBUF, DM])
        xh = ph.sb("xh", [P, 2, DM])
        sq = ph.sb("sq", [P, DM])
        ss = ph.sb("ss", [P, NBUF])
        rt = ph.sb("rt", [P, NBUF])
        rs = ph.sb("rs", [P, NBUF])
        eps = ph.sb("eps", [P, 1])
        gain = ph.sb("gain", [P, len(gains), KT])
        ident = ph.sb("ident", [P, P])
        tp = ph.ps("tp", [P, 2, 2, 512])
        loaded = [ph.sem(f"h{n}_loaded") for n in range(NBUF)]
        g_loaded, id_done, eps_done, rooted, scaled, turned, out_done, v_own, a_own = (
            ph.sem(n) for n in ("g_loaded", "id_done", "eps_done", "rooted", "scaled", "turned", "out_done", "v_own", "a_own"))
        with nc.Block() as block:

            @block.sync
            def _(sp):
                for n, g in enumerate(gains):
                    sp.dma_start(gain[:, n], g).then_inc(g_loaded, 16)
                for t in range(TT):
                    if t >= NBUF:
                        sp.wait_ge(scaled, t - NBUF + 1)
                    sp.dma_start(hb[:, t % NBUF], h[P * t:P * t + P]).then_inc(loaded[t % NBUF], 16)

            @block.gpsimd
            def _(pool):
                make_identity(nc, pool, ident, id_done)

            @block.scalar
            def _(act):
                a = Chain(act, a_own)
                act.wait_ge(eps_done, 1)
                for t in range(TT):
                    b = t % NBUF
                    act.wait_ge(loaded[b], 16 * (t // NBUF + 1))
                    if t >= NBUF:
                        act.wait_ge(scaled, t - NBUF + 1)
                    a(nc.scalar.activation(sq[:], hb[:, b], ACT.Square, accum_out=ss[:, b:b + 1]))
                    nc.scalar.activation(rt[:, b:b + 1], ss[:, b:b + 1], ACT.Sqrt, scale=1.0 / DM,
                                         bias=eps[:]).then_inc(rooted, 1)

            @block.vector
            def _(dve):
                v = Chain(dve, v_own)
                nc.vector.memset(eps[:], NORM_EPS).then_inc(eps_done, 1)
                dve.wait_ge(g_loaded, 16 * len(gains))

                def evacuate(t):
                    dve.wait_ge(turned, t + 1)
                    for n, out in enumerate(outs):
                        for c in range(2):
                            last = nc.vector.tensor_tensor(
                                out[:, 4 * c:4 * c + 4, P * t:P * t + P],
                                tp[:, t % 2, c].rearrange("p (k q) -> p k q", k=4),
                                gain[:, n, 4 * c:4 * c + 4].unsqueeze(2).to_broadcast([P, 4, P]), ALU.mult)
                    last.then_inc(out_done, 1)

                for t in range(TT):
                    b = t % NBUF
                    dve.wait_ge(rooted, t + 1)
                    v(nc.vector.reciprocal(rs[:, b:b + 1], rt[:, b:b + 1]))
                    if t >= 2:
                        dve.wait_ge(turned, t - 1)
                    nc.vector.tensor_scalar(xh[:, t % 2], hb[:, b], rs[:, b:b + 1], None,
                                            ALU.mult).then_inc(scaled, 1)
                    if t >= 1:
                        evacuate(t - 1)
                evacuate(TT - 1)

            @block.tensor
            def _(pe):
                pe.wait_ge(id_done, 2)
                for t in range(TT):
                    pe.wait_ge(scaled, t + 1)
                    if t >= 2:
                        pe.wait_ge(out_done, t - 1)
                    for k in range(KT):
                        last = nc.tensor.transpose(tp[:, t % 2, k // 4, P * (k % 4):P * (k % 4) + P],
                                                   xh[:, t % 2, P * k:P * k + P], ident[:])
                    last.then_inc(turned, 1)


def project_back(nc, src, w_dram, h_in, h_out):
    with Phase(nc, "pb") as ph:
        NBUF = 3
        w = ph.sb("w", [P, KT, DM])
        hb = ph.sb("hb", [P, NBUF, DM])
        ho = ph.sb("ho", [P, 2, DM])
        acc = ph.ps("acc", [P, 3, 2, 512])
        w_loaded, done, summed = (ph.sem(n) for n in ("w_loaded", "done", "summed"))
        loaded = [ph.sem(f"h{n}_loaded") for n in range(NBUF)]
        stored = [ph.sem(f"h{n}_stored") for n in range(2)]
        with nc.Block() as block:

            @block.sync
            def _(sp):
                for k in range(KT):
                    sp.dma_start(w[:, k], w_dram[P * k:P * k + P]).then_inc(w_loaded, 16)
                for t in range(TT):
                    if t >= NBUF:
                        sp.wait_ge(summed, t - NBUF + 1)
                    sp.dma_start(hb[:, t % NBUF], h_in[P * t:P * t + P]).then_inc(loaded[t % NBUF], 16)

            @block.scalar
            def _(act):
                for t in range(TT):
                    act.wait_ge(summed, t + 1)
                    act.dma_start(h_out[P * t:P * t + P], ho[:, t % 2]).then_inc(stored[t % 2], 16)
                for b in range(2):
                    act.wait_ge(stored[b], 16 * ((TT + 1 - b) // 2))

            @block.tensor
            def _(pe):
                pe.wait_ge(w_loaded, 16 * KT)
                for t in range(TT):
                    if t >= 3:
                        pe.wait_ge(summed, t - 2)
                    for c in range(2):
                        for k in range(KT):
                            last = nc.tensor.matmul(acc[:, t % 3, c], src[:, k, P * t:P * t + P],
                                                    w[:, k, 512 * c:512 * c + 512], start=(k == 0), stop=(k == KT - 1))
                    last.then_inc(done, 1)

            @block.vector
            def _(dve):
                for t in range(TT):
                    dve.wait_ge(done, t + 1)
                    dve.wait_ge(loaded[t % NBUF], 16 * (t // NBUF + 1))
                    if t >= 2:
                        dve.wait_ge(stored[t % 2], 16 * (t // 2))
                    nc.vector.tensor_tensor(ho[:, t % 2], acc[:, t % 3].rearrange("p a b -> p (a b)"),
                                            hb[:, t % NBUF], ALU.add).then_inc(summed, 1)


def conv_mixer(nc, D, h_in, h_out):
    with Phase(nc, "cz") as pz:
        zT = pz.sb("zT", [P, KT, TP])
        with Phase(nc, "cm") as ph:
            hnT = ph.sb("hnT", [P, KT, TP])
            norm_transpose(nc, h_in, [hnT], [D["norm_mix_g_t"][0]])
            w = ph.sb("w", [P, 2, 3, KT, P])
            taps = ph.sb("taps", [P, KT, 3])
            bT = ph.sb("bT", [P, 2, T])
            cT = ph.sb("cT", [P, 2, 352])
            z = ph.sb("z", [P, 2, T + 2])
            acc = ph.ps("acc", [P, 2, 3, 512])
            w_loaded = [ph.sem(f"w{n}_loaded") for n in range(2)]
            w_used = [ph.sem(f"w{n}_used") for n in range(2)]
            taps_loaded, done, copied, z_made, conv_done, v_own = (
                ph.sem(n) for n in ("taps_loaded", "done", "copied", "z_made", "conv_done", "v_own"))
            NC = len(CUTS)
            with nc.Block() as block:

                @block.sync
                def _(sp):
                    sp.dma_start(taps[:], D["conv_w_2_t"]).then_inc(taps_loaded, 16)
                    for j in range(KT):
                        if j >= 2:
                            sp.wait_ge(done, NC * (j - 1))
                        sp.dma_start(w[:, j % 2], D["conv_w_in_t"][j]).then_inc(w_loaded[j % 2], 16)

                @block.tensor
                def _(pe):
                    for j in range(KT):
                        pe.wait_ge(w_loaded[j % 2], 16 * (j // 2 + 1))
                        for n, (at, cols) in enumerate(CUTS):
                            u = NC * j + n
                            if u >= 2:
                                pe.wait_ge(z_made, u - 1)
                                pe.wait_ge(copied, u - 1)
                            for s in range(3):
                                for k in range(KT):
                                    last = nc.tensor.matmul(acc[:, u % 2, s, 0:cols], w[:, j % 2, s, k],
                                                            hnT[:, k, at:at + cols], start=(k == 0), stop=(k == KT - 1))
                            last.then_inc(done, 1)

                @block.scalar
                def _(act):
                    for j in range(KT):
                        if j >= 2:
                            act.wait_ge(conv_done, j - 1)
                        for n, (at, cols) in enumerate(CUTS):
                            u = NC * j + n
                            act.wait_ge(done, u + 1)
                            if u >= 2:
                                act.wait_ge(z_made, u - 1)
                            nc.scalar.copy(bT[:, j % 2, at:at + cols], acc[:, u % 2, 0, 0:cols])
                            nc.scalar.copy(cT[:, u % 2, 0:cols], acc[:, u % 2, 1, 0:cols]).then_inc(copied, 1)

                @block.vector
                def _(dve):
                    v = Chain(dve, v_own)
                    v.hold(nc.vector.memset(zT[:, :, T:TP], 0.0))
                    v(nc.vector.memset(z[:, :, 0:2], 0.0))
                    dve.wait_ge(taps_loaded, 16)
                    for j in range(KT):
                        for n, (at, cols) in enumerate(CUTS):
                            u = NC * j + n
                            dve.wait_ge(copied, u + 1)
                            nc.vector.tensor_tensor(z[:, j % 2, 2 + at:2 + at + cols], cT[:, u % 2, 0:cols],
                                                    acc[:, u % 2, 2, 0:cols], ALU.mult).then_inc(z_made, 1)
                        dve.wait_ge(z_made, NC * (j + 1))
                        v(nc.vector.tensor_scalar(zT[:, j, 0:T], z[:, j % 2, 0:T], taps[:, j, 0:1], None, ALU.mult))
                        for s in (1, 2):
                            v(nc.vector.scalar_tensor_tensor(out=zT[:, j, 0:T], in0=z[:, j % 2, s:s + T],
                                                             scalar=taps[:, j, s:s + 1], in1=zT[:, j, 0:T],
                                                             op0=ALU.mult, op1=ALU.add))
                        v(nc.vector.tensor_tensor(zT[:, j, 0:T], zT[:, j, 0:T], bT[:, j % 2], ALU.mult))
                        dve.sem_inc(conv_done, 1)
        project_back(nc, zT, D["conv_w_out_2"], h_in, h_out)


def mla(nc, D, h_in, h_out):
    with Phase(nc, "ml") as pm:
        cq = pm.sb("cqT", [P, QR // P, TP])
        ckv = pm.sb("ckvT", [P, KVR // P, TP])
        kr = pm.sb("kr", [P, 2, T])
        with Phase(nc, "mn") as ph:
            hq = ph.sb("hq", [P, KT, TP])
            hk = ph.sb("hk", [P, KT, TP])
            norm_transpose(nc, h_in, [hq, hk], [D["norm_mix_g_t"][1], D["kv_norm_g_t"]])
            latents(nc, D, hq, hk, cq, ckv, kr)
        oT = pm.sb("oT", [P, HEADS, TP])
        heads(nc, D, cq, ckv, kr, oT)
        project_back(nc, oT, D["w_o_2"], h_in, h_out)


def latents(nc, D, hq, hk, cq, ckv, kr):
    QT, CT = QR // P, KVR // P
    with Phase(nc, "la") as ph:
        wq = ph.sb("wq", [P, KT, QR])
        wk = ph.sb("wk", [P, KT, KVR])
        wr = ph.sb("wr", [P, KT, 2, P])
        gq = ph.sb("gq", [P, QT])
        gk = ph.sb("gk", [P, CT])
        cosT = ph.sb("cosT", [P, T])
        sinT = ph.sb("sinT", [P, T])
        ident = ph.sb("ident", [P, P])
        lat = ph.sb("lat", [P, 2, QR + KVR])
        sq = ph.sb("sq", [P, QR])
        ss = ph.sb("ss", [P, 2, 2])
        rs = ph.sb("rs", [P, 2, 2])
        eps = ph.sb("eps", [P, 1])
        rot = ph.sb("rot", [P, 2, 352])
        acc = ph.ps("acc", [P, 2, 2, 512])
        tp = ph.ps("tp", [P, 2, 512])
        tk = ph.ps("tk", [P, 2, 512])
        loaded, id_done, eps_done, done, squared, rooted, scaled, turned, out_done, v_own, a_own, rope_done, rope_out = (
            ph.sem(n) for n in ("loaded", "id_done", "eps_done", "done", "squared", "rooted", "scaled", "turned", "out_done",
                                "v_own", "a_own", "rope_done", "rope_out"))
        with nc.Block() as block:

            @block.sync
            def _(sp):
                for dst, src in ((wq, "w_dq_t"), (wk, "w_dkv_t"), (wr, "w_rope_t"), (gq, "cq_g_t"), (gk, "ckv_g_t"),
                                 (cosT, "cos_t"), (sinT, "sin_t")):
                    sp.dma_start(dst[:], D[src]).then_inc(loaded, 16)

            @block.gpsimd
            def _(pool):
                make_identity(nc, pool, ident, id_done)

            @block.tensor
            def _(pe):
                pe.wait_ge(loaded, 16 * 7)
                pe.wait_ge(id_done, 2)

                def turn(t):
                    pe.wait_ge(scaled, t + 1)
                    for n in range(QT + CT):
                        dst = tp[:, t % 2, P * n:P * n + P] if n < QT else tk[:, t % 2, P * (n - QT):P * (n - QT) + P]
                        last = nc.tensor.transpose(dst, lat[:, t % 2, P * n:P * n + P], ident[:])
                    last.then_inc(turned, 1)

                for t in range(TT):
                    if t >= 2:
                        pe.wait_ge(scaled, t - 1)
                        pe.wait_ge(out_done, t - 1)
                    for w, src, cols, c in ((wq, hq, QR, 0), (wk, hk, KVR, 1)):
                        for k in range(KT):
                            last = nc.tensor.matmul(acc[:, t % 2, c, 0:cols], src[:, k, P * t:P * t + P], w[:, k],
                                                    start=(k == 0), stop=(k == KT - 1))
                    last.then_inc(done, 1)
                    if t >= 1:
                        turn(t - 1)
                turn(TT - 1)
                pe.wait_ge(out_done, TT)
                for n, (at, cols) in enumerate(CUTS):
                    if n >= 2:
                        pe.wait_ge(rope_out, n - 1)
                    for s in range(2):
                        for k in range(KT):
                            last = nc.tensor.matmul(acc[:, n % 2, s, 0:cols], wr[:, k, s], hk[:, k, at:at + cols],
                                                    start=(k == 0), stop=(k == KT - 1))
                    last.then_inc(rope_done, 1)

            @block.scalar
            def _(act):
                a = Chain(act, a_own)
                act.wait_ge(eps_done, 1)
                for t in range(TT):
                    b = t % 2
                    act.wait_ge(done, t + 1)
                    if t >= 2:
                        act.wait_ge(scaled, t - 1)
                    a(nc.scalar.activation(sq[:], acc[:, b, 0, 0:QR], ACT.Square, accum_out=ss[:, b, 0:1]))
                    a(nc.scalar.activation(sq[:, 0:KVR], acc[:, b, 1, 0:KVR], ACT.Square, accum_out=ss[:, b, 1:2]))
                    nc.scalar.activation(ss[:, b, 0:1], ss[:, b, 0:1], ACT.Sqrt, scale=1.0 / QR, bias=eps[:])
                    nc.scalar.activation(ss[:, b, 1:2], ss[:, b, 1:2], ACT.Sqrt, scale=1.0 / KVR,
                                         bias=eps[:]).then_inc(rooted, 1)

            @block.vector
            def _(dve):
                v = Chain(dve, v_own)
                nc.vector.memset(eps[:], NORM_EPS).then_inc(eps_done, 1)
                v(nc.vector.memset(kr[:], 0.0))
                dve.wait_ge(loaded, 16 * 7)

                def evacuate(t):
                    dve.wait_ge(turned, t + 1)
                    nc.vector.tensor_tensor(cq[:, :, P * t:P * t + P],
                                            tp[:, t % 2, 0:QR].rearrange("p (k q) -> p k q", k=QT),
                                            gq[:].unsqueeze(2).to_broadcast([P, QT, P]), ALU.mult)
                    nc.vector.tensor_tensor(ckv[:, :, P * t:P * t + P],
                                            tk[:, t % 2, 0:KVR].rearrange("p (k q) -> p k q", k=CT),
                                            gk[:].unsqueeze(2).to_broadcast([P, CT, P]), ALU.mult).then_inc(out_done, 1)

                for t in range(TT):
                    b = t % 2
                    dve.wait_ge(rooted, t + 1)
                    v(nc.vector.reciprocal(rs[:, b], ss[:, b]))
                    if t >= 2:
                        dve.wait_ge(turned, t - 1)
                    nc.vector.tensor_scalar(lat[:, b, 0:QR], acc[:, b, 0, 0:QR], rs[:, b, 0:1], None, ALU.mult)
                    nc.vector.tensor_scalar(lat[:, b, QR:], acc[:, b, 1, 0:KVR], rs[:, b, 1:2], None,
                                            ALU.mult).then_inc(scaled, 1)
                    if t >= 1:
                        evacuate(t - 1)
                evacuate(TT - 1)
                for n, (at, cols) in enumerate(CUTS):
                    dve.wait_ge(rope_done, n + 1)
                    v.hold(nc.vector.tensor_tensor(rot[:, 0, 0:cols], acc[:, n % 2, 0, 0:cols], cosT[:, at:at + cols], ALU.mult))
                    v(nc.vector.tensor_tensor(rot[:, 1, 0:cols], acc[:, n % 2, 1, 0:cols], sinT[:, at:at + cols], ALU.mult))
                    for h in range(2):
                        hp = slice(HALF * h, HALF * h + HALF)
                        v.hold(nc.vector.tensor_tensor(kr[hp, h, at:at + cols], rot[hp, 0, 0:cols], rot[hp, 1, 0:cols], ALU.add))
                    v.wait()
                    dve.sem_inc(rope_out, 1)


def heads(nc, D, cq, ckv, kr, oT):
    QT, CT = QR // P, KVR // P
    with Phase(nc, "hd") as ph:
        wq = ph.sb("wq", [P, 2, QT, 4, P])
        wkv = ph.sb("wkv", [P, 2, CT, 4, P])
        cosT = ph.sb("cosT", [P, T])
        sinT = ph.sb("sinT", [P, T])
        qn = ph.sb("qn", [P, 2, TP])
        qr = ph.sb("qr", [P, TP])
        rot = ph.sb("rot", [P, 352])
        kn = ph.sb("kn", [P, 2, TP])
        vv = ph.sb("vv", [P, TT, 2, VD])
        pr = ph.sb("pr", [P, 2, TP])
        pT = ph.sb("pT", [P, 2, TT, P])
        mx = ph.sb("mx", [P, 2])
        nm = ph.sb("nm", [P, 2])
        ls = ph.sb("ls", [P, 2])
        rl = ph.sb("rl", [P, 2])
        osb = ph.sb("osb", [P, 2, VD])
        ident = ph.sb("ident", [P, P])
        mask = ph.sb("mask", [P, P])
        s_ps = ph.ps("s", [P, 3 * 512])
        t_ps = ph.ps("t", [P, 2, 512])
        o_ps = ph.ps("o", [P, 512])
        p_ps = ph.ps("p", [P, 2, 512])
        w_loaded = [ph.sem(f"w{n}_loaded") for n in range(2)]
        (tab_loaded, id_done, mask_done, w_used, pdone, pout, v_own, a_own, ready, scored, maxed, exped, turned, turned_out,
         mixed, normed, oturned, oout, sfree) = (ph.sem(n) for n in (
             "tab_loaded", "id_done", "mask_done", "w_used", "pdone", "pout", "v_own", "a_own", "ready", "scored", "maxed",
             "exped", "turned", "turned_out", "mixed", "normed", "oturned", "oout", "sfree"))
        NPAIR = HEADS // 2
        jobs = ([("qn", h, c) for h in range(2) for c in range(3)] + [("qa", 0, c) for c in range(3) for _ in (0,)]
                + [("kn", h, c) for h in range(2) for c in range(3)] + [("v", 0, t) for t in range(TT)])
        order = []
        for kind, h, c in jobs:
            order.append((kind, h, c))
            if kind == "qa":
                order.append(("qb", h, c))
        NJ = len(order)
        units = [(t, h) for t in range(TT) for h in range(2)]
        NU = len(units)

        def quads(t):
            return -(-(t + 1) // 4)
        NQ = sum(quads(t) for t, _ in units)
        qbase = [sum(quads(t) for t, _ in units[:n]) for n in range(NU)]
        with nc.Block() as block:

            @block.sync
            def _(sp):
                sp.dma_start(cosT[:], D["cos_t"]).then_inc(tab_loaded, 16)
                sp.dma_start(sinT[:], D["sin_t"]).then_inc(tab_loaded, 16)
                for j in range(NPAIR):
                    if j >= 2:
                        sp.wait_ge(pdone, NJ * (j - 1))
                    sp.dma_start(wq[:, j % 2], D["w_uq_t"][j]).then_inc(w_loaded[j % 2], 16)
                    sp.dma_start(wkv[:, j % 2], D["w_ukv_t"][j]).then_inc(w_loaded[j % 2], 16)

            @block.gpsimd
            def _(pool):
                make_identity(nc, pool, ident, id_done)
                nc.gpsimd.memset(mask[:], 0.0).then_inc(mask_done, 1)
                pool.wait_ge(mask_done, 1)
                nc.gpsimd.affine_select(out=mask[:], in_=mask[:], compare_op=ALU.is_ge, fill=MASKED, base=0,
                                        pattern=[[-1, P]], channel_multiplier=1).then_inc(mask_done, 1)

            @block.tensor
            def _(pe):
                mm = nc.tensor.matmul
                pe.wait_ge(id_done, 2)
                for j in range(NPAIR):
                    b = j % 2
                    pe.wait_ge(w_loaded[b], 32 * (j // 2 + 1))
                    for n, (kind, h, c) in enumerate(order):
                        m = NJ * j + n
                        if m >= 2:
                            pe.wait_ge(pout, m - 1)
                        bank = p_ps[:, m % 2]
                        if kind == "v":
                            for k in range(CT):
                                last = mm(bank[:, 0:2 * VD], ckv[:, k, P * c:P * c + P],
                                          wkv[:, b, k, 2:4].rearrange("p a b -> p (a b)"),
                                          start=(k == 0), stop=(k == CT - 1))
                        else:
                            at, cols = CUTS[c]
                            w, src, kt = (wkv, ckv, CT) if kind == "kn" else (wq, cq, QT)
                            which = {"kn": h, "qn": h, "qa": 2, "qb": 3}[kind]
                            for k in range(kt):
                                last = mm(bank[:, 0:cols], w[:, b, k, which], src[:, k, at:at + cols],
                                          start=(k == 0), stop=(k == kt - 1))
                        last.then_inc(pdone, 1)
                    pe.wait_ge(ready, j + 1)

                    def score(n):
                        t, h = units[n]
                        u = NU * j + n
                        if u >= 1:
                            pe.wait_ge(exped, u)
                        for c in range(quads(t)):
                            keys = min(P * (t + 1), T) - 512 * c
                            cols = min(512, keys)
                            bank = s_ps[:, 512 * c:512 * c + cols]
                            mm(bank, qn[:, h, P * t:P * t + P], kn[:, h, 512 * c:512 * c + cols], start=True, stop=False)
                            last = mm(bank, qr[:, P * t:P * t + P], kr[:, h, 512 * c:512 * c + cols], start=False, stop=True)
                        last.then_inc(scored, 1)

                    score(0)
                    for n, (t, h) in enumerate(units):
                        u = NU * j + n
                        pe.wait_ge(exped, u + 1)
                        if n + 1 < NU:
                            score(n + 1)
                        for c in range(quads(t)):
                            q = NQ * j + qbase[n] + c
                            if q >= 2:
                                pe.wait_ge(turned_out, q - 1)
                            for s in range(4 * c, min(4 * c + 4, t + 1)):
                                k = min(P, T - P * s)
                                last = nc.tensor.transpose(t_ps[0:k, q % 2, P * (s % 4):P * (s % 4) + P],
                                                           pr[:, u % 2, P * s:P * s + k], ident[:])
                            last.then_inc(turned, 1)
                        pe.wait_ge(turned_out, NQ * j + qbase[n] + quads(t))
                        if u >= 1:
                            pe.wait_ge(oout, u)
                        for s in range(t + 1):
                            k = min(P, T - P * s)
                            last = mm(o_ps[:, 0:VD], pT[0:k, u % 2, s], vv[0:k, s, h], start=(s == 0), stop=(s == t))
                        last.then_inc(mixed, 1)
                        pe.wait_ge(normed, u + 1)
                        nc.tensor.transpose(o_ps[:, P:2 * P], osb[:, u % 2], ident[:]).then_inc(oturned, 1)

            @block.scalar
            def _(act):
                a = Chain(act, a_own)
                for j in range(NPAIR):
                    for n, (t, h) in enumerate(units):
                        u = NU * j + n
                        act.wait_ge(maxed, u + 1)
                        if u >= 2:
                            act.wait_ge(mixed, u - 1)
                        keys = min(P * (t + 1), T)
                        nc.scalar.activation(pr[:, u % 2, 0:keys], s_ps[:, 0:keys], ACT.Exp, scale=ATT_SCALE,
                                             bias=nm[:, u % 2:u % 2 + 1], accum_out=ls[:, u % 2:u % 2 + 1]).then_inc(exped, 1)
                        for c in range(quads(t)):
                            q = NQ * j + qbase[n] + c
                            act.wait_ge(turned, q + 1)
                            full = [s for s in range(4 * c, min(4 * c + 4, t + 1)) if P * s + P <= T]
                            part = [s for s in range(4 * c, min(4 * c + 4, t + 1)) if P * s + P > T]
                            if full:
                                last = nc.scalar.copy(pT[:, u % 2, full[0]:full[-1] + 1],
                                                      t_ps[:, q % 2, 0:P * len(full)].rearrange("p (s q) -> p s q", q=P))
                            if part:
                                s = part[0]
                                last = nc.scalar.copy(pT[0:T - P * s, u % 2, s], t_ps[0:T - P * s, q % 2, P * (s % 4):P * (s % 4) + P])
                            last.then_inc(turned_out, 1)

            @block.vector
            def _(dve):
                v = Chain(dve, v_own)
                v.hold(nc.vector.memset(qn[:, :, T:], 0.0))
                v(nc.vector.memset(qr[:, T:], 0.0))
                dve.wait_ge(tab_loaded, 32)
                dve.wait_ge(mask_done, 2)
                for j in range(NPAIR):
                    if j:
                        dve.wait_ge(mixed, NU * j)
                    for n, (kind, h, c) in enumerate(order):
                        m = NJ * j + n
                        dve.wait_ge(pdone, m + 1)
                        bank = p_ps[:, m % 2]
                        if kind == "v":
                            v.hold(nc.vector.tensor_copy(vv[:, c].rearrange("p a b -> p (a b)"), bank[:, 0:2 * VD]))
                        else:
                            at, cols = CUTS[c]
                            if kind == "qn":
                                v.hold(nc.vector.tensor_copy(qn[:, h, at:at + cols], bank[:, 0:cols]))
                            elif kind == "kn":
                                v.hold(nc.vector.tensor_copy(kn[:, h, at:at + cols], bank[:, 0:cols]))
                            elif kind == "qa":
                                v(nc.vector.tensor_tensor(qr[:, at:at + cols], bank[:, 0:cols], cosT[:, at:at + cols], ALU.mult))
                            else:
                                v(nc.vector.tensor_tensor(rot[:, 0:cols], bank[:, 0:cols], sinT[:, at:at + cols], ALU.mult))
                                v(nc.vector.tensor_tensor(qr[:, at:at + cols], qr[:, at:at + cols], rot[:, 0:cols], ALU.add))
                        v.wait()
                        dve.sem_inc(pout, 1)
                    dve.sem_inc(ready, 1)
                    def finish(n):
                        u = NU * j + n
                        t, h = units[n]
                        b = u % 2
                        dve.wait_ge(mixed, u + 1)
                        v(nc.vector.reciprocal(rl[:, b:b + 1], ls[:, b:b + 1]))
                        nc.vector.tensor_scalar(osb[:, b], o_ps[:, 0:VD], rl[:, b:b + 1], None, ALU.mult).then_inc(normed, 1)
                        dve.wait_ge(oturned, u + 1)
                        nc.vector.tensor_copy(oT[:, 2 * j + h, P * t:P * t + P], o_ps[:, P:2 * P]).then_inc(oout, 1)

                    for n, (t, h) in enumerate(units):
                        u = NU * j + n
                        dve.wait_ge(scored, u + 1)
                        keys = min(P * (t + 1), T)
                        diag = s_ps[:, P * t:keys]
                        v(nc.vector.tensor_tensor(diag, diag, mask[:, 0:keys - P * t], ALU.add))
                        v(nc.vector.tensor_reduce(mx[:, u % 2:u % 2 + 1], s_ps[:, 0:keys], AX.X, ALU.max))
                        nc.vector.tensor_scalar(nm[:, u % 2:u % 2 + 1], mx[:, u % 2:u % 2 + 1], -ATT_SCALE, None,
                                                ALU.mult).then_inc(maxed, 1)
                        if n >= 1:
                            finish(n - 1)
                    finish(NU - 1)

QUEUE_ROWS = SLOTS // P
SPILL_PAIRS = SPILL_BLOCKS // 2
LG = GROUPS + EXPERTS
BIG = 1.0e30
ROUTE_CUT = TT * EXPERTS // 2


def moe(nc, D, layer, h_in, h_out):
    with Phase(nc, f"mo{layer}") as pm:
        slot_f = pm.sb("slot_f", [P, TT, 2])
        dest = pm.sb("dest", [P, TT, 2], I32)
        gate = pm.sb("gate", [P, TT, 2])
        queue = pm.sb("queue", [P, QUEUE_ROWS], I32)
        spill = pm.sb("spill", [1, SPILL_BLOCKS + 1], I32)
        route(nc, D, layer, h_in, slot_f, dest, gate, queue, spill)
        experts(nc, D, layer, queue, spill)
        combine(nc, D, h_in, h_out, dest, gate)


def route(nc, D, layer, h_in, slot_f, dest, gate, queue, spill):
    with Phase(nc, "rt") as ph:
        NBUF = 3
        hb = ph.sb("hb", [P, NBUF, DM])
        hn = ph.sb("hn", [P, 2, DM])
        hnT = ph.sb("hnT", [P, 2, KT, P])
        gb = ph.sb("gb", [P, DM])
        wr = ph.sb("wr", [P, KT, LG])
        sq = ph.sb("sq", [P, DM])
        ss = ph.sb("ss", [P, NBUF])
        rt = ph.sb("rt", [P, NBUF])
        rs = ph.sb("rs", [P, NBUF])
        eps = ph.sb("eps", [P, 1])
        ident = ph.sb("ident", [P, P])
        lg = ph.sb("lg", [P, TT, LG])
        tp = ph.ps("tp", [P, 2, 2, 512])
        lg_ps = ph.ps("lg_ps", [P, 512])
        rk_ps = ph.ps("rk_ps", [P, 2, 512])
        zero_q = ph.sb("zero_q", [P, QUEUE_ROWS], I32)
        zero_y = ph.sb("zero_y", [P, DM])
        ys_zero = ph.sem("ys_zero")
        up = ph.sb("up", [P, P])
        ones = ph.sb("ones", [P, P])
        valid = ph.sb("valid", [P, TT])
        pri = ph.sb("pri", [P, 8])
        pri_i = ph.sb("pri_i", [P, 8], I32)
        first = ph.sb("first", [P, EXPERTS])
        first_i = ph.sb("first_i", [P, EXPERTS], I32)
        steps = ph.sb("steps", [P, PER_EXPERT_SPILL])
        steps_i = ph.sb("steps_i", [P, PER_EXPERT_SPILL], I32)
        blocks = ph.sb("blocks", [P, SPILL_BLOCKS])
        blocks_i = ph.sb("blocks_i", [P, SPILL_BLOCKS], I32)
        tok = ph.sb("tok", [P, TT], I32)
        m8 = ph.sb("m8", [P, TT])
        cand = ph.sb("cand", [P, TT, 8])
        ohg = ph.sb("ohg", [P, TT, 8])
        gexp = ph.sb("gexp", [P, TT, 8])
        pg = ph.sb("pg", [P, TT])
        ein = ph.sb("ein", [P, TT, 8])
        oh = ph.sb("oh", [P, 2, TT, 8])
        top = ph.sb("top", [P, 2, TT])
        ed = ph.sb("ed", [P, TT])
        big = ph.sb("big", [P, TT, EXPERTS])
        chosen = ph.sb("chosen", [P, 2, TT, EXPERTS])
        both = ph.sb("both", [P, TT, EXPERTS])
        base = ph.sb("base", [P, TT + 1, EXPERTS])
        rank = ph.sb("rank", [P, TT, EXPERTS])
        over = ph.sb("over", [P, EXPERTS, PER_EXPERT_SPILL])
        nspill = ph.sb("nspill", [P, EXPERTS])
        send = ph.sb("send", [P, EXPERTS])
        jump = ph.sb("jump", [P, EXPERTS])
        owner = ph.sb("owner", [1, SPILL_BLOCKS, EXPERTS])
        owners = ph.sb("owners", [1, SPILL_BLOCKS + 1])
        ones_row = ph.sb("ones_row", [P, EXPERTS])
        h_loaded = [ph.sem(f"h{n}_loaded") for n in range(NBUF)]
        hn_stored = [ph.sem(f"hn{n}_stored") for n in range(2)]
        (w_loaded, const_done, rooted, scaled, turned, evac, lg_done, lg_out, v_own, a_own, soft_in, soft_out, diff_in,
         diff_out, picked, ranked, totals_out, totals_done, slots_ready, queue_zero, scattered, queue_loaded,
         consts_cast) = (ph.sem(n) for n in (
             "w_loaded", "const_done", "rooted", "scaled", "turned", "evac", "lg_done", "lg_out", "v_own", "a_own", "soft_in",
             "soft_out", "diff_in", "diff_out", "picked", "ranked", "totals_out", "totals_done", "slots_ready", "queue_zero",
             "scattered", "queue_loaded", "consts_cast"))
        table, hn_dram = D["table"], D["hn"]
        with nc.Block() as block:

            @block.sync
            def _(sp):
                sp.dma_start(wr[:], D["w_route_t"][layer]).then_inc(w_loaded, 16)
                sp.dma_start(gb[:], D["norm_ffn_g_2"][layer].partition_broadcast(P)).then_inc(w_loaded, 16)
                for t in range(TT):
                    if t >= NBUF:
                        sp.wait_ge(scaled, t - NBUF + 1)
                    sp.dma_start(hb[:, t % NBUF], h_in[P * t:P * t + P]).then_inc(h_loaded[t % NBUF], 16)

            @block.gpsimd
            def _(pool):
                g = nc.gpsimd
                for m in (ident, up, ones, valid, zero_q, zero_y):
                    g.memset(m[:], 0 if m is zero_q else 0.0 if m is ident or m is zero_y else 1.0).then_inc(const_done, 1)
                g.iota(pri_i[:], pattern=[[-1, 8]], base=8, channel_multiplier=0).then_inc(const_done, 1)
                g.iota(first_i[:], pattern=[[CAP, EXPERTS]], base=0, channel_multiplier=0).then_inc(const_done, 1)
                g.iota(steps_i[:], pattern=[[CAP, PER_EXPERT_SPILL]], base=CAP, channel_multiplier=0).then_inc(const_done, 1)
                g.iota(blocks_i[:], pattern=[[1, SPILL_BLOCKS]], base=0, channel_multiplier=0).then_inc(const_done, 1)
                g.iota(tok[:], pattern=[[P, TT]], base=0, channel_multiplier=1).then_inc(const_done, 1)
                pool.wait_ge(const_done, 11)
                g.affine_select(out=ident[:], in_=ident[:], compare_op=ALU.not_equal, fill=1.0, base=0,
                                pattern=[[-1, P]], channel_multiplier=1).then_inc(const_done, 1)
                g.affine_select(out=up[:], in_=up[:], compare_op=ALU.is_gt, fill=0.0, base=0,
                                pattern=[[1, P]], channel_multiplier=-1).then_inc(const_done, 1)
                g.affine_select(out=valid[:], in_=valid[:], compare_op=ALU.is_gt, fill=0.0, base=T,
                                pattern=[[-P, TT]], channel_multiplier=-1).then_inc(const_done, 1)
                if layer == 0:
                    for n in range(SPILL_BLOCKS * CAP // P):
                        pool.dma_start(D["ys"][MAIN_SLOTS + P * n:MAIN_SLOTS + P * n + P], zero_y[:]).then_inc(ys_zero, 16)
                pool.dma_start(table.rearrange("(p q) a -> p (q a)", p=P), zero_q[:]).then_inc(queue_zero, 16)
                pool.wait_ge(queue_zero, 16)
                pool.wait_ge(slots_ready, 1)
                for t in range(TT):
                    for c in range(2):
                        g.indirect_dma_start(table[:, :], bass.IndirectOffsetOnAxis(ap=dest[0:rows_of(t), t, c:c + 1], axis=0),
                                             tok[0:rows_of(t), t:t + 1], None).then_inc(scattered, 16)
                pool.wait_ge(scattered, 16 * 2 * TT)
                pool.dma_start(queue[:], table.rearrange("(q p) a -> p (q a)", p=P), allow_slow_non_contiguous=True).then_inc(queue_loaded, 16)
                pool.wait_ge(queue_loaded, 16)
                if layer == 0:
                    pool.wait_ge(ys_zero, 16 * (SPILL_BLOCKS * CAP // P))

            @block.scalar
            def _(act):
                a = Chain(act, a_own)
                act.wait_ge(consts_cast, 1)
                for t in range(TT):
                    b = t % NBUF
                    act.wait_ge(h_loaded[b], 16 * (t // NBUF + 1))
                    if t >= NBUF:
                        act.wait_ge(scaled, t - NBUF + 1)
                    a(nc.scalar.activation(sq[:], hb[:, b], ACT.Square, accum_out=ss[:, b:b + 1]))
                    nc.scalar.activation(rt[:, b:b + 1], ss[:, b:b + 1], ACT.Sqrt, scale=1.0 / DM,
                                         bias=eps[:]).then_inc(rooted, 1)
                    act.wait_ge(scaled, t + 1)
                    act.dma_start(hn_dram[P * t:P * t + P], hn[:, t % 2]).then_inc(hn_stored[t % 2], 16)
                act.wait_ge(soft_in, 1)
                nc.scalar.activation(gexp[:], gexp[:], ACT.Exp).then_inc(soft_out, 1)
                act.wait_ge(diff_in, 1)
                nc.scalar.activation(ed[:], ed[:], ACT.Exp).then_inc(diff_out, 1)
                for b in range(2):
                    act.wait_ge(hn_stored[b], 16 * ((TT + 1 - b) // 2))

            @block.tensor
            def _(pe):
                pe.wait_ge(const_done, 14)
                pe.wait_ge(w_loaded, 32)
                for t in range(TT):
                    pe.wait_ge(scaled, t + 1)
                    if t >= 2:
                        pe.wait_ge(evac, t - 1)
                    for k in range(KT):
                        last = nc.tensor.transpose(tp[:, t % 2, k // 4, P * (k % 4):P * (k % 4) + P],
                                                   hn[:, t % 2, P * k:P * k + P], ident[:])
                    last.then_inc(turned, 1)
                    pe.wait_ge(evac, t + 1)
                    if t >= 1:
                        pe.wait_ge(lg_out, t)
                    for k in range(KT):
                        last = nc.tensor.matmul(lg_ps[:, 0:LG], hnT[:, t % 2, k], wr[:, k], start=(k == 0), stop=(k == KT - 1))
                    last.then_inc(lg_done, 1)
                pe.wait_ge(picked, 1)
                flat = both[:].rearrange("p t e -> p (t e)")
                for n, m in enumerate((ones, up)):
                    if n:
                        pe.wait_ge(totals_out, 1)
                    for c in range(2):
                        last = nc.tensor.matmul(rk_ps[:, c, 0:ROUTE_CUT], m[:], flat[:, ROUTE_CUT * c:ROUTE_CUT * c + ROUTE_CUT],
                                                start=True, stop=True)
                    last.then_inc(totals_done if n == 0 else ranked, 1)

            @block.vector
            def _(dve):
                v = Chain(dve, v_own)
                V = nc.vector
                tt, ts, stt, red = V.tensor_tensor, V.tensor_scalar, V.scalar_tensor_tensor, V.tensor_reduce
                dve.wait_ge(const_done, 14)
                v.hold(V.memset(eps[:], NORM_EPS))
                v.hold(V.memset(ones_row[:], 1.0))
                for dst, src in ((pri, pri_i), (first, first_i), (steps, steps_i), (blocks, blocks_i)):
                    v.hold(V.tensor_copy(dst[:], src[:]))
                v.wait()
                dve.sem_inc(consts_cast, 1)
                dve.wait_ge(w_loaded, 32)

                def evacuate(t):
                    dve.wait_ge(turned, t + 1)
                    if t >= 2:
                        dve.wait_ge(lg_done, t - 1)
                    V.tensor_copy(hnT[:, t % 2].rearrange("p k q -> p (k q)"),
                                  tp[:, t % 2].rearrange("p a b -> p (a b)")).then_inc(evac, 1)
                    dve.wait_ge(lg_done, t + 1)
                    V.tensor_copy(lg[:, t], lg_ps[:, 0:LG]).then_inc(lg_out, 1)

                for t in range(TT):
                    b = t % NBUF
                    dve.wait_ge(rooted, t + 1)
                    v(V.reciprocal(rs[:, b:b + 1], rt[:, b:b + 1]))
                    if t >= 2:
                        dve.wait_ge(turned, t - 1)
                        dve.wait_ge(hn_stored[t % 2], 16 * (t // 2))
                    stt(out=hn[:, t % 2], in0=hb[:, b], scalar=rs[:, b:b + 1], in1=gb[:], op0=ALU.mult,
                        op1=ALU.mult).then_inc(scaled, 1)
                    if t >= 1:
                        evacuate(t - 1)
                evacuate(TT - 1)
                dve.wait_ge(lg_out, TT)

                def wide(x, n=8):
                    return x.unsqueeze(2).to_broadcast([P, TT, n])

                def row8(x):
                    return x.unsqueeze(1).to_broadcast([P, TT, 8])

                def first_max(values, best, hot):
                    v(red(best, values, AX.X, ALU.max))
                    v(tt(cand[:], values, wide(best), ALU.is_equal))
                    v(tt(cand[:], cand[:], row8(pri[:]), ALU.mult))
                    v(red(m8[:], cand[:], AX.X, ALU.max))
                    v(tt(hot, cand[:], wide(m8[:]), ALU.is_equal))

                groups = lg[:, :, 0:GROUPS]
                first_max(groups, pg[:], ohg[:])
                v(tt(gexp[:], groups, wide(pg[:]), ALU.subtract))
                dve.sem_inc(soft_in, 1)
                el = lg[:, :, GROUPS:].rearrange("p t (g e) -> p t g e", g=GROUPS)
                bg = big[:].rearrange("p t (g e) -> p t g e", g=GROUPS)
                for t in range(TT):
                    v.hold(tt(bg[:, t], el[:, t], ohg[:, t].unsqueeze(2).to_broadcast([P, GROUPS, 8]), ALU.mult))
                v.wait()
                v(red(ein[:], bg.rearrange("p t g e -> p t e g"), AX.X, ALU.add))
                first_max(ein[:], top[:, 0], oh[:, 0])
                v(stt(out=ein[:], in0=oh[:, 0], scalar=-BIG, in1=ein[:], op0=ALU.mult, op1=ALU.add))
                first_max(ein[:], top[:, 1], oh[:, 1])
                v(tt(ed[:], top[:, 1], top[:, 0], ALU.subtract))
                dve.sem_inc(diff_in, 1)
                dve.wait_ge(soft_out, 1)
                v(red(pg[:], gexp[:], AX.X, ALU.add))
                v(V.reciprocal(pg[:], pg[:]))
                dve.wait_ge(diff_out, 1)
                v(ts(m8[:], ed[:], 1.0, None, ALU.add))
                v(V.reciprocal(m8[:], m8[:]))
                v(tt(gate[:, :, 0], pg[:], m8[:], ALU.mult))
                v(tt(gate[:, :, 1], gate[:, :, 0], ed[:], ALU.mult))
                v(tt(ohg[:], ohg[:], wide(valid[:]), ALU.mult))
                for c in range(2):
                    for t in range(TT):
                        v.hold(tt(chosen[:, c, t].rearrange("p (g e) -> p g e", g=GROUPS),
                                  ohg[:, t].unsqueeze(2).to_broadcast([P, GROUPS, 8]),
                                  oh[:, c, t].unsqueeze(1).to_broadcast([P, GROUPS, 8]), ALU.mult))
                v.wait()
                v(tt(both[:], chosen[:, 0], chosen[:, 1], ALU.add))
                dve.sem_inc(picked, 1)
                dve.wait_ge(totals_done, 1)
                cut = lambda x, c: x.rearrange("p t e -> p (t e)")[:, ROUTE_CUT * c:ROUTE_CUT * c + ROUTE_CUT]
                for c in range(2):
                    v.hold(V.tensor_copy(cut(big[:], c), rk_ps[:, c, 0:ROUTE_CUT]))
                v(V.memset(base[:, 0], 0.0))
                dve.sem_inc(totals_out, 1)
                for t in range(TT):
                    v(tt(base[:, t + 1], base[:, t], big[:, t], ALU.add))
                dve.wait_ge(ranked, 1)
                for c in range(2):
                    v.hold(tt(cut(rank[:], c), rk_ps[:, c, 0:ROUTE_CUT], cut(base[:, 0:TT], c), ALU.add))
                v.wait()
                v(tt(over[:], base[:, TT].unsqueeze(2).to_broadcast([P, EXPERTS, PER_EXPERT_SPILL]),
                     steps[:].unsqueeze(1).to_broadcast([P, EXPERTS, PER_EXPERT_SPILL]), ALU.is_gt))
                v(red(nspill[:], over[:], AX.X, ALU.add))
                v(V.tensor_tensor_scan(send[:], ones_row[:], nspill[:], 0.0, ALU.mult, ALU.add))
                v(tt(jump[:], send[:], nspill[:], ALU.subtract))
                v(ts(jump[:], jump[:], float(CAP), float(MAIN_SLOTS - CAP), ALU.mult, ALU.add))
                v(tt(jump[:], jump[:], first[:], ALU.subtract))
                v(ts(big[:], rank[:], float(CAP), None, ALU.is_ge))
                for x, op in ((jump, ALU.mult), (first, ALU.add)):
                    v(tt(big[:], big[:], x[:].unsqueeze(1).to_broadcast([P, TT, EXPERTS]), op))
                v(tt(rank[:], rank[:], big[:], ALU.add))
                for c in range(2):
                    v(tt(big[:], rank[:], chosen[:, c], ALU.mult))
                    v(red(slot_f[:, :, c], big[:], AX.X, ALU.add))
                v(V.tensor_copy(dest[:], slot_f[:]))
                dve.sem_inc(slots_ready, 1)
                v(tt(owner[:], send[0:1].unsqueeze(1).to_broadcast([1, SPILL_BLOCKS, EXPERTS]),
                     blocks[0:1].unsqueeze(2).to_broadcast([1, SPILL_BLOCKS, EXPERTS]), ALU.is_le))
                v(red(owners[:, 0:SPILL_BLOCKS], owner[:], AX.X, ALU.add))
                v(ts(owners[:, 0:SPILL_BLOCKS], owners[:, 0:SPILL_BLOCKS], float(EXPERTS - 1), None, ALU.min))
                v(V.tensor_copy(owners[:, SPILL_BLOCKS:], send[0:1, EXPERTS - 1:]))
                v(V.tensor_copy(spill[:], owners[:]))


def experts(nc, D, layer, queue, spill):
    with Phase(nc, "ex") as ph:
        wgu = ph.sb("wgu", [P, 2, 2, 2, KT, DE])
        wd = ph.sb("wd", [P, 2, 2, 2, DM])
        ib = ph.sb("ib", [P, 2], I32)
        xe = ph.sb("xe", [P, 2, DM])
        xT = ph.sb("xT", [P, 2, KT, P])
        sg = ph.sb("sg", [P, 2, DE])
        hs = ph.sb("hs", [P, 2, DE])
        hT = ph.sb("hT", [P, 2, 2, P])
        ysb = ph.sb("ysb", [P, 2, DM])
        ident = ph.sb("ident", [P, P])
        x_ps = ph.ps("x_ps", [P, 2, 512])
        h_ps = ph.ps("h_ps", [P, 2, 512])
        ht_ps = ph.ps("ht_ps", [P, 2, 512])
        y_ps = ph.ps("y_ps", [P, 2, 512])
        id_done = ph.sem("id_done")
        names = ["gu_loaded", "gu_used", "d_loaded", "d_used", "idx_ready", "x_loaded", "x_used", "x_turned", "xT_out",
                 "h_done", "silu_done", "h_out", "h_turned", "hT_out", "y_done", "y_out", "y_stored", "stored_seen"]
        S = [{n: ph.sem(f"{n}{b}") for n in names} for b in range(3)]
        wg_d, wu_d, wd_d = D["w_gate_2"][layer], D["w_up_2"][layer], D["w_down_2"][layer]
        hn_dram, ys = D["hn"], D["ys"]

        def gate_up_loads(sp, b, s, pair):
            for n, e in enumerate(pair):
                for c, src in enumerate((wg_d, wu_d)):
                    sp.dma_start(wgu[:, b, n, c], src[bass.ds(e, 1)].rearrange("a (p k) f -> (a p) k f", k=KT)
                                 ).then_inc(s["gu_loaded"], 16)

        def down_loads(sp, b, s, pair):
            for n, e in enumerate(pair):
                sp.dma_start(wd[:, b, n], wd_d[bass.ds(e, 1)].rearrange("a (p k) f -> (a p) k f", k=2)
                             ).then_inc(s["d_loaded"], 16)

        def gather(pool, b, s, row):
            pool.sem_inc(s["idx_ready"], 1)
            nc.gpsimd.tensor_copy(ib[:, b:b + 1], queue[:, bass.ds(row, 1)]).then_inc(s["idx_ready"], 1)
            pool.wait_ge(s["idx_ready"], 2)
            nc.gpsimd.indirect_dma_start(xe[:, b], None, hn_dram[:, :], bass.IndirectOffsetOnAxis(ap=ib[:, b:b + 1], axis=0)
                                         ).then_inc(s["x_loaded"], 16)
            pool.sem_clear(s["idx_ready"])

        def products(pe, b, s, count):
            pe.wait_ge(s["x_loaded"], 16 * count)
            for k in range(KT):
                last = nc.tensor.transpose(x_ps[:, k // 4, P * (k % 4):P * (k % 4) + P], xe[:, b, k::KT], ident[:])
            last.then_inc(s["x_turned"], 1)
            pe.wait_ge(s["xT_out"], 2 * count)
            pe.wait_ge(s["gu_loaded"], 64 * count)
            for k in range(KT):
                for n in range(2):
                    half = slice(CAP * n, CAP * n + CAP)
                    last = nc.tensor.matmul(h_ps[half, b].rearrange("p (a b) -> p a b", a=2), xT[:, b, k, half],
                                            wgu[:, b, n, :, k], start=(k == 0), stop=(k == KT - 1))
            last.then_inc(s["h_done"], 1)
            pe.wait_ge(s["h_out"], count)
            for k in range(2):
                last = nc.tensor.transpose(ht_ps[:, b, P * k:P * k + P], hs[:, b, k::2], ident[:])
            last.then_inc(s["h_turned"], 1)
            pe.wait_ge(s["hT_out"], count)
            pe.wait_ge(s["d_loaded"], 32 * count)
            for c in range(2):
                for k in range(2):
                    for n in range(2):
                        half = slice(CAP * n, CAP * n + CAP)
                        last = nc.tensor.matmul(y_ps[half, c], hT[:, b, k, half], wd[:, b, n, k, 512 * c:512 * c + 512],
                                                start=(k == 0), stop=(k == 1))
            last.then_inc(s["y_done"], 1)
            pe.wait_ge(s["y_out"], 2 * count)

        def scalar_part(act, b, s, row, count):
            act.wait_ge(s["x_turned"], count)
            nc.scalar.copy(xT[:, b, 0:4].rearrange("p k q -> p (k q)"), x_ps[:, 0]).then_inc(s["xT_out"], 1)
            act.wait_ge(s["h_done"], count)
            nc.scalar.activation(sg[:, b], h_ps[:, b, 0:DE], ACT.Silu).then_inc(s["silu_done"], 1)
            act.wait_ge(s["h_turned"], count)
            nc.scalar.copy(hT[:, b].rearrange("p k q -> p (k q)"), ht_ps[:, b, 0:2 * P]).then_inc(s["hT_out"], 1)
            act.wait_ge(s["y_done"], count)
            nc.scalar.copy(ysb[:, b, 0:512], y_ps[:, 0]).then_inc(s["y_out"], 1)
            act.wait_ge(s["y_out"], 2 * count)
            act.dma_start(ys[bass.ds(row * P, P)], ysb[:, b]).then_inc(s["y_stored"], 16)

        def vector_part(dve, b, s, count, before):
            dve.wait_ge(s["x_turned"], count)
            nc.vector.tensor_copy(xT[:, b, 4:8].rearrange("p k q -> p (k q)"), x_ps[:, 1]).then_inc(s["xT_out"], 1)
            dve.wait_ge(s["silu_done"], count)
            nc.vector.tensor_tensor(hs[:, b], sg[:, b], h_ps[:, b, DE:], ALU.mult).then_inc(s["h_out"], 1)
            dve.wait_ge(s["y_done"], count)
            before()
            nc.vector.tensor_copy(ysb[:, b, 512:], y_ps[:, 1]).then_inc(s["y_out"], 1)

        MAIN = PAIRS_M // 2
        with nc.Block() as block:

            @block.sync
            def _(sp):
                with sp.Fori(0, MAIN) as i:
                    for b in range(2):
                        s = S[b]
                        pair = [4 * i + 2 * b, 4 * i + 2 * b + 1]
                        sp.wait_ge(s["gu_used"], i + 1)
                        gate_up_loads(sp, b, s, pair)
                        sp.wait_ge(s["d_used"], i + 1)
                        down_loads(sp, b, s, pair)

            @block.gpsimd
            def _(pool):
                make_identity(nc, pool, ident, id_done)
                with pool.Fori(0, MAIN) as i:
                    for b in range(2):
                        s = S[b]
                        pool.wait_ge(s["x_used"], i + 1)
                        gather(pool, b, s, 2 * i + b)

            @block.tensor
            def _(pe):
                pe.wait_ge(id_done, 2)
                for b in range(2):
                    for n in ("gu_used", "d_used", "x_used"):
                        pe.sem_inc(S[b][n], 1)
                with pe.Fori(0, MAIN) as i:
                    for b in range(2):
                        products(pe, b, S[b], i + 1)
                        for n in ("gu_used", "d_used", "x_used"):
                            pe.sem_inc(S[b][n], 1)

            @block.scalar
            def _(act):
                for b in range(2):
                    act.sem_inc(S[b]["y_stored"], 16)
                with act.Fori(0, MAIN) as i:
                    for b in range(2):
                        act.wait_ge(S[b]["y_stored"], 16 * i + 16)
                        scalar_part(act, b, S[b], 2 * i + b, i + 1)
                for b in range(2):
                    act.wait_ge(S[b]["y_stored"], 16 * MAIN + 16)

            @block.vector
            def _(dve):
                with dve.Fori(0, MAIN) as i:
                    for b in range(2):
                        vector_part(dve, b, S[b], i + 1, lambda: dve.wait_ge(S[b]["y_stored"], 16 * i + 16))

        s = S[2]
        with nc.Block() as block:

            def spilled(eng):
                return eng.value_load(spill[0:1, SPILL_BLOCKS:], min_val=0, max_val=SPILL_BLOCKS)

            @block.sync
            def _(sp):
                total = spilled(sp)
                with sp.Fori(0, SPILL_PAIRS) as i:
                    with sp.If(2 * i < total):
                        sp.wait_ge(s["gu_used"], i + 1)
                        pair = [sp.value_load(spill[0:1, bass.ds(2 * i + n, 1)], min_val=0, max_val=EXPERTS - 1)
                                for n in range(2)]
                        gate_up_loads(sp, 0, s, pair)
                        down_loads(sp, 0, s, pair)

            @block.gpsimd
            def _(pool):
                total = spilled(pool)
                with pool.Fori(0, SPILL_PAIRS) as i:
                    with pool.If(2 * i < total):
                        pool.wait_ge(s["x_used"], i + 1)
                        gather(pool, 0, s, PAIRS_M + i)

            @block.tensor
            def _(pe):
                for n in ("gu_used", "x_used"):
                    pe.sem_inc(s[n], 1)
                total = spilled(pe)
                with pe.Fori(0, SPILL_PAIRS) as i:
                    with pe.If(2 * i < total):
                        products(pe, 0, s, i + 1)
                        for n in ("gu_used", "x_used"):
                            pe.sem_inc(s[n], 1)

            @block.scalar
            def _(act):
                total = spilled(act)
                with act.Fori(0, SPILL_PAIRS) as i:
                    with act.If(2 * i < total):
                        scalar_part(act, 0, s, PAIRS_M + i, i + 1)
                        act.wait_ge(s["y_stored"], 16 * i + 16)
                        act.sem_inc(s["stored_seen"], 1)

            @block.vector
            def _(dve):
                total = spilled(dve)
                dve.sem_inc(s["stored_seen"], 1)
                with dve.Fori(0, SPILL_PAIRS) as i:
                    with dve.If(2 * i < total):
                        vector_part(dve, 0, s, i + 1, lambda: dve.wait_ge(s["stored_seen"], i + 1))


def combine(nc, D, h_in, h_out, dest, gate):
    with Phase(nc, "cb") as ph:
        NBUF = 3
        hb = ph.sb("hb", [P, NBUF, DM])
        yb = ph.sb("yb", [P, NBUF, 2, DM])
        ho = ph.sb("ho", [P, 2, DM])
        zero_done, v_own, summed = ph.sem("zero_done"), ph.sem("v_own"), ph.sem("summed")
        loaded = [ph.sem(f"h{n}_loaded") for n in range(NBUF)]
        gathered = [ph.sem(f"y{n}_gathered") for n in range(NBUF)]
        stored = [ph.sem(f"h{n}_stored") for n in range(2)]
        with nc.Block() as block:

            @block.sync
            def _(sp):
                for t in range(TT):
                    if t >= NBUF:
                        sp.wait_ge(summed, t - NBUF + 1)
                    sp.dma_start(hb[:, t % NBUF], h_in[P * t:P * t + P]).then_inc(loaded[t % NBUF], 16)

            @block.gpsimd
            def _(pool):
                pool.wait_ge(zero_done, 1)
                for t in range(TT):
                    if t >= NBUF:
                        pool.wait_ge(summed, t - NBUF + 1)
                    for c in range(2):
                        r = rows_of(t)
                        nc.gpsimd.indirect_dma_start(yb[0:r, t % NBUF, c], None, D["ys"][:, :],
                                                     bass.IndirectOffsetOnAxis(ap=dest[0:r, t, c:c + 1], axis=0)
                                                     ).then_inc(gathered[t % NBUF], 16)

            @block.scalar
            def _(act):
                for t in range(TT):
                    act.wait_ge(summed, t + 1)
                    act.dma_start(h_out[P * t:P * t + P], ho[:, t % 2]).then_inc(stored[t % 2], 16)
                for b in range(2):
                    act.wait_ge(stored[b], 16 * ((TT + 1 - b) // 2))

            @block.vector
            def _(dve):
                v = Chain(dve, v_own)
                nc.vector.memset(yb[:], 0.0).then_inc(zero_done, 1)
                for t in range(TT):
                    dve.wait_ge(loaded[t % NBUF], 16 * (t // NBUF + 1))
                    dve.wait_ge(gathered[t % NBUF], 32 * (t // NBUF + 1))
                    if t >= 2:
                        dve.wait_ge(stored[t % 2], 16 * (t // 2))
                    v(nc.vector.scalar_tensor_tensor(out=ho[:, t % 2], in0=yb[:, t % NBUF, 0], scalar=gate[:, t, 0:1],
                                                     in1=hb[:, t % NBUF], op0=ALU.mult, op1=ALU.add))
                    nc.vector.scalar_tensor_tensor(out=ho[:, t % 2], in0=yb[:, t % NBUF, 1], scalar=gate[:, t, 1:2],
                                                   in1=ho[:, t % 2], op0=ALU.mult, op1=ALU.add).then_inc(summed, 1)


def final_norm(nc, D, h):
    with Phase(nc, "fn") as ph:
        NBUF = 3
        hb = ph.sb("hb", [P, NBUF, DM])
        ho = ph.sb("ho", [P, NBUF, DM])
        gb = ph.sb("gb", [P, DM])
        sq = ph.sb("sq", [P, DM])
        ss = ph.sb("ss", [P, NBUF])
        rs = ph.sb("rs", [P, NBUF])
        eps = ph.sb("eps", [P, 1])
        g_loaded, eps_done, rooted, scaled, v_own, a_own = (
            ph.sem(n) for n in ("g_loaded", "eps_done", "rooted", "scaled", "v_own", "a_own"))
        loaded = [ph.sem(f"h{n}_loaded") for n in range(NBUF)]
        stored = [ph.sem(f"o{n}_stored") for n in range(NBUF)]
        with nc.Block() as block:

            @block.sync
            def _(sp):
                sp.dma_start(gb[:], D["final_norm_g_2"].partition_broadcast(P)).then_inc(g_loaded, 16)
                for t in range(NB):
                    if t >= NBUF:
                        sp.wait_ge(scaled, t - NBUF + 1)
                    sp.dma_start(hb[:, t % NBUF], h[META + P * t:META + P * t + P]).then_inc(loaded[t % NBUF], 16)

            @block.scalar
            def _(act):
                a = Chain(act, a_own)
                act.wait_ge(eps_done, 1)
                for t in range(NB):
                    b = t % NBUF
                    act.wait_ge(loaded[b], 16 * (t // NBUF + 1))
                    if t >= NBUF:
                        act.wait_ge(scaled, t - NBUF + 1)
                    a(nc.scalar.activation(sq[:], hb[:, b], ACT.Square, accum_out=ss[:, b:b + 1]))
                    nc.scalar.activation(ss[:, b:b + 1], ss[:, b:b + 1], ACT.Sqrt, scale=1.0 / DM,
                                         bias=eps[:]).then_inc(rooted, 1)
                    act.wait_ge(scaled, t + 1)
                    act.dma_start(D["out"][P * t:P * t + P], ho[:, b]).then_inc(stored[b], 16)
                for b in range(NBUF):
                    act.wait_ge(stored[b], 16 * ((NB + NBUF - 1 - b) // NBUF))

            @block.vector
            def _(dve):
                v = Chain(dve, v_own)
                nc.vector.memset(eps[:], NORM_EPS).then_inc(eps_done, 1)
                dve.wait_ge(g_loaded, 16)
                for t in range(NB):
                    b = t % NBUF
                    dve.wait_ge(rooted, t + 1)
                    v(nc.vector.reciprocal(rs[:, b:b + 1], ss[:, b:b + 1]))
                    if t >= NBUF:
                        dve.wait_ge(stored[b], 16 * (t // NBUF))
                    nc.vector.scalar_tensor_tensor(out=ho[:, b], in0=hb[:, b], scalar=rs[:, b:b + 1], in1=gb[:],
                                                   op0=ALU.mult, op1=ALU.mult).then_inc(scaled, 1)


def scratch(nc, D):
    for name, shape, dt in (("h0", (TP, DM), F32), ("h1", (TP, DM), F32), ("h2", (TP, DM), F32), ("h3", (TP, DM), F32),
                            ("h4", (TP, DM), F32), ("hn", (TP, DM), F32), ("ys", (SLOTS, DM), F32), ("table", (SLOTS, 1), I32)):
        if name not in D:
            D[name] = nc.dram_tensor(f"s_{name}", shape, dt, kind="Internal").ap()


def program(nc, D):
    Phase.seen.clear()
    scratch(nc, D)
    first(nc, D)
    conv_mixer(nc, D, D["h0"], D["h1"])
    moe(nc, D, 0, D["h1"], D["h2"])
    mla(nc, D, D["h2"], D["h3"])
    moe(nc, D, 1, D["h3"], D["h4"])
    final_norm(nc, D, D["h4"])


def by_partition(a, *order):
    return np.ascontiguousarray(a.reshape(-1, P, *a.shape[1:]).swapaxes(0, 1))


def lay_out(inputs):
    a = {k: np.ascontiguousarray(np.asarray(v)) for k, v in inputs.items()}
    o = {n: a[n] for n in ("meta_tokens_2", "norm_ffn_g_2", "w_gate_2", "w_up_2", "w_down_2", "final_norm_g_2")}
    for n in ("x", "attn_sinks", "lru_wa", "lru_wx", "rwkv_w2", "rwkv_a2", "w_out", "ln_g", "ln_b", "conv_w_out_2", "w_o_2"):
        o[n] = a[n][0]
    o["xT"] = by_partition(a["x"][0].T)
    w = a["w_in"][0]
    q, k, v, ga, xb, gb, c, gc = np.split(w, np.cumsum([512, 128, 128, 512, 256, 256, 832, 256])[:-1], axis=1)
    swapped = np.concatenate([k[:, HALF:], k[:, :HALF]], 1)
    tiles = np.concatenate([ga, gb, gc, q, k, swapped, xb, c, np.zeros((DM, HALF + P), w.dtype)], 1)
    o["w_in_t"] = np.ascontiguousarray(tiles.reshape(KT, P, PROJ_TILES + 1, P).transpose(2, 1, 0, 3))
    o["w_v_t"] = by_partition(v)

    def vectors(rows):
        return np.ascontiguousarray(np.stack(rows).reshape(-1, 2, P).transpose(2, 1, 0))

    o["lru_vec"] = vectors([*a["conv_w"][0], a["conv_b"][0], a["lru_ba"][0], a["lru_bx"][0], a["lru_lambda"][0]])
    mu = a["rwkv_mu"][0]
    o["rwkv_vec"] = vectors([mu[0:256], mu[256:512], mu[512:768], a["rwkv_w0"][0], a["rwkv_a0"][0], a["rwkv_kk"][0],
                             a["rwkv_ka"][0], a["rwkv_rk"][0].reshape(-1), a["rwkv_gn_w"][0], a["rwkv_gn_b"][0]])
    o["rwkv_mu_lo"] = np.ascontiguousarray(mu[768:].reshape(HALF, 1))
    o["norm_mix_g_t"] = np.stack([by_partition(g) for g in a["norm_mix_g_2"]])
    o["kv_norm_g_t"] = by_partition(a["kv_norm_g_2"])
    o["conv_w_in_t"] = np.ascontiguousarray(a["conv_w_in_2"][0].reshape(KT, P, 3, KT, P).transpose(3, 1, 2, 0, 4))
    o["conv_w_2_t"] = np.ascontiguousarray(a["conv_w_2"][0].reshape(3, KT, P).transpose(2, 1, 0))
    o["w_dq_t"] = by_partition(a["w_dq_2"][0])
    dkv = a["w_dkv_2"]
    o["w_dkv_t"] = by_partition(dkv[:, :KVR])
    rope = dkv[:, KVR:]
    turned = np.concatenate([rope[:, ROPE // 2:], rope[:, :ROPE // 2]], 1)
    o["w_rope_t"] = by_partition(np.stack([np.concatenate([rope, rope], 1), np.concatenate([turned, turned], 1)], 1))
    o["cq_g_t"] = by_partition(a["cq_norm_g_2"][0])
    o["ckv_g_t"] = by_partition(a["ckv_norm_g_2"])
    inv = np.float32(10000.0) ** (-np.arange(0, ROPE, 2, dtype=np.float32) / np.float32(ROPE))
    angle = np.arange(T, dtype=np.float32)[:, None] * inv[None, :]
    cos, sin = np.cos(angle).T, np.sin(angle).T
    o["cos_t"] = np.ascontiguousarray(np.concatenate([cos] * 4, 0))
    o["sin_t"] = np.ascontiguousarray(np.concatenate([-sin, sin] * 2, 0))
    uq = a["w_uq_2"][0].reshape(QR // P, P, HEADS // 2, 2, NOPE + ROPE)
    nope, rq = uq[..., :NOPE], uq[..., NOPE:]
    rs = np.concatenate([rq[..., ROPE // 2:], rq[..., :ROPE // 2]], -1)
    o["w_uq_t"] = np.ascontiguousarray(np.stack(
        [nope[:, :, :, 0], nope[:, :, :, 1], rq.reshape(QR // P, P, HEADS // 2, P), rs.reshape(QR // P, P, HEADS // 2, P)],
        3).transpose(2, 1, 0, 3, 4))
    ukv = a["w_ukv_2"].reshape(KVR // P, P, HEADS // 2, 2, 2, P)
    o["w_ukv_t"] = np.ascontiguousarray(ukv.transpose(2, 1, 0, 4, 3, 5).reshape(HEADS // 2, P, KVR // P, 4, P))
    o["w_route_t"] = np.stack([by_partition(np.concatenate([g, e], 1)) for g, e in zip(a["w_grp_2"], a["w_exp_2"])])
    return o


def kernel(**inputs):
    import concourse.bacc as bacc
    from concourse.bass_utils import run_bass_kernel_spmd

    nc = bacc.Bacc("TRN2", target_bir_lowering=False, num_devices=1)
    arrays = {f"in_{n}": x for n, x in lay_out(inputs).items()}
    D = {n[3:]: nc.dram_tensor(n, x.shape, mybir.dt.from_np(x.dtype), kind="ExternalInput").ap() for n, x in arrays.items()}
    D["out"] = nc.dram_tensor("out_0", (SEQ, DM), F32, kind="ExternalOutput").ap()
    program(nc, D)
    r = run_bass_kernel_spmd(nc, [arrays], core_ids=[0])
    return r.results[0]["out_0"].reshape(1, SEQ, DM)
```

```python
import numpy as np
import concourse.bass as bass
from concourse import mybir
from contextlib import ExitStack

F32 = mybir.dt.float32
I32 = mybir.dt.int32
U32 = mybir.dt.uint32
ALU = mybir.AluOpType
ACT = mybir.ActivationFunctionType
AX = mybir.AxisListType
P = 128
HALF = 64

SEQ = 1024
DM = 1024
KT = DM // P
NB = SEQ // P
PAIRS = 4
KV = 2
G_T, Q_T, K_T, KS_T, XB_T, R_T, CK_T, CV_T, WA_T = 0, 8, 12, 13, 14, 16, 18, 20, 22
PROJ_TILES = 23
GATE_TILES = 8
HEAD_SCALE = 64.0 ** -0.5
MASKED = -1.0e30
CHUNK = 64
NCH = SEQ // CHUNK
LN_EPS = 1e-5
GN_EPS = 64e-5
ALPHA = 2.0 ** 0.25
DECAY_HALF = float(np.exp(-0.5))
RANK = 32


class Chain:

    def __init__(self, eng, sem):
        self.eng, self.sem, self.n = eng, sem, 0

    def __call__(self, ins):
        self.n += 1
        ins.then_inc(self.sem, 1)
        self.eng.wait_ge(self.sem, self.n)

    def hold(self, ins):
        self.n += 1
        ins.then_inc(self.sem, 1)

    def wait(self):
        self.eng.wait_ge(self.sem, self.n)

    def restart(self):
        if self.n:
            self.eng.sem_clear(self.sem)
        self.n = 0


class Phase:

    seen = {}

    def __init__(self, nc, name):
        again = Phase.seen[name] = Phase.seen.get(name, -1) + 1
        self.nc, self.name, self.ctx, self.sems = nc, f"{name}{again}", ExitStack(), []

    def __enter__(self):
        return self

    def __exit__(self, kind, *rest):
        self.ctx.close()
        if kind is None and self.sems:
            self.nc.clear_and_free_semaphores(self.sems)
            self.nc.all_engine_barrier()

    def sb(self, name, shape, dt=F32):
        return self.ctx.enter_context(self.nc.sbuf_tensor(f"{self.name}__{name}", shape, dt))

    def ps(self, name, shape, dt=F32):
        return self.ctx.enter_context(self.nc.psum_tensor(f"{self.name}__{name}", shape, dt))

    def sem(self, name):
        self.sems.append(self.nc.alloc_semaphore(f"{self.name}__{name}"))
        return self.sems[-1]


def col(v):
    return v.rearrange("(p a) -> p a", a=1)


TL = 2
ORDER = [XB_T, XB_T + 1, WA_T, R_T, R_T + 1, CK_T, CK_T + 1, CV_T, CV_T + 1, G_T + 4, G_T + 5,
         Q_T, Q_T + 1, Q_T + 2, Q_T + 3, K_T, KS_T, G_T, G_T + 1, G_T + 2, G_T + 3, G_T + 6, G_T + 7]
GATE_AT = ORDER.index(G_T + 5) + 1


def front(nc, D, proj, vpad, kkb, bb, dlt, wc, vec):
    with Phase(nc, "fr") as ph:
        xT = ph.sb("xT", [P, KT, SEQ])
        wbuf = ph.sb("w", [P, 2, KT, P])
        wv = ph.sb("wv", [P, KT, P])
        cum = ph.sb("cum", [P, TL, SEQ])
        aa = ph.sb("aa", [P, TL, SEQ])
        lw = ph.sb("lw", [P, TL, SEQ])
        keep = ph.sb("keep", [P, SEQ], mybir.dt.bfloat16)
        ones2 = ph.sb("ones2", [P, P])
        w2a2 = ph.sb("w2a2", [HALF, TL * P])
        muwa = ph.sb("muwa", [HALF, 1])
        eps = ph.sb("eps", [P, 1])
        lvec = ph.sb("lvec", [P, TL, 8])
        sp8 = ph.sb("sp8", [P, TL, 2])
        wa = ph.sb("wa", [P, TL, P])
        wx = ph.sb("wx", [P, TL, P])
        acc = ph.ps("acc", [P, 2, 2, 512])
        aux = ph.ps("aux", [P, TL, 2, 512])
        xc, rg, ig, uv, av = cum, aa, lw, dlt, proj[:, XB_T:XB_T + TL]
        lo = proj[0:HALF, WA_T]
        rr, kx, vv = (proj[:, m:m + TL] for m in (R_T, CK_T, CV_T))
        wv_loaded, loaded, vec_loaded = ph.sem("wv_loaded"), ph.sem("loaded"), ph.sem("vec_loaded")
        x_loaded = ph.sem("x_loaded")
        w_loaded = [ph.sem("w0_loaded"), ph.sem("w1_loaded")]
        (done, evac, aux_done, aux_free, v_own, a_own, zeroed, conv_done, low_ready, tanh_low, sig_done, decay_done,
         tanh_done, root_in, root_done, logs_done, sq_ready, norm_done, cum_done, bonus_in, exp_done) = (ph.sem(n) for n in (
             "done", "evac", "aux_done", "aux_free", "v_own", "a_own", "zeroed", "conv_done", "low_ready", "tanh_low",
             "sig_done", "decay_done", "tanh_done", "root_in", "root_done", "logs_done", "sq_ready", "norm_done",
             "cum_done", "bonus_in", "exp_done"))
        w_dram = D["w_in_t"]

        def flat(x):
            return x.rearrange("p a b -> p (a b)")

        with nc.Block() as block:

            @block.sync
            def _(sp):
                for b in range(2):
                    sp.dma_start(wbuf[:, b], w_dram[ORDER[b]]).then_inc(w_loaded[b], 16)
                    for k in range(b, KT, 2):
                        sp.dma_start(xT[:, k], D["xT"][:, k]).then_inc(x_loaded, 16)
                for m in range(2, PROJ_TILES):
                    sp.wait_ge(done, m - 1)
                    sp.dma_start(wbuf[:, m % 2], w_dram[ORDER[m]]).then_inc(w_loaded[m % 2], 16)

            @block.gpsimd
            def _(pool):
                pool.dma_start(lvec[:], D["lru_vec"]).then_inc(vec_loaded, 16)
                pool.dma_start(vec[:], D["rwkv_vec"]).then_inc(loaded, 16)
                pool.dma_start(muwa[:], D["rwkv_mu_lo"]).then_inc(loaded, 16)
                pool.dma_start(w2a2[0:RANK], D["rwkv_w2"]).then_inc(loaded, 16)
                pool.dma_start(w2a2[RANK:2 * RANK], D["rwkv_a2"]).then_inc(loaded, 16)
                pool.wait_ge(zeroed, 1)
                for w, name in ((wa, "lru_wa"), (wx, "lru_wx")):
                    for n in range(4):
                        h = n % 2
                        pool.dma_start(w[HALF * h:HALF * h + HALF, n // 2, HALF * h:HALF * h + HALF],
                                       D[name][n]).then_inc(loaded, 16)
                pool.dma_start(wv[:], D["w_v_t"]).then_inc(wv_loaded, 16)

            @block.tensor
            def _(pe):
                mm = nc.tensor.matmul
                pe.wait_ge(x_loaded, 16 * KT)

                def small(n, weights, moving, *waits):
                    if n:
                        pe.wait_ge(aux_free, n)
                    for s, value in waits:
                        pe.wait_ge(s, value)
                    for t in range(TL):
                        for c in range(2):
                            last = mm(aux[:, t, c], weights(t), moving(t)[:, 512 * c:512 * c + 512], start=True, stop=True)
                    last.then_inc(aux_done, 1)

                def smalls(m):
                    if m == 4:
                        small(0, lambda t: wa[:, t], lambda t: xc[:, t], (conv_done, 1), (loaded, 16 * 12))
                    if m == 5:
                        small(1, lambda t: wx[:, t], lambda t: xc[:, t])
                    if m == 10:
                        small(2, lambda t: w2a2[0:RANK, P * t:P * t + P], lambda t: lo[0:RANK], (tanh_low, 1))
                    if m == 11:
                        small(3, lambda t: w2a2[RANK:2 * RANK, P * t:P * t + P], lambda t: lo[RANK:2 * RANK])
                    if m == 14:
                        small(4, lambda t: ones2[:], lambda t: dlt[:, t], (sq_ready, 1))
                    if m == 18:
                        small(5, lambda t: ones2[:], lambda t: dlt[:, t], (bonus_in, 1))

                for m in range(PROJ_TILES):
                    b = m % 2
                    pe.wait_ge(w_loaded[b], 16 * (m // 2 + 1))
                    if m >= 2:
                        pe.wait_ge(evac, m - 1)
                    for c in range(2):
                        for k in range(KT):
                            last = mm(acc[:, b, c], wbuf[:, b, k], xT[:, k, 512 * c:512 * c + 512],
                                      start=(k == 0), stop=(k == KT - 1))
                    last.then_inc(done, 1)
                    smalls(m)
                pe.wait_ge(wv_loaded, 16)
                pe.wait_ge(aux_free, 6)
                for t in range(NB):
                    for k in range(KT):
                        last = mm(aux[:, 0, t // 4, P * (t % 4):P * (t % 4) + P], xT[:, k, P * t:P * t + P], wv[:, k],
                                  start=(k == 0), stop=(k == KT - 1))
                last.then_inc(aux_done, 1)

            @block.scalar
            def _(act):
                a = Chain(act, a_own)

                def evacuate(m):
                    act.wait_ge(done, m + 1)
                    gate = ORDER[m] < GATE_TILES
                    nc.scalar.activation(proj[:, ORDER[m]], flat(acc[:, m % 2]),
                                         ACT.Silu if gate else ACT.Copy).then_inc(evac, 1)

                act.wait_ge(vec_loaded, 16)
                a(nc.scalar.activation(sp8[:, :, 0:1], lvec[:, :, 7:8], ACT.Exp, scale=-1.0))
                a(nc.scalar.activation(sp8[:, :, 1:2], sp8[:, :, 0:1], ACT.Ln, bias=1.0))
                for m in range(5):
                    evacuate(m)
                for n, (out, bias) in enumerate(((rg, 5), (ig, 6))):
                    act.wait_ge(aux_done, n + 1)
                    for t in range(TL):
                        a.hold(nc.scalar.activation(out[:, t], flat(aux[:, t]), ACT.Sigmoid, bias=lvec[:, t, bias:bias + 1]))
                    a.wait()
                    act.sem_inc(aux_free, 1)
                    evacuate(5 + n)
                act.sem_inc(sig_done, 1)
                act.wait_ge(low_ready, 1)
                a(nc.scalar.activation(lo[0:RANK], lo[0:RANK], ACT.Tanh))
                act.sem_inc(tanh_low, 1)
                act.wait_ge(decay_done, 1)
                a.hold(nc.scalar.activation(av, rg[:], ACT.Exp))
                a.hold(nc.scalar.activation(uv[:], rg[:], ACT.Tanh))
                a.wait()
                act.sem_inc(tanh_done, 1)
                evacuate(7)
                act.wait_ge(root_in, 1)
                a(nc.scalar.activation(uv[:], uv[:], ACT.Sqrt))
                act.sem_inc(root_done, 1)
                for m in range(8, 11):
                    evacuate(m)
                for n, (out, bias) in enumerate(((lw, 3), (aa, 4))):
                    act.wait_ge(logs_done, 1)
                    act.wait_ge(aux_done, n + 3)
                    for t in range(TL):
                        a.hold(nc.scalar.activation(out[:, t], flat(aux[:, t]), ACT.Sigmoid, bias=vec[:, t, bias:bias + 1]))
                    a.wait()
                    act.sem_inc(aux_free, 1)
                    evacuate(11 + n)
                act.sem_inc(sig_done, 1)
                for m in range(13, 15):
                    evacuate(m)
                act.wait_ge(aux_done, 5)
                a(nc.scalar.activation(dlt[:], aux[:].rearrange("p t a b -> p t (a b)"), ACT.Sqrt, bias=eps[:]))
                act.sem_inc(aux_free, 1)
                act.sem_inc(norm_done, 1)
                for m in range(15, 19):
                    evacuate(m)
                act.wait_ge(cum_done, 1)
                act.wait_ge(bonus_in, 1)
                a.hold(nc.scalar.activation(aa[:], cum[:], ACT.Exp))
                a.hold(nc.scalar.activation(lw[:], lw[:], ACT.Exp))
                a.wait()
                a(nc.scalar.activation(cum[:], cum[:], ACT.Exp, scale=-1.0))
                act.sem_inc(exp_done, 1)
                for m in range(19, PROJ_TILES):
                    evacuate(m)

            @block.vector
            def _(dve):
                v = Chain(dve, v_own)
                V = nc.vector
                v.hold(V.memset(wa[:], 0.0))
                v(V.memset(wx[:], 0.0))
                dve.sem_inc(zeroed, 1)
                v.hold(V.memset(eps[:], 1e-12))
                v.hold(V.memset(vpad[:], 0.0))
                v.hold(V.memset(ones2[:], 0.0))
                v(V.memset(keep[:], 1.0))
                v.hold(V.memset(keep[:].rearrange("p (n c) -> p n c", c=CHUNK)[:, :, 0:1], 0.0))
                for h in range(2):
                    v.hold(V.memset(ones2[HALF * h:HALF * h + HALF, HALF * h:HALF * h + HALF], 1.0))
                v.wait()
                dve.wait_ge(vec_loaded, 16)
                for t in range(TL):
                    dve.wait_ge(evac, t + 1)
                    v.hold(V.tensor_scalar(xc[:, t], proj[:, XB_T + t], lvec[:, t, 3:4], lvec[:, t, 4:5], ALU.mult, ALU.add))
                v.wait()
                for back in range(1, 4):
                    for t in range(TL):
                        v.hold(V.scalar_tensor_tensor(out=xc[:, t, back:], in0=proj[:, XB_T + t, 0:SEQ - back],
                                                      scalar=lvec[:, t, 3 - back:4 - back], in1=xc[:, t, back:],
                                                      op0=ALU.mult, op1=ALU.add))
                    v.wait()
                dve.sem_inc(conv_done, 1)

                def shift(x, delta, mu):
                    v.hold(V.tensor_scalar(delta[:, 0:1], x[:, 0:1], -1.0, None, ALU.mult))
                    v(V.tensor_tensor(delta[:, 1:SEQ], x[:, 0:SEQ - 1], x[:, 1:SEQ], ALU.subtract))
                    v(V.scalar_tensor_tensor(out=x, in0=delta, scalar=mu, in1=x, op0=ALU.mult, op1=ALU.add))

                dve.wait_ge(loaded, 16 * 12)
                dve.wait_ge(evac, 3)
                shift(lo, bb[0:HALF, 0], muwa[:, 0:1])
                dve.sem_inc(low_ready, 1)
                for t in range(TL):
                    dve.wait_ge(evac, 4 + t)
                    shift(rr[:, t], bb[:, t], vec[:, t, 0:1])
                dve.wait_ge(sig_done, 1)
                for t in range(TL):
                    v.hold(V.tensor_scalar(rg[:, t], rg[:, t], sp8[:, t, 1:2], -8.0, ALU.mult, ALU.mult))
                v.wait()
                dve.sem_inc(decay_done, 1)
                v(V.tensor_tensor(ig[:], ig[:], xc[:], ALU.mult))
                dve.wait_ge(tanh_done, 1)
                v(V.tensor_tensor(xc[:], av, av, ALU.mult))
                v(V.tensor_scalar(xc[:], xc[:], 1.0, -1.0, ALU.add, ALU.mult))
                v(V.tensor_tensor(uv[:], uv[:], xc[:], ALU.mult))
                dve.sem_inc(root_in, 1)
                for t in range(TL):
                    dve.wait_ge(evac, 6 + t)
                    shift(kx[:, t], bb[:, t], vec[:, t, 1:2])
                dve.wait_ge(root_done, 1)
                v(V.tensor_tensor(uv[:], uv[:], ig[:], ALU.mult))
                dve.sem_inc(logs_done, 1)
                for t in range(TL):
                    v.hold(V.tensor_tensor_scan(xc[:, t], av[:, t], uv[:, t], 0.0, ALU.mult, ALU.add))
                v.wait()
                for t in range(TL):
                    dve.wait_ge(evac, 8 + t)
                    shift(vv[:, t], bb[:, t], vec[:, t, 2:3])
                for t in range(TL):
                    v.hold(V.tensor_scalar(kkb[:, t], kx[:, t], vec[:, t, 5:6], None, ALU.mult))
                v.wait()
                v(V.tensor_tensor(dlt[:], kkb[:], kkb[:], ALU.mult))
                dve.sem_inc(sq_ready, 1)
                dve.wait_ge(evac, GATE_AT)
                v(V.tensor_tensor(proj[:, G_T + 4:G_T + 6], proj[:, G_T + 4:G_T + 6], xc[:], ALU.mult))
                dve.wait_ge(sig_done, 2)
                for t in range(TL):
                    v(V.tensor_scalar(bb[:, t], aa[:, t], -1.0, vec[:, t, 6:7], ALU.add, ALU.mult))
                    v(V.scalar_tensor_tensor(out=kx[:, t], in0=bb[:, t], scalar=1.0, in1=kx[:, t],
                                             op0=ALU.add, op1=ALU.mult))
                v(V.tensor_scalar(lw[:], lw[:], -DECAY_HALF, None, ALU.mult))
                for t in range(TL):
                    v.hold(V.tensor_tensor_scan(cum[:, t], keep[:], lw[:, t], 0.0, ALU.mult, ALU.add))
                v.wait()
                v(V.tensor_tensor(lw[:], cum[:], lw[:], ALU.subtract))
                dve.sem_inc(cum_done, 1)
                dve.wait_ge(norm_done, 1)
                v(V.reciprocal(dlt[:], dlt[:]))
                v(V.tensor_tensor(kkb[:], kkb[:], dlt[:], ALU.mult))
                v(V.tensor_tensor(bb[:], kkb[:], aa[:], ALU.mult))
                for t in range(TL):
                    v.hold(V.scalar_tensor_tensor(out=dlt[:, t], in0=rr[:, t], scalar=vec[:, t, 7:8],
                                                  in1=kx[:, t], op0=ALU.mult, op1=ALU.mult))
                v.wait()
                dve.sem_inc(bonus_in, 1)
                dve.wait_ge(aux_done, 6)
                v(V.tensor_tensor(dlt[:], aux[:].rearrange("p t a b -> p t (a b)"), vv, ALU.mult))
                dve.sem_inc(aux_free, 1)
                dve.wait_ge(exp_done, 1)
                V.tensor_copy(wc[:], aa[:].rearrange("p t (n c) -> p t n c", c=CHUNK)[:, :, :, CHUNK - 1])
                V.tensor_tensor(rr, rr, aa[:], ALU.mult)
                V.scalar_tensor_tensor(out=kkb[:], in0=kkb[:], scalar=-1.0, in1=lw[:], op0=ALU.mult, op1=ALU.mult)
                V.tensor_tensor(bb[:], bb[:], cum[:], ALU.mult)
                v(V.tensor_tensor(kx, kx, cum[:], ALU.mult))
                dve.wait_ge(aux_done, 7)
                for g in range(KV):
                    V.tensor_copy(vpad[:, 1:NB + 1, g, HALF:2 * HALF],
                                  aux[:, 0].rearrange("p a (b c) -> p (a b) c", c=P)[:, :, HALF * g:HALF * g + HALF])


def window_attention(nc, D, proj, vpad):
    with Phase(nc, "swa") as ph:
        kd = ph.sb("kd", [P, KV, 2, SEQ + P])
        mask = ph.sb("mask", [P, NB, 2 * P])
        ident = ph.sb("ident", [P, P])
        qs = ph.sb("qs", [P, PAIRS, P])
        vs = ph.sb("vs", [P, 2, KV, 3 * HALF])
        sinks = ph.sb("sinks", [P, 2 * PAIRS])
        nsinks = ph.sb("nsinks", [P, 2 * PAIRS])
        sc = ph.sb("sc", [P, PAIRS, 2, 2 * P])
        mx = ph.sb("mx", [P, PAIRS, 2])
        nm = ph.sb("nm", [P, PAIRS, 2])
        ls = ph.sb("ls", [P, PAIRS, 2])
        es = ph.sb("es", [P, PAIRS, 2])
        den = ph.sb("den", [P, PAIRS, 2])
        rd = ph.sb("rd", [P, PAIRS, 2])
        pT = ph.sb("pT", [P, 2, 4, P])
        s_ps = ph.ps("s", [P, PAIRS, 512])
        t_ps = ph.ps("t", [P, 2, 512])
        o_ps = ph.ps("o", [P, 2, 512])
        const_done, sinks_loaded = ph.sem("const_done"), ph.sem("sinks_loaded")
        mask_done, v_own, a_own = ph.sem("mask_done"), ph.sem("v_own"), ph.sem("a_own")
        staged = ph.sem("staged")
        scored = ph.sem("scored")
        maxed = ph.sem("maxed")
        exped = ph.sem("exped")
        normed = ph.sem("normed")
        turned = ph.sem("turned")
        turned_out = ph.sem("turned_out")
        mixed = ph.sem("mixed")
        gated = ph.sem("gated")
        with nc.Block() as block:

            @block.sync
            def _(sp):
                sp.dma_start(sinks[:], D["attn_sinks"].partition_broadcast(P)).then_inc(sinks_loaded, 16)

            @block.gpsimd
            def _(pool):
                nc.gpsimd.memset(mask[:], 0.0).then_inc(mask_done, 1)
                nc.gpsimd.memset(ident[:], 0.0).then_inc(mask_done, 1)
                pool.wait_ge(mask_done, 2)
                nc.gpsimd.affine_select(out=mask[:, :, 0:P], in_=mask[:, :, 0:P], compare_op=ALU.is_gt,
                                        fill=MASKED, base=0, pattern=[[0, NB], [1, P]],
                                        channel_multiplier=-1).then_inc(mask_done, 1)
                nc.gpsimd.affine_select(out=mask[:, :, P:2 * P], in_=mask[:, :, P:2 * P], compare_op=ALU.is_ge,
                                        fill=MASKED, base=0, pattern=[[0, NB], [-1, P]],
                                        channel_multiplier=1).then_inc(mask_done, 1)
                nc.gpsimd.affine_select(out=ident[:], in_=ident[:], compare_op=ALU.not_equal, fill=1.0,
                                        base=0, pattern=[[-1, P]], channel_multiplier=1).then_inc(mask_done, 1)
                pool.wait_ge(mask_done, 5)
                nc.gpsimd.memset(mask[:, 0, 0:P], MASKED).then_inc(mask_done, 1)

            @block.tensor
            def _(pe):
                pe.wait_ge(mask_done, 6)
                with pe.Fori(0, NB) as i:
                    pe.wait_ge(staged, i + 1)
                    for j in range(PAIRS):
                        g = j // 2
                        nc.tensor.matmul(s_ps[:, j].rearrange("p (a b) -> p a b", a=2), qs[:, j],
                                         kd[:, g, :, bass.ds(i * P, 2 * P)],
                                         start=True, stop=True).then_inc(scored, 1)
                    for j in range(PAIRS):
                        g = j // 2
                        pe.wait_ge(normed, i * PAIRS + j + 1)
                        pe.wait_ge(turned_out, i * PAIRS + j + 1)
                        for c in range(4):
                            last = nc.tensor.transpose(t_ps[:, j % 2, P * c:P * c + P],
                                                       sc[:, j, c // 2, P * (c % 2):P * (c % 2) + P], ident[:])
                        last.then_inc(turned, 1)
                        pe.wait_ge(turned_out, i * PAIRS + j + 3)
                        pe.wait_ge(gated, i * PAIRS + j + 1)
                        for c in range(4):
                            h, b = c // 2, c % 2
                            last = nc.tensor.matmul(o_ps[:, j % 2, 0:P],
                                                    vs[:, b, g, HALF - HALF * h:3 * HALF - HALF * h],
                                                    pT[:, j % 2, c], start=(c == 0), stop=(c == 3))
                        last.then_inc(mixed, 1)

            @block.scalar
            def _(act):
                act.sem_inc(turned_out, 2)
                act.wait_ge(sinks_loaded, 16)
                with act.Fori(0, NB) as i:
                    for j in range(PAIRS):
                        act.wait_ge(maxed, i * PAIRS + j + 1)
                        for h in range(2):
                            nc.scalar.activation(sc[:, j, h], sc[:, j, h], ACT.Exp, bias=nm[:, j, h:h + 1],
                                                 accum_out=ls[:, j, h:h + 1])
                        for h in range(2):
                            last = nc.scalar.activation(es[:, j, h:h + 1], sinks[:, 2 * j + h:2 * j + h + 1], ACT.Exp,
                                                        bias=nm[:, j, h:h + 1])
                        last.then_inc(exped, 1)
                    for j in range(PAIRS):
                        act.wait_ge(turned, i * PAIRS + j + 1)
                        if j >= 2:
                            act.wait_ge(mixed, i * PAIRS + j - 1)
                        nc.scalar.copy(pT[:, j % 2], t_ps[:, j % 2].rearrange("p (c q) -> p c q", c=4)).then_inc(turned_out, 1)

            @block.vector
            def _(dve):
                v = Chain(dve, v_own)
                dve.sem_inc(gated, 2)
                v.hold(nc.vector.memset(kd[:], 0.0))
                dve.wait_ge(sinks_loaded, 16)
                v(nc.vector.tensor_scalar(nsinks[:], sinks[:], -1.0, None, ALU.mult))
                for src in range(2):
                    for h in range(2):
                        g = h if src == 0 else 1 - h
                        v.hold(nc.vector.tensor_copy(kd[HALF * h:HALF * h + HALF, g, h, P:],
                                                     proj[HALF * h:HALF * h + HALF, K_T + src]))
                v.wait()
                dve.wait_ge(mask_done, 6)
                with dve.Fori(0, NB) as i:
                    v.restart()
                    v.hold(nc.vector.tensor_copy(qs[:], proj[:, Q_T:Q_T + PAIRS, bass.ds(i * P, P)]))
                    v(nc.vector.tensor_copy(vs[:], vpad[:, bass.ds(i, 2)]))
                    dve.sem_inc(staged, 1)
                    for j in range(PAIRS):
                        dve.wait_ge(scored, i * PAIRS + j + 1)
                        v(nc.vector.scalar_tensor_tensor(
                            out=sc[:, j], in0=s_ps[:, j].rearrange("p (a b) -> p a b", a=2), scalar=HEAD_SCALE,
                            in1=mask[:, bass.ds(i, 1)].to_broadcast([P, 2, 2 * P]), op0=ALU.mult, op1=ALU.add))
                        v(nc.vector.tensor_reduce(mx[:, j], sc[:, j], AX.X, ALU.max))
                        nc.vector.scalar_tensor_tensor(out=nm[:, j], in0=mx[:, j], scalar=-1.0,
                                                       in1=nsinks[:, 2 * j:2 * j + 2], op0=ALU.mult,
                                                       op1=ALU.min).then_inc(maxed, 1)
                    for j in range(PAIRS):
                        dve.wait_ge(exped, i * PAIRS + j + 1)
                        v(nc.vector.tensor_tensor(den[:, j], ls[:, j], es[:, j], ALU.add))
                        v(nc.vector.reciprocal(rd[:, j], den[:, j]))
                        nc.vector.tensor_tensor(sc[:, j], sc[:, j],
                                                rd[:, j].unsqueeze(2).to_broadcast([P, 2, 2 * P]),
                                                ALU.mult).then_inc(normed, 1)
                    for j in range(PAIRS):
                        dve.wait_ge(mixed, i * PAIRS + j + 1)
                        out = proj[:, G_T + j, bass.ds(i * P, P)]
                        nc.vector.tensor_tensor(out, o_ps[:, j % 2, 0:P], out, ALU.mult).then_inc(gated, 1)
                dve.wait_ge(gated, NB * PAIRS + 2)


def chunks(nc, D, proj, kkb, bb, bonus, wc, vec):
    U = 4
    rr, k2, vv = (proj[:, m:m + TL] for m in (R_T, CK_T, CV_T))
    N1, LT, N2, MT = 3, 4, 5, 6
    V_, K_, B_ = 0, 1, 2
    SQ = 5
    with Phase(nc, "rwc") as ph:
        dg = ph.sb("dg", [P, TL, 2, 6, P])
        big = ph.sb("big", [P, U, 7, P])
        pw = ph.sb("pw", [P, U, 2, P])
        inv = ph.sb("inv", [P, U, P])
        vt = ph.sb("vt", [P, U, HALF])
        am = ph.sb("am", [P, U, P + HALF])
        tav = ph.sb("tav", [P, U, P + HALF])
        gr = ph.sb("gr", [P, U, 2, P])
        hz = ph.sb("hz", [P, U, HALF])
        z = ph.sb("z", [P, TL, 2, HALF])
        wcs = ph.sb("wcs", [P, TL, 2])
        masks = ph.sb("masks", [P, 4, P])
        lowm = ph.sb("lowm", [P, P])
        ident = ph.sb("ident", [P, P])
        idh = ph.sb("idh", [P, HALF])
        st = ph.sb("st", [P, U, 6])
        mv = ph.sb("mv", [P, U, 2])
        rs = ph.sb("rs", [P, U])
        eps = ph.sb("eps", [P, 1])
        ydg = ph.sb("ydg", [P, U, P])
        yo = ph.sb("yo", [P, TL, 2, CHUNK])
        X = [ph.ps(f"x{u}", [P, 512]) for u in range(U)]
        Y = [ph.ps(f"y{u}", [P, 512]) for u in range(U)]
        (const_done, v_own, staged, crossed, masked, tok_out, inv_init, sq_done, pw_out, am_done, am_out, inv_done, inv_out,
         tav_done, tav_out, gr_done, gr_out, z_done, z_out, var_ready, rooted, y_in, y_turned) = (ph.sem(n) for n in (
             "const_done", "v_own", "staged", "crossed", "masked", "tok_out", "inv_init", "sq_done", "pw_out", "am_done",
             "am_out", "inv_done", "inv_out", "tav_done", "tav_out", "gr_done", "gr_out", "z_done", "z_out", "var_ready",
             "rooted", "y_in", "y_turned"))

        def feature(u, n):
            return dg[:, u // 2, u % 2, n]

        with nc.Block() as block:

            @block.gpsimd
            def _(pool):
                g = nc.gpsimd

                def select(m, op, mult, step, fill=0.0, base=0):
                    g.affine_select(out=m, in_=m, compare_op=op, fill=fill, base=base,
                                    pattern=[[step, m.shape[1]]], channel_multiplier=mult).then_inc(const_done, 1)

                g.memset(masks[:], 1.0).then_inc(const_done, 1)
                g.memset(lowm[:], 1.0).then_inc(const_done, 1)
                g.memset(ident[:], 0.0).then_inc(const_done, 1)
                g.memset(idh[:], 0.0).then_inc(const_done, 1)
                pool.wait_ge(const_done, 4)
                for n in range(4):
                    select(masks[:, n], ALU.is_ge if n % 2 == 0 else ALU.is_gt, -1, 1)
                select(lowm[:], ALU.is_gt, 1, -1)
                select(ident[:], ALU.not_equal, 1, -1, 1.0)
                select(idh[:], ALU.not_equal, 1, -1, 1.0)
                pool.wait_ge(const_done, 11)
                select(idh[:], ALU.not_equal, 1, -1, 1.0, -HALF)
                with pool.Fori(0, NCH // 2) as i:
                    for u in range(U):
                        pool.wait_ge(masked, i * U + u + 1)
                        g.tensor_tensor(inv[:, u], big[:, u, LT], ident[:], ALU.add)
                        pool.wait_ge(tok_out, i * U + u + 1)
                        g.tensor_tensor(vt[:, u], big[:, u, V_, 0:HALF], big[:, u, V_, HALF:P],
                                        ALU.add).then_inc(inv_init, 1)

            @block.vector
            def _(dve):
                v = Chain(dve, v_own)
                V = nc.vector
                for b in (dg, z, ydg):
                    v.hold(V.memset(b[:], 0.0))
                v(V.memset(eps[:], GN_EPS))
                dve.wait_ge(const_done, 12)
                for u in range(U):
                    v.hold(V.tensor_copy(feature(u, 0), ident[:]))
                v.wait()
                with dve.Fori(0, NCH // 2) as i:
                    v.restart()
                    now = bass.ds(i * 2 * CHUNK, 2 * CHUNK)
                    V.tensor_copy(wcs[:], wc[:, :, bass.ds(2 * i, 2)])
                    for h in range(2):
                        hp = slice(HALF * h, HALF * h + HALF)
                        for n, src in ((1, rr), (2, kkb), (3, bb), (4, k2), (5, vv)):
                            last = V.tensor_copy(dg[hp, :, :, n, hp],
                                                 src[hp, :, now].rearrange("p t (c k) -> p t c k", c=2))
                    last.then_inc(staged, 1)
                    for u in range(U):
                        dve.wait_ge(crossed, i * U + u + 1)
                        V.tensor_tensor(big[:, u, N1:], X[u][:].rearrange("p (a b) -> p a b", a=4), masks[:], ALU.mult)
                        V.tensor_tensor(pw[:, u, 0], Y[u][:, 0:P], lowm[:], ALU.mult).then_inc(masked, 1)
                    for n in range(SQ):
                        for u in range(U):
                            dve.wait_ge(inv_done, i * U * SQ + U * n + u + 1)
                            if n == 0:
                                dve.wait_ge(inv_init, i * U + u + 1)
                            V.tensor_tensor(inv[:, u], inv[:, u], Y[u][:, 2 * P:3 * P], ALU.add).then_inc(inv_out, 1)
                    for u in range(U):
                        dve.wait_ge(gr_done, i * U + u + 1)
                        V.tensor_tensor(gr[:, u], Y[u][:, 0:2 * P].rearrange("p (a b) -> p a b", a=2),
                                        dg[:, u // 2, u % 2, 0:2], ALU.add)
                        V.tensor_scalar(hz[:, u], Y[u][:, 2 * P:2 * P + HALF], wcs[:, u // 2, u % 2:u % 2 + 1], None,
                                        ALU.mult).then_inc(gr_out, 1)
                    dve.wait_ge(gr_out, i * U + U)
                    for c in range(2):
                        for t in range(TL):
                            u = 2 * t + c
                            dve.wait_ge(z_done, i * U + 2 * c + t + 1)
                            V.scalar_tensor_tensor(out=z[:, t, 1 - c], in0=X[u][:, 3 * P:3 * P + HALF],
                                                   scalar=wcs[:, t, c:c + 1], in1=hz[:, u], op0=ALU.mult,
                                                   op1=ALU.add).then_inc(z_out, 1)
                    for u in range(U):
                        v.hold(V.bn_stats(st[:, u], Y[u][:, 2 * P + HALF:3 * P]))
                    v.wait()
                    for u in range(U):
                        last = V.bn_aggr(mv[:, u], st[:, u])
                    last.then_inc(var_ready, 1)
                    dve.wait_ge(rooted, i + 1)
                    v(V.reciprocal(rs[:], rs[:]))
                    for u in range(U):
                        for h in range(2):
                            hp = slice(HALF * h, HALF * h + HALF)
                            last = V.tensor_scalar(ydg[hp, u, hp], Y[u][hp, 2 * P + HALF:3 * P], mv[hp, u, 0:1],
                                                   rs[hp, u:u + 1], ALU.subtract, ALU.mult)
                        last.then_inc(y_in, 1)
                    for u in range(U):
                        t = u // 2
                        dve.wait_ge(y_turned, i * U + u + 1)
                        v.hold(V.tensor_scalar(yo[:, t, u % 2], X[u][:, 3 * P + HALF:4 * P], vec[:, t, 8:9],
                                               vec[:, t, 9:10], ALU.mult, ALU.add))
                    v.wait()
                    yf = yo[:].rearrange("p t c k -> p t (c k)")
                    v(V.tensor_tensor(yf, yf, bonus[:, :, now], ALU.add))
                    out = proj[:, G_T + 6:G_T + 8, now]
                    v(V.tensor_tensor(out, out, yf, ALU.mult))

            @block.scalar
            def _(act):
                with act.Fori(0, NCH // 2) as i:
                    for u in range(U):
                        act.wait_ge(masked, i * U + u + 1)
                        nc.scalar.copy(big[:, u, 0:3].rearrange("p a b -> p (a b)"), Y[u][:, P:4 * P]).then_inc(tok_out, 1)
                    for n in range(SQ):
                        for u in range(U):
                            act.wait_ge(sq_done, i * U * SQ + U * n + u + 1)
                            nc.scalar.copy(pw[:, u].rearrange("p a b -> p (a b)"), X[u][:, 0:2 * P]).then_inc(pw_out, 1)
                        if n == 0:
                            for u in range(U):
                                act.wait_ge(am_done, i * U + u + 1)
                                nc.scalar.copy(am[:, u], Y[u][:, 0:P + HALF]).then_inc(am_out, 1)
                    for u in range(U):
                        act.wait_ge(tav_done, i * U + u + 1)
                        nc.scalar.copy(tav[:, u], X[u][:, 0:P + HALF]).then_inc(tav_out, 1)
                    act.wait_ge(var_ready, i + 1)
                    nc.scalar.activation(rs[:], mv[:, :, 1], ACT.Sqrt, bias=eps[:]).then_inc(rooted, 1)

            @block.tensor
            def _(pe):
                mm = nc.tensor.matmul
                with pe.Fori(0, NCH // 2) as i:
                    pe.wait_ge(staged, i + 1)
                    for u in range(U):
                        ra = dg[:, u // 2, u % 2, 1:3].rearrange("p a b -> p (a b)")
                        mm(X[u][:, 0:2 * P], feature(u, 3), ra, start=True, stop=True)
                        mm(X[u][:, 2 * P:4 * P], feature(u, 4), ra, start=True, stop=True)
                        mm(Y[u][:, 0:P], feature(u, 2), feature(u, 3), start=True, stop=True)
                        for n, src in enumerate((5, 4, 3)):
                            last = nc.tensor.transpose(Y[u][:, P + P * n:2 * P + P * n], feature(u, src), ident[:])
                        last.then_inc(crossed, 1)
                    for u in range(U):
                        pe.wait_ge(masked, i * U + u + 1)
                        mm(X[u][:, 0:P], big[:, u, LT], pw[:, u, 0], start=True, stop=True)
                        mm(X[u][:, P:2 * P], pw[:, u, 0], big[:, u, LT], start=True, stop=True).then_inc(sq_done, 1)
                    for u in range(U):
                        pe.wait_ge(tok_out, i * U + u + 1)
                        nc.tensor.transpose(Y[u][:, 0:P], feature(u, 2), ident[:])
                        pe.wait_ge(inv_init, i * U + u + 1)
                        mm(Y[u][:, P:P + HALF], big[:, u, MT], vt[:, u], start=True, stop=True).then_inc(am_done, 1)
                    for n in range(SQ):
                        for u in range(U):
                            pe.wait_ge(pw_out, i * U * SQ + U * n + u + 1)
                            if n:
                                pe.wait_ge(inv_out, i * U * SQ + U * (n - 1) + u + 1)
                            else:
                                pe.wait_ge(am_out, i * U + u + 1)
                            mm(Y[u][:, 2 * P:3 * P], pw[:, u, 0], inv[:, u], start=True, stop=True).then_inc(inv_done, 1)
                            if n < SQ - 1:
                                mm(X[u][:, 0:P], pw[:, u, 1], pw[:, u, 0], start=True, stop=True)
                                mm(X[u][:, P:2 * P], pw[:, u, 0], pw[:, u, 1], start=True, stop=True).then_inc(sq_done, 1)
                    for u in range(U):
                        pe.wait_ge(inv_out, i * U * SQ + U * (SQ - 1) + u + 1)
                        mm(X[u][:, 0:P + HALF], inv[:, u], am[:, u], start=True, stop=True).then_inc(tav_done, 1)
                    for u in range(U):
                        pe.wait_ge(tav_out, i * U + u + 1)
                        tmv = tav[:, u, P:P + HALF]
                        mm(Y[u][:, 0:2 * P], tav[:, u, 0:P], big[:, u, B_:N1 + 1].rearrange("p a b -> p (a b)"),
                           start=True, stop=True)
                        h = Y[u][:, 2 * P:2 * P + HALF]
                        mm(h, big[:, u, B_], tmv, start=True, stop=False)
                        mm(h, big[:, u, K_], vt[:, u], start=False, stop=True)
                        y = Y[u][:, 2 * P + HALF:3 * P]
                        mm(y, big[:, u, N1], tmv, start=True, stop=False)
                        mm(y, big[:, u, N2], vt[:, u], start=False, stop=False).then_inc(gr_done, 1)
                    for c in range(2):
                        for t in range(TL):
                            u = 2 * t + c
                            pe.wait_ge(gr_out, i * U + u + 1)
                            if c:
                                pe.wait_ge(z_out, i * U + t + 1)
                            mm(X[u][:, 3 * P:3 * P + HALF], gr[:, u, 0], z[:, t, c], start=True, stop=True)
                            mm(Y[u][:, 2 * P + HALF:3 * P], gr[:, u, 1], z[:, t, c], start=False,
                               stop=True).then_inc(z_done, 1)
                    for u in range(U):
                        pe.wait_ge(y_in, i * U + u + 1)
                        mm(X[u][:, 3 * P + HALF:4 * P], ydg[:, u], idh[:], start=True, stop=True).then_inc(y_turned, 1)
                    pe.wait_ge(z_out, i * U + U)



META = 16
T = META + SEQ
NORM_EPS = 1e-6


def make_identity(nc, pool, ident, sem):
    nc.gpsimd.memset(ident[:], 0.0).then_inc(sem, 1)
    pool.wait_ge(sem, 1)
    nc.gpsimd.affine_select(out=ident[:], in_=ident[:], compare_op=ALU.not_equal, fill=1.0,
                            base=0, pattern=[[-1, P]], channel_multiplier=1).then_inc(sem, 1)


class NormTurn:

    def __init__(self, nc, ph, outs, gains, spans, tile, made):
        self.nc, self.outs, self.gains, self.spans, self.tile, self.made = nc, outs, gains, spans, tile, made
        self.xh = ph.sb("xh", [P, 2, DM])
        self.sq = ph.sb("sq", [P, DM], mybir.dt.bfloat16)
        self.ss, self.rt, self.rs = (ph.sb(n, [P, 2]) for n in ("ss", "rt", "rs"))
        self.eps = ph.sb("neps", [P, 1])
        self.gain = ph.sb("gain", [P, len(gains), KT])
        self.ident = ph.sb("ident", [P, P])
        self.tp = ph.ps("tp", [P, 2, 2, 512])
        self.g_loaded, self.id_done, self.rooted, self.scaled, self.turned, self.out_done, self.own = (
            ph.sem(n) for n in ("g_loaded", "id_done", "nrooted", "scaled", "turned", "out_done", "n_own"))

    def load(self, sp):
        for n, g in enumerate(self.gains):
            sp.dma_start(self.gain[:, n], g).then_inc(self.g_loaded, 16)

    def constants(self, pool):
        make_identity(self.nc, pool, self.ident, self.id_done)
        self.nc.gpsimd.memset(self.eps[:], NORM_EPS).then_inc(self.id_done, 1)

    def square(self, act, n):
        r, b = self.spans[n][1], n % 2
        act.wait_ge(self.id_done, 3)
        act.wait_ge(self.made, n + 1)
        if n >= 2:
            act.wait_ge(self.scaled, n - 1)
        self.nc.scalar.activation(self.sq[0:r], self.tile(n), ACT.Square,
                                  accum_out=self.ss[0:r, b:b + 1]).then_inc(self.own, 1)
        act.wait_ge(self.own, n + 1)
        self.nc.scalar.activation(self.rt[0:r, b:b + 1], self.ss[0:r, b:b + 1], ACT.Sqrt, scale=1.0 / DM,
                                  bias=self.eps[0:r]).then_inc(self.rooted, 1)

    def scale(self, dve, v, n):
        r, b = self.spans[n][1], n % 2
        dve.wait_ge(self.rooted, n + 1)
        v(self.nc.vector.reciprocal(self.rs[0:r, b:b + 1], self.rt[0:r, b:b + 1]))
        if n >= 2:
            dve.wait_ge(self.turned, n - 1)
        self.nc.vector.tensor_scalar(self.xh[0:r, b], self.tile(n), self.rs[0:r, b:b + 1], None,
                                     ALU.mult).then_inc(self.scaled, 1)

    def turn(self, pe, n):
        r, b = self.spans[n][1], n % 2
        pe.wait_ge(self.scaled, n + 1)
        pe.wait_ge(self.id_done, 3)
        if n >= 2:
            pe.wait_ge(self.out_done, n - 1)
        for k in range(KT):
            last = self.nc.tensor.transpose(self.tp[:, b, k // 4, P * (k % 4):P * (k % 4) + r],
                                            self.xh[0:r, b, P * k:P * k + P], self.ident[0:r, 0:r])
        last.then_inc(self.turned, 1)

    def out(self, dve, n):
        (at, r), b = self.spans[n], n % 2
        dve.wait_ge(self.g_loaded, 16 * len(self.gains))
        dve.wait_ge(self.turned, n + 1)
        for i, out in enumerate(self.outs):
            for c in range(2):
                last = self.nc.vector.tensor_tensor(
                    out[:, 4 * c:4 * c + 4, at:at + r],
                    self.tp[:, b, c].rearrange("p (k q) -> p k q", k=4)[:, :, 0:r],
                    self.gain[:, i, 4 * c:4 * c + 4].unsqueeze(2).to_broadcast([P, 4, r]), ALU.mult)
        last.then_inc(self.out_done, 1)


def first_out(nc, D, proj, hnT):
    with Phase(nc, "fo") as ph:
        wo = ph.sb("wo", [P, KT, DM])
        xb = ph.sb("xb", [P, 2, DM])
        hb = ph.sb("hb", [P, 2, DM])
        gb = ph.sb("gb", [P, 2, DM])
        st = ph.sb("st", [P, 2, 6])
        mv = ph.sb("mv", [P, 2])
        rs = ph.sb("lrs", [P, 1])
        eps = ph.sb("eps", [P, 1])
        acc = ph.ps("acc", [P, 2, 2, 512])
        w_loaded, gb_loaded, v_own, made, meta_in, pad_ready, padded = (
            ph.sem(n) for n in ("w_loaded", "gb_loaded", "v_own", "made", "meta_in", "pad_ready", "padded"))
        stored = [ph.sem("h0_stored"), ph.sem("h1_stored")]
        x_loaded = [ph.sem("x0_loaded"), ph.sem("x1_loaded")]
        done, var_ready, rooted, summed = ph.sem("done"), ph.sem("var_ready"), ph.sem("rooted"), ph.sem("summed")
        h = D["h0"]
        spans = [(0, META)] + [(META + P * t, P) for t in range(NB)]
        norm = NormTurn(nc, ph, [hnT], [D["norm_mix_g_t"][0]], spans,
                        lambda n: hb[:, (n - 1) % 2] if n else hb[0:META, 1], made)
        with nc.Block() as block:

            @block.sync
            def _(sp):
                sp.dma_start(hb[0:META, 1], D["meta_tokens_2"]).then_inc(meta_in, 16)
                for k in range(KT):
                    sp.dma_start(wo[:, k], D["w_out"][P * k:P * k + P]).then_inc(w_loaded, 16)
                for t in range(2):
                    sp.dma_start(xb[:, t], D["x"][P * t:P * t + P]).then_inc(x_loaded[t], 16)
                sp.dma_start(gb[:, 0], D["ln_g"].partition_broadcast(P)).then_inc(gb_loaded, 16)
                sp.dma_start(gb[:, 1], D["ln_b"].partition_broadcast(P)).then_inc(gb_loaded, 16)
                norm.load(sp)
                sp.wait_ge(meta_in, 16)
                sp.dma_start(h[0:META], hb[0:META, 1]).then_inc(padded, 16)
                for t in range(NB):
                    sp.wait_ge(made, t + 2)
                    sp.dma_start(h[META + P * t:META + P * t + P], hb[:, t % 2]).then_inc(stored[t % 2], 16)
                    if t + 2 < NB:
                        sp.dma_start(xb[:, t % 2], D["x"][P * (t + 2):P * (t + 3)]).then_inc(x_loaded[t % 2], 16)
                sp.wait_ge(padded, 16)
                sp.wait_ge(summed, NB)
                sp.dma_start(h[META + SEQ:], xb[0:P - META, 0]).then_inc(padded, 16)
                sp.wait_ge(padded, 32)
                for b in range(2):
                    sp.wait_ge(stored[b], 16 * (NB // 2))

            @block.gpsimd
            def _(pool):
                norm.constants(pool)

            @block.tensor
            def _(pe):
                pe.wait_ge(w_loaded, 16 * KT)
                for t in range(NB):
                    if t >= 2:
                        pe.wait_ge(var_ready, t - 1)
                    for c in range(2):
                        for k in range(KT):
                            last = nc.tensor.matmul(acc[:, t % 2, c], proj[:, G_T + k, P * t:P * t + P],
                                                    wo[:, k, 512 * c:512 * c + 512], start=(k == 0), stop=(k == KT - 1))
                    last.then_inc(done, 1)
                    if t >= 1:
                        norm.turn(pe, t - 1)
                for n in (NB - 1, NB):
                    norm.turn(pe, n)

            @block.vector
            def _(dve):
                v = Chain(dve, v_own)
                nc.vector.memset(hnT[:, :, T:], 0.0).then_inc(pad_ready, 1)
                v(nc.vector.memset(eps[:], LN_EPS))
                dve.wait_ge(meta_in, 16)
                dve.sem_inc(made, 1)
                norm.scale(dve, v, 0)
                dve.wait_ge(gb_loaded, 32)
                dve.wait_ge(padded, 16)
                for t in range(NB):
                    b = t % 2
                    dve.wait_ge(done, t + 1)
                    dve.wait_ge(x_loaded[b], 16 * (t // 2 + 1))
                    if t >= 2:
                        dve.wait_ge(stored[b], 16 * (t // 2))
                    v(nc.vector.scalar_tensor_tensor(out=hb[:, b], in0=xb[:, b], scalar=ALPHA,
                                                     in1=acc[:, b].rearrange("p a b -> p (a b)"),
                                                     op0=ALU.mult, op1=ALU.add))
                    for c in range(2):
                        v.hold(nc.vector.bn_stats(st[:, c], hb[:, b, 512 * c:512 * c + 512]))
                    v.wait()
                    v(nc.vector.bn_aggr(mv[:], st[:].rearrange("p a b -> p (a b)")))
                    dve.sem_inc(var_ready, 1)
                    if t >= 1:
                        norm.scale(dve, v, t)
                    dve.wait_ge(rooted, t + 1)
                    v(nc.vector.reciprocal(rs[:], rs[:]))
                    v(nc.vector.tensor_scalar(hb[:, b], hb[:, b], mv[:, 0:1], rs[:], ALU.subtract, ALU.mult))
                    v(nc.vector.tensor_tensor(hb[:, b], hb[:, b], gb[:, 0], ALU.mult))
                    v(nc.vector.tensor_tensor(hb[:, b], hb[:, b], gb[:, 1], ALU.add))
                    dve.sem_inc(made, 1)
                    if t == NB - 1:
                        v(nc.vector.memset(xb[:, 0], 0.0))
                        dve.sem_inc(summed, NB)
                    if t >= 1:
                        norm.out(dve, t - 1)
                norm.scale(dve, v, NB)
                norm.out(dve, NB - 1)
                norm.out(dve, NB)

            @block.scalar
            def _(act):
                norm.square(act, 0)
                for t in range(NB):
                    act.wait_ge(var_ready, t + 1)
                    nc.scalar.activation(rs[:], mv[:, 1:2], ACT.Sqrt, bias=eps[:]).then_inc(rooted, 1)
                    norm.square(act, t + 1)


def first(nc, D, proj):
    with Phase(nc, "V") as pv:
        vpad = pv.sb("vpad", [P, NB + 1, KV, 3 * HALF])
        kkb = pv.sb("kkb", [P, TL, SEQ])
        bb = pv.sb("bb", [P, TL, SEQ])
        bonus = pv.sb("bonus", [P, TL, SEQ])
        wc = pv.sb("wc", [P, TL, NCH])
        vec = pv.sb("vec", [P, TL, 10])
        front(nc, D, proj, vpad, kkb, bb, bonus, wc, vec)
        window_attention(nc, D, proj, vpad)
        chunks(nc, D, proj, kkb, bb, bonus, wc, vec)

TT = -(-T // P)
TP = TT * P
LAST = T - (TT - 1) * P
CUTS = [(0, 352), (352, 352), (704, T - 704)]
GROUPS = 8
LG = GROUPS + 64
PER_GROUP = 8
EXPERTS = GROUPS * PER_GROUP
DE = 256
CAP = 64
MAIN_SLOTS = EXPERTS * CAP
SPILL_BLOCKS = 2 * T // CAP
SPILL_BLOCKS += SPILL_BLOCKS % 2
PER_EXPERT_SPILL = (T - 1) // CAP
SLOTS = MAIN_SLOTS + SPILL_BLOCKS * CAP
PAIRS_M = EXPERTS // 2
HEADS = 8
NOPE = 128
ROPE = 64
QR = 384
KVR = 256
VD = 128
ATT_SCALE = float(NOPE + ROPE) ** -0.5


def rows_of(t):
    return P if t < TT - 1 else LAST


def back_and_route(nc, D, layer, src, w_dram, h_in, h_out, lg):
    with Phase(nc, "pb") as ph:
        NBUF = 2
        w = ph.sb("w", [P, KT, DM])
        hb = ph.sb("hb", [P, NBUF, DM])
        ho = ph.sb("ho", [P, 2, DM])
        hn = ph.sb("hn", [P, 2, DM])
        hnT = ph.sb("hnT", [P, 2, KT, P])
        gb = ph.sb("gb", [P, DM])
        wr = ph.sb("wr", [P, KT, LG])
        sq = ph.sb("sq", [P, DM], mybir.dt.bfloat16)
        ss, rt, rs = (ph.sb(n, [P, 2]) for n in ("ss", "rt", "rs"))
        eps = ph.sb("eps", [P, 1])
        ident = ph.sb("ident", [P, P])
        acc = ph.ps("acc", [P, 2, 2, 512])
        tp = ph.ps("tp", [P, 2, 512])
        lg_ps = ph.ps("lg_ps", [P, 2, 512])
        (w_loaded, r_loaded, done, summed, id_done, squared, rooted, scaled, turned, evac, lg_done, lg_out, v_own) = (
            ph.sem(n) for n in ("w_loaded", "r_loaded", "done", "summed", "id_done", "squared", "rooted", "scaled", "turned",
                                "evac", "lg_done", "lg_out", "v_own"))
        loaded = [ph.sem(f"h{n}_loaded") for n in range(NBUF)]
        stored = [ph.sem(f"h{n}_stored") for n in range(2)]
        hn_stored = [ph.sem(f"hn{n}_stored") for n in range(2)]
        with nc.Block() as block:

            @block.sync
            def _(sp):
                for k in range(KT):
                    sp.dma_start(w[:, k], w_dram[P * k:P * k + P]).then_inc(w_loaded, 16)
                sp.dma_start(wr[:], D["w_route_t"][layer]).then_inc(r_loaded, 16)
                sp.dma_start(gb[:], D["norm_ffn_g_2"][layer].partition_broadcast(P)).then_inc(r_loaded, 16)
                for t in range(TT):
                    if t >= NBUF:
                        sp.wait_ge(summed, t - NBUF + 1)
                    sp.dma_start(hb[:, t % NBUF], h_in[P * t:P * t + P]).then_inc(loaded[t % NBUF], 16)

            @block.gpsimd
            def _(pool):
                make_identity(nc, pool, ident, id_done)
                nc.gpsimd.memset(eps[:], NORM_EPS).then_inc(id_done, 1)

            @block.scalar
            def _(act):
                act.wait_ge(id_done, 3)

                def logits_out(t):
                    act.wait_ge(lg_done, t + 1)
                    nc.scalar.copy(lg[:, t], lg_ps[:, t % 2, 0:LG]).then_inc(lg_out, 1)

                for t in range(TT):
                    b = t % 2
                    act.wait_ge(summed, t + 1)
                    act.dma_start(h_out[P * t:P * t + P], ho[:, b]).then_inc(stored[b], 16)
                    if t >= 2:
                        act.wait_ge(scaled, t - 1)
                    nc.scalar.activation(sq[:], ho[:, b], ACT.Square, accum_out=ss[:, b:b + 1]).then_inc(squared, 1)
                    act.wait_ge(squared, t + 1)
                    nc.scalar.activation(rt[:, b:b + 1], ss[:, b:b + 1], ACT.Sqrt, scale=1.0 / DM,
                                         bias=eps[:]).then_inc(rooted, 1)
                    act.wait_ge(scaled, t + 1)
                    act.dma_start(D["hn"][P * t:P * t + P], hn[:, b]).then_inc(hn_stored[b], 16)
                    if t >= 2:
                        logits_out(t - 2)
                logits_out(TT - 2)
                logits_out(TT - 1)
                for b in range(2):
                    act.wait_ge(stored[b], 16 * ((TT + 1 - b) // 2))
                    act.wait_ge(hn_stored[b], 16 * ((TT + 1 - b) // 2))

            @block.tensor
            def _(pe):
                pe.wait_ge(w_loaded, 16 * KT)
                pe.wait_ge(id_done, 3)

                def turn(t):
                    pe.wait_ge(scaled, t + 1)
                    if t >= 1:
                        pe.wait_ge(evac, t)
                    for k in range(KT):
                        last = nc.tensor.transpose(tp[:, k // 4, P * (k % 4):P * (k % 4) + P],
                                                   hn[:, t % 2, P * k:P * k + P], ident[:])
                    last.then_inc(turned, 1)

                def logits(t):
                    pe.wait_ge(evac, t + 1)
                    pe.wait_ge(r_loaded, 32)
                    if t >= 2:
                        pe.wait_ge(lg_out, t - 1)
                    for k in range(KT):
                        last = nc.tensor.matmul(lg_ps[:, t % 2, 0:LG], hnT[:, t % 2, k], wr[:, k],
                                                start=(k == 0), stop=(k == KT - 1))
                    last.then_inc(lg_done, 1)

                for t in range(TT):
                    if t >= 2:
                        pe.wait_ge(summed, t - 1)
                    for c in range(2):
                        for k in range(KT):
                            last = nc.tensor.matmul(acc[:, t % 2, c], src[:, k, P * t:P * t + P],
                                                    w[:, k, 512 * c:512 * c + 512], start=(k == 0), stop=(k == KT - 1))
                    last.then_inc(done, 1)
                    if t >= 1:
                        turn(t - 1)
                    if t >= 2:
                        logits(t - 2)
                logits(TT - 2)
                turn(TT - 1)
                logits(TT - 1)

            @block.vector
            def _(dve):
                v = Chain(dve, v_own)
                dve.wait_ge(r_loaded, 32)

                def scale(t):
                    b = t % 2
                    dve.wait_ge(rooted, t + 1)
                    v(nc.vector.reciprocal(rs[:, b:b + 1], rt[:, b:b + 1]))
                    if t >= 2:
                        dve.wait_ge(turned, t - 1)
                        dve.wait_ge(hn_stored[b], 16 * (t // 2))
                    nc.vector.scalar_tensor_tensor(out=hn[:, b], in0=ho[:, b], scalar=rs[:, b:b + 1], in1=gb[:],
                                                   op0=ALU.mult, op1=ALU.mult).then_inc(scaled, 1)

                def evacuate(t):
                    dve.wait_ge(turned, t + 1)
                    if t >= 2:
                        dve.wait_ge(lg_done, t - 1)
                    nc.vector.tensor_copy(hnT[:, t % 2].rearrange("p k q -> p (k q)"),
                                          tp[:].rearrange("p a b -> p (a b)")).then_inc(evac, 1)

                for t in range(TT):
                    dve.wait_ge(done, t + 1)
                    dve.wait_ge(loaded[t % NBUF], 16 * (t // NBUF + 1))
                    if t >= 2:
                        dve.wait_ge(stored[t % 2], 16 * (t // 2))
                    nc.vector.tensor_tensor(ho[:, t % 2], acc[:, t % 2].rearrange("p a b -> p (a b)"),
                                            hb[:, t % NBUF], ALU.add).then_inc(summed, 1)
                    scale(t)
                    if t >= 1:
                        evacuate(t - 1)
                evacuate(TT - 1)


def conv_mixer(nc, D, hnT, zT):
    with Phase(nc, "cm") as ph:
        w = ph.sb("w", [P, 2, 3, KT, P])
        taps = ph.sb("taps", [P, KT, 3])
        bT = ph.sb("bT", [P, 2, T])
        cT = ph.sb("cT", [P, 2, 352])
        z = ph.sb("z", [P, 2, T + 2])
        acc = ph.ps("acc", [P, 2, 3, 512])
        w_loaded = [ph.sem(f"w{n}_loaded") for n in range(2)]
        w_used = [ph.sem(f"w{n}_used") for n in range(2)]
        taps_loaded, done, copied, z_made, conv_done, v_own = (
            ph.sem(n) for n in ("taps_loaded", "done", "copied", "z_made", "conv_done", "v_own"))
        NC = len(CUTS)
        with nc.Block() as block:

            @block.sync
            def _(sp):
                sp.dma_start(taps[:], D["conv_w_2_t"]).then_inc(taps_loaded, 16)
                for j in range(KT):
                    if j >= 2:
                        sp.wait_ge(done, NC * (j - 1))
                    sp.dma_start(w[:, j % 2], D["conv_w_in_t"][j]).then_inc(w_loaded[j % 2], 16)

            @block.tensor
            def _(pe):
                for j in range(KT):
                    pe.wait_ge(w_loaded[j % 2], 16 * (j // 2 + 1))
                    for n, (at, cols) in enumerate(CUTS):
                        u = NC * j + n
                        if u >= 2:
                            pe.wait_ge(z_made, u - 1)
                            pe.wait_ge(copied, u - 1)
                        for s in range(3):
                            for k in range(KT):
                                last = nc.tensor.matmul(acc[:, u % 2, s, 0:cols], w[:, j % 2, s, k],
                                                        hnT[:, k, at:at + cols], start=(k == 0), stop=(k == KT - 1))
                        last.then_inc(done, 1)

            @block.scalar
            def _(act):
                for j in range(KT):
                    if j >= 2:
                        act.wait_ge(conv_done, j - 1)
                    for n, (at, cols) in enumerate(CUTS):
                        u = NC * j + n
                        act.wait_ge(done, u + 1)
                        if u >= 2:
                            act.wait_ge(z_made, u - 1)
                        nc.scalar.copy(bT[:, j % 2, at:at + cols], acc[:, u % 2, 0, 0:cols])
                        nc.scalar.copy(cT[:, u % 2, 0:cols], acc[:, u % 2, 1, 0:cols]).then_inc(copied, 1)

            @block.vector
            def _(dve):
                v = Chain(dve, v_own)
                v.hold(nc.vector.memset(zT[:, :, T:TP], 0.0))
                v(nc.vector.memset(z[:, :, 0:2], 0.0))
                dve.wait_ge(taps_loaded, 16)
                for j in range(KT):
                    for n, (at, cols) in enumerate(CUTS):
                        u = NC * j + n
                        dve.wait_ge(copied, u + 1)
                        nc.vector.tensor_tensor(z[:, j % 2, 2 + at:2 + at + cols], cT[:, u % 2, 0:cols],
                                                acc[:, u % 2, 2, 0:cols], ALU.mult).then_inc(z_made, 1)
                    dve.wait_ge(z_made, NC * (j + 1))
                    v(nc.vector.tensor_scalar(zT[:, j, 0:T], z[:, j % 2, 0:T], taps[:, j, 0:1], None, ALU.mult))
                    for s in (1, 2):
                        v(nc.vector.scalar_tensor_tensor(out=zT[:, j, 0:T], in0=z[:, j % 2, s:s + T],
                                                         scalar=taps[:, j, s:s + 1], in1=zT[:, j, 0:T],
                                                         op0=ALU.mult, op1=ALU.add))
                    v(nc.vector.tensor_tensor(zT[:, j, 0:T], zT[:, j, 0:T], bT[:, j % 2], ALU.mult))
                    dve.sem_inc(conv_done, 1)


def latents(nc, D, hq, hk, cq, ckv, kr):
    QT, CT = QR // P, KVR // P
    with Phase(nc, "la") as ph:
        wq = ph.sb("wq", [P, KT, QR])
        wk = ph.sb("wk", [P, KT, KVR])
        wr = ph.sb("wr", [P, KT, 2, P])
        gq = ph.sb("gq", [P, QT])
        gk = ph.sb("gk", [P, CT])
        cosT = ph.sb("cosT", [P, T])
        sinT = ph.sb("sinT", [P, T])
        ident = ph.sb("ident", [P, P])
        lat = ph.sb("lat", [P, 2, QR + KVR])
        sq = ph.sb("sq", [P, QR])
        ss = ph.sb("ss", [P, 2, 2])
        rs = ph.sb("rs", [P, 2, 2])
        eps = ph.sb("eps", [P, 1])
        rot = ph.sb("rot", [P, 2, 352])
        acc = ph.ps("acc", [P, 2, 2, 512])
        tp = ph.ps("tp", [P, 2, 512])
        tk = ph.ps("tk", [P, 2, 512])
        loaded, id_done, eps_done, done, squared, rooted, scaled, turned, out_done, v_own, a_own, rope_done, rope_out = (
            ph.sem(n) for n in ("loaded", "id_done", "eps_done", "done", "squared", "rooted", "scaled", "turned", "out_done",
                                "v_own", "a_own", "rope_done", "rope_out"))
        with nc.Block() as block:

            @block.sync
            def _(sp):
                for dst, src in ((wq, "w_dq_t"), (wk, "w_dkv_t"), (wr, "w_rope_t"), (gq, "cq_g_t"), (gk, "ckv_g_t"),
                                 (cosT, "cos_t"), (sinT, "sin_t")):
                    sp.dma_start(dst[:], D[src]).then_inc(loaded, 16)

            @block.gpsimd
            def _(pool):
                make_identity(nc, pool, ident, id_done)

            @block.tensor
            def _(pe):
                pe.wait_ge(loaded, 16 * 7)
                pe.wait_ge(id_done, 2)

                def turn(t):
                    pe.wait_ge(scaled, t + 1)
                    for n in range(QT + CT):
                        dst = tp[:, t % 2, P * n:P * n + P] if n < QT else tk[:, t % 2, P * (n - QT):P * (n - QT) + P]
                        last = nc.tensor.transpose(dst, lat[:, t % 2, P * n:P * n + P], ident[:])
                    last.then_inc(turned, 1)

                for t in range(TT):
                    if t >= 2:
                        pe.wait_ge(scaled, t - 1)
                        pe.wait_ge(out_done, t - 1)
                    for w, src, cols, c in ((wq, hq, QR, 0), (wk, hk, KVR, 1)):
                        for k in range(KT):
                            last = nc.tensor.matmul(acc[:, t % 2, c, 0:cols], src[:, k, P * t:P * t + P], w[:, k],
                                                    start=(k == 0), stop=(k == KT - 1))
                    last.then_inc(done, 1)
                    if t >= 1:
                        turn(t - 1)
                turn(TT - 1)
                pe.wait_ge(out_done, TT)
                for n, (at, cols) in enumerate(CUTS):
                    if n >= 2:
                        pe.wait_ge(rope_out, n - 1)
                    for s in range(2):
                        for k in range(KT):
                            last = nc.tensor.matmul(acc[:, n % 2, s, 0:cols], wr[:, k, s], hk[:, k, at:at + cols],
                                                    start=(k == 0), stop=(k == KT - 1))
                    last.then_inc(rope_done, 1)

            @block.scalar
            def _(act):
                a = Chain(act, a_own)
                act.wait_ge(eps_done, 1)
                for t in range(TT):
                    b = t % 2
                    act.wait_ge(done, t + 1)
                    if t >= 2:
                        act.wait_ge(scaled, t - 1)
                    a(nc.scalar.activation(sq[:], acc[:, b, 0, 0:QR], ACT.Square, accum_out=ss[:, b, 0:1]))
                    a(nc.scalar.activation(sq[:, 0:KVR], acc[:, b, 1, 0:KVR], ACT.Square, accum_out=ss[:, b, 1:2]))
                    nc.scalar.activation(ss[:, b, 0:1], ss[:, b, 0:1], ACT.Sqrt, scale=1.0 / QR, bias=eps[:])
                    nc.scalar.activation(ss[:, b, 1:2], ss[:, b, 1:2], ACT.Sqrt, scale=1.0 / KVR,
                                         bias=eps[:]).then_inc(rooted, 1)

            @block.vector
            def _(dve):
                v = Chain(dve, v_own)
                nc.vector.memset(eps[:], NORM_EPS).then_inc(eps_done, 1)
                v(nc.vector.memset(kr[:], 0.0))
                dve.wait_ge(loaded, 16 * 7)

                def evacuate(t):
                    dve.wait_ge(turned, t + 1)
                    nc.vector.tensor_tensor(cq[:, :, P * t:P * t + P],
                                            tp[:, t % 2, 0:QR].rearrange("p (k q) -> p k q", k=QT),
                                            gq[:].unsqueeze(2).to_broadcast([P, QT, P]), ALU.mult)
                    nc.vector.tensor_tensor(ckv[:, :, P * t:P * t + P],
                                            tk[:, t % 2, 0:KVR].rearrange("p (k q) -> p k q", k=CT),
                                            gk[:].unsqueeze(2).to_broadcast([P, CT, P]), ALU.mult).then_inc(out_done, 1)

                for t in range(TT):
                    b = t % 2
                    dve.wait_ge(rooted, t + 1)
                    v(nc.vector.reciprocal(rs[:, b], ss[:, b]))
                    if t >= 2:
                        dve.wait_ge(turned, t - 1)
                    nc.vector.tensor_scalar(lat[:, b, 0:QR], acc[:, b, 0, 0:QR], rs[:, b, 0:1], None, ALU.mult)
                    nc.vector.tensor_scalar(lat[:, b, QR:], acc[:, b, 1, 0:KVR], rs[:, b, 1:2], None,
                                            ALU.mult).then_inc(scaled, 1)
                    if t >= 1:
                        evacuate(t - 1)
                evacuate(TT - 1)
                for n, (at, cols) in enumerate(CUTS):
                    dve.wait_ge(rope_done, n + 1)
                    v.hold(nc.vector.tensor_tensor(rot[:, 0, 0:cols], acc[:, n % 2, 0, 0:cols], cosT[:, at:at + cols], ALU.mult))
                    v(nc.vector.tensor_tensor(rot[:, 1, 0:cols], acc[:, n % 2, 1, 0:cols], sinT[:, at:at + cols], ALU.mult))
                    for h in range(2):
                        hp = slice(HALF * h, HALF * h + HALF)
                        v.hold(nc.vector.tensor_tensor(kr[hp, h, at:at + cols], rot[hp, 0, 0:cols], rot[hp, 1, 0:cols], ALU.add))
                    v.wait()
                    dve.sem_inc(rope_out, 1)


def heads(nc, D, cq, ckv, kr, oT):
    QT, CT = QR // P, KVR // P
    with Phase(nc, "hd") as ph:
        wq = ph.sb("wq", [P, 2, QT, 4, P])
        wkv = ph.sb("wkv", [P, 2, CT, 4, P])
        cosT = ph.sb("cosT", [P, T])
        sinT = ph.sb("sinT", [P, T])
        qn = ph.sb("qn", [P, 2, TP])
        qr = ph.sb("qr", [P, TP])
        rot = ph.sb("rot", [P, 352])
        kn = ph.sb("kn", [P, 2, TP])
        vv = ph.sb("vv", [P, TT, 2, VD])
        pr = ph.sb("pr", [P, 2, TP])
        pT = ph.sb("pT", [P, 2, TT, P])
        mx = ph.sb("mx", [P, 2])
        nm = ph.sb("nm", [P, 2])
        ls = ph.sb("ls", [P, 2])
        rl = ph.sb("rl", [P, 2])
        osb = ph.sb("osb", [P, 2, VD])
        ident = ph.sb("ident", [P, P])
        mask = ph.sb("mask", [P, P])
        s_ps = ph.ps("s", [P, 3 * 512])
        t_ps = ph.ps("t", [P, 2, 512])
        o_ps = ph.ps("o", [P, 512])
        p_ps = ph.ps("p", [P, 2, 512])
        w_loaded = [ph.sem(f"w{n}_loaded") for n in range(2)]
        (tab_loaded, id_done, mask_done, w_used, pdone, pout, v_own, a_own, ready, scored, maxed, exped, turned, turned_out,
         mixed, normed, oturned, oout, sfree) = (ph.sem(n) for n in (
             "tab_loaded", "id_done", "mask_done", "w_used", "pdone", "pout", "v_own", "a_own", "ready", "scored", "maxed",
             "exped", "turned", "turned_out", "mixed", "normed", "oturned", "oout", "sfree"))
        NPAIR = HEADS // 2
        jobs = ([("qn", h, c) for h in range(2) for c in range(3)] + [("qa", 0, c) for c in range(3) for _ in (0,)]
                + [("kn", h, c) for h in range(2) for c in range(3)] + [("v", 0, t) for t in range(TT)])
        order = []
        for kind, h, c in jobs:
            order.append((kind, h, c))
            if kind == "qa":
                order.append(("qb", h, c))
        NJ = len(order)
        units = [(t, h) for t in range(TT) for h in range(2)]
        NU = len(units)

        def quads(t):
            return -(-(t + 1) // 4)
        NQ = sum(quads(t) for t, _ in units)
        qbase = [sum(quads(t) for t, _ in units[:n]) for n in range(NU)]
        with nc.Block() as block:

            @block.sync
            def _(sp):
                sp.dma_start(cosT[:], D["cos_t"]).then_inc(tab_loaded, 16)
                sp.dma_start(sinT[:], D["sin_t"]).then_inc(tab_loaded, 16)
                for j in range(NPAIR):
                    if j >= 2:
                        sp.wait_ge(pdone, NJ * (j - 1))
                    sp.dma_start(wq[:, j % 2], D["w_uq_t"][j]).then_inc(w_loaded[j % 2], 16)
                    sp.dma_start(wkv[:, j % 2], D["w_ukv_t"][j]).then_inc(w_loaded[j % 2], 16)

            @block.gpsimd
            def _(pool):
                make_identity(nc, pool, ident, id_done)
                nc.gpsimd.memset(mask[:], 0.0).then_inc(mask_done, 1)
                pool.wait_ge(mask_done, 1)
                nc.gpsimd.affine_select(out=mask[:], in_=mask[:], compare_op=ALU.is_ge, fill=MASKED, base=0,
                                        pattern=[[-1, P]], channel_multiplier=1).then_inc(mask_done, 1)

            @block.tensor
            def _(pe):
                mm = nc.tensor.matmul
                pe.wait_ge(id_done, 2)
                for j in range(NPAIR):
                    b = j % 2
                    pe.wait_ge(w_loaded[b], 32 * (j // 2 + 1))
                    for n, (kind, h, c) in enumerate(order):
                        m = NJ * j + n
                        if m >= 2:
                            pe.wait_ge(pout, m - 1)
                        bank = p_ps[:, m % 2]
                        if kind == "v":
                            for k in range(CT):
                                last = mm(bank[:, 0:2 * VD], ckv[:, k, P * c:P * c + P],
                                          wkv[:, b, k, 2:4].rearrange("p a b -> p (a b)"),
                                          start=(k == 0), stop=(k == CT - 1))
                        else:
                            at, cols = CUTS[c]
                            w, src, kt = (wkv, ckv, CT) if kind == "kn" else (wq, cq, QT)
                            which = {"kn": h, "qn": h, "qa": 2, "qb": 3}[kind]
                            for k in range(kt):
                                last = mm(bank[:, 0:cols], w[:, b, k, which], src[:, k, at:at + cols],
                                          start=(k == 0), stop=(k == kt - 1))
                        last.then_inc(pdone, 1)
                    pe.wait_ge(ready, j + 1)

                    def score(n):
                        t, h = units[n]
                        u = NU * j + n
                        if u >= 1:
                            pe.wait_ge(exped, u)
                        for c in range(quads(t)):
                            keys = min(P * (t + 1), T) - 512 * c
                            cols = min(512, keys)
                            bank = s_ps[:, 512 * c:512 * c + cols]
                            mm(bank, qn[:, h, P * t:P * t + P], kn[:, h, 512 * c:512 * c + cols], start=True, stop=False)
                            last = mm(bank, qr[:, P * t:P * t + P], kr[:, h, 512 * c:512 * c + cols], start=False, stop=True)
                        last.then_inc(scored, 1)

                    score(0)
                    for n, (t, h) in enumerate(units):
                        u = NU * j + n
                        pe.wait_ge(exped, u + 1)
                        if n + 1 < NU:
                            score(n + 1)
                        for c in range(quads(t)):
                            q = NQ * j + qbase[n] + c
                            if q >= 2:
                                pe.wait_ge(turned_out, q - 1)
                            for s in range(4 * c, min(4 * c + 4, t + 1)):
                                k = min(P, T - P * s)
                                last = nc.tensor.transpose(t_ps[0:k, q % 2, P * (s % 4):P * (s % 4) + P],
                                                           pr[:, u % 2, P * s:P * s + k], ident[:])
                            last.then_inc(turned, 1)
                        pe.wait_ge(turned_out, NQ * j + qbase[n] + quads(t))
                        if u >= 1:
                            pe.wait_ge(oout, u)
                        for s in range(t + 1):
                            k = min(P, T - P * s)
                            last = mm(o_ps[:, 0:VD], pT[0:k, u % 2, s], vv[0:k, s, h], start=(s == 0), stop=(s == t))
                        last.then_inc(mixed, 1)
                        pe.wait_ge(normed, u + 1)
                        nc.tensor.transpose(o_ps[:, P:2 * P], osb[:, u % 2], ident[:]).then_inc(oturned, 1)

            @block.scalar
            def _(act):
                a = Chain(act, a_own)
                for j in range(NPAIR):
                    for n, (t, h) in enumerate(units):
                        u = NU * j + n
                        act.wait_ge(maxed, u + 1)
                        if u >= 2:
                            act.wait_ge(mixed, u - 1)
                        keys = min(P * (t + 1), T)
                        nc.scalar.activation(pr[:, u % 2, 0:keys], s_ps[:, 0:keys], ACT.Exp, scale=ATT_SCALE,
                                             bias=nm[:, u % 2:u % 2 + 1], accum_out=ls[:, u % 2:u % 2 + 1]).then_inc(exped, 1)
                        for c in range(quads(t)):
                            q = NQ * j + qbase[n] + c
                            act.wait_ge(turned, q + 1)
                            full = [s for s in range(4 * c, min(4 * c + 4, t + 1)) if P * s + P <= T]
                            part = [s for s in range(4 * c, min(4 * c + 4, t + 1)) if P * s + P > T]
                            if full:
                                last = nc.scalar.copy(pT[:, u % 2, full[0]:full[-1] + 1],
                                                      t_ps[:, q % 2, 0:P * len(full)].rearrange("p (s q) -> p s q", q=P))
                            if part:
                                s = part[0]
                                last = nc.scalar.copy(pT[0:T - P * s, u % 2, s], t_ps[0:T - P * s, q % 2, P * (s % 4):P * (s % 4) + P])
                            last.then_inc(turned_out, 1)

            @block.vector
            def _(dve):
                v = Chain(dve, v_own)
                v.hold(nc.vector.memset(qn[:, :, T:], 0.0))
                v(nc.vector.memset(qr[:, T:], 0.0))
                dve.wait_ge(tab_loaded, 32)
                dve.wait_ge(mask_done, 2)
                for j in range(NPAIR):
                    if j:
                        dve.wait_ge(mixed, NU * j)
                    for n, (kind, h, c) in enumerate(order):
                        m = NJ * j + n
                        dve.wait_ge(pdone, m + 1)
                        bank = p_ps[:, m % 2]
                        if kind == "v":
                            v.hold(nc.vector.tensor_copy(vv[:, c].rearrange("p a b -> p (a b)"), bank[:, 0:2 * VD]))
                        else:
                            at, cols = CUTS[c]
                            if kind == "qn":
                                v.hold(nc.vector.tensor_copy(qn[:, h, at:at + cols], bank[:, 0:cols]))
                            elif kind == "kn":
                                v.hold(nc.vector.tensor_copy(kn[:, h, at:at + cols], bank[:, 0:cols]))
                            elif kind == "qa":
                                v(nc.vector.tensor_tensor(qr[:, at:at + cols], bank[:, 0:cols], cosT[:, at:at + cols], ALU.mult))
                            else:
                                v(nc.vector.tensor_tensor(rot[:, 0:cols], bank[:, 0:cols], sinT[:, at:at + cols], ALU.mult))
                                v(nc.vector.tensor_tensor(qr[:, at:at + cols], qr[:, at:at + cols], rot[:, 0:cols], ALU.add))
                        v.wait()
                        dve.sem_inc(pout, 1)
                    dve.sem_inc(ready, 1)
                    def finish(n):
                        u = NU * j + n
                        t, h = units[n]
                        b = u % 2
                        dve.wait_ge(mixed, u + 1)
                        v(nc.vector.reciprocal(rl[:, b:b + 1], ls[:, b:b + 1]))
                        nc.vector.tensor_scalar(osb[:, b], o_ps[:, 0:VD], rl[:, b:b + 1], None, ALU.mult).then_inc(normed, 1)
                        dve.wait_ge(oturned, u + 1)
                        nc.vector.tensor_copy(oT[:, 2 * j + h, P * t:P * t + P], o_ps[:, P:2 * P]).then_inc(oout, 1)

                    for n, (t, h) in enumerate(units):
                        u = NU * j + n
                        dve.wait_ge(scored, u + 1)
                        keys = min(P * (t + 1), T)
                        diag = s_ps[:, P * t:keys]
                        v(nc.vector.tensor_tensor(diag, diag, mask[:, 0:keys - P * t], ALU.add))
                        v(nc.vector.tensor_reduce(mx[:, u % 2:u % 2 + 1], s_ps[:, 0:keys], AX.X, ALU.max))
                        nc.vector.tensor_scalar(nm[:, u % 2:u % 2 + 1], mx[:, u % 2:u % 2 + 1], -ATT_SCALE, None,
                                                ALU.mult).then_inc(maxed, 1)
                        if n >= 1:
                            finish(n - 1)
                    finish(NU - 1)

QUEUE_ROWS = SLOTS // P
SPILL_PAIRS = SPILL_BLOCKS // 2
EMPTY = 1 << 20
BIG = 1.0e30
ROUTE_CUT = TT * EXPERTS // 2


def route(nc, D, lg, gate, queue, spill, start_weights):
    with Phase(nc, "rt") as ph:
        slot_f = ph.sb("slot_f", [P, TT, 2])
        dest = ph.sb("dest", [P, TT, 2], I32)
        rk_ps = ph.ps("rk_ps", [P, 2, 512])
        zero_q = ph.sb("zero_q", [P, QUEUE_ROWS], I32)
        up = ph.sb("up", [P, P])
        ones = ph.sb("ones", [P, P])
        valid = ph.sb("valid", [P, TT])
        pri = ph.sb("pri", [P, 8])
        pri_i = ph.sb("pri_i", [P, 8], I32)
        first = ph.sb("first", [P, EXPERTS])
        first_i = ph.sb("first_i", [P, EXPERTS], I32)
        steps = ph.sb("steps", [P, PER_EXPERT_SPILL])
        steps_i = ph.sb("steps_i", [P, PER_EXPERT_SPILL], I32)
        blocks = ph.sb("blocks", [P, SPILL_BLOCKS])
        blocks_i = ph.sb("blocks_i", [P, SPILL_BLOCKS], I32)
        choice = ph.sb("choice", [P, TT, 2], I32)
        m8 = ph.sb("m8", [P, TT])
        cand = ph.sb("cand", [P, TT, 8])
        ohg = ph.sb("ohg", [P, TT, 8])
        gexp = ph.sb("gexp", [P, TT, 8])
        pg = ph.sb("pg", [P, TT])
        ein = ph.sb("ein", [P, TT, 8])
        oh = ph.sb("oh", [P, 2, TT, 8])
        top = ph.sb("top", [P, 2, TT])
        ed = ph.sb("ed", [P, TT])
        big = ph.sb("big", [P, TT, EXPERTS])
        chosen = ph.sb("chosen", [P, 2, TT, EXPERTS])
        both = ph.sb("both", [P, TT, EXPERTS])
        base = ph.sb("base", [P, TT + 1, EXPERTS])
        rank = ph.sb("rank", [P, TT, EXPERTS])
        over = ph.sb("over", [P, EXPERTS, PER_EXPERT_SPILL])
        nspill = ph.sb("nspill", [P, EXPERTS])
        send = ph.sb("send", [P, EXPERTS])
        jump = ph.sb("jump", [P, EXPERTS])
        owner = ph.sb("owner", [1, SPILL_BLOCKS, EXPERTS])
        owners = ph.sb("owners", [1, SPILL_BLOCKS + 1])
        ones_row = ph.sb("ones_row", [P, EXPERTS])
        names = ("const_done", "v_own", "soft_in", "soft_out", "diff_in", "diff_out", "picked", "ranked", "totals_out",
                 "totals_done", "slots_ready", "queue_zero", "scattered", "queue_loaded")
        (const_done, v_own, soft_in, soft_out, diff_in, diff_out, picked, ranked, totals_out, totals_done, slots_ready,
         queue_zero, scattered, queue_loaded) = (ph.sem(n) for n in names)
        table = D["table"]
        with nc.Block() as block:

            @block.sync
            def _(sp):
                start_weights(sp)

            @block.gpsimd
            def _(pool):
                g = nc.gpsimd
                for m in (up, ones, valid, zero_q):
                    g.memset(m[:], EMPTY if m is zero_q else 1.0).then_inc(const_done, 1)
                g.iota(pri_i[:], pattern=[[-1, 8]], base=8, channel_multiplier=0).then_inc(const_done, 1)
                g.iota(first_i[:], pattern=[[CAP, EXPERTS]], base=0, channel_multiplier=0).then_inc(const_done, 1)
                g.iota(steps_i[:], pattern=[[CAP, PER_EXPERT_SPILL]], base=CAP, channel_multiplier=0).then_inc(const_done, 1)
                g.iota(blocks_i[:], pattern=[[1, SPILL_BLOCKS]], base=0, channel_multiplier=0).then_inc(const_done, 1)
                g.iota(choice[:], pattern=[[2 * P, TT], [1, 2]], base=0, channel_multiplier=2).then_inc(const_done, 1)
                pool.wait_ge(const_done, 9)
                g.affine_select(out=up[:], in_=up[:], compare_op=ALU.is_gt, fill=0.0, base=0,
                                pattern=[[1, P]], channel_multiplier=-1).then_inc(const_done, 1)
                g.affine_select(out=valid[:], in_=valid[:], compare_op=ALU.is_gt, fill=0.0, base=T,
                                pattern=[[-P, TT]], channel_multiplier=-1).then_inc(const_done, 1)
                pool.dma_start(table.rearrange("(p q) a -> p (q a)", p=P), zero_q[:]).then_inc(queue_zero, 16)
                pool.wait_ge(queue_zero, 16)
                pool.wait_ge(slots_ready, 1)
                for t in range(TT):
                    for c in range(2):
                        g.indirect_dma_start(table[:, :], bass.IndirectOffsetOnAxis(ap=dest[0:rows_of(t), t, c:c + 1], axis=0),
                                             choice[0:rows_of(t), t, c:c + 1], None).then_inc(scattered, 16)
                pool.wait_ge(scattered, 16 * 2 * TT)
                pool.dma_start(queue[:, 1], table.rearrange("(q p) a -> p (q a)", p=P), allow_slow_non_contiguous=True).then_inc(queue_loaded, 16)
                pool.wait_ge(queue_loaded, 16)

            @block.scalar
            def _(act):
                act.wait_ge(soft_in, 1)
                nc.scalar.activation(gexp[:], gexp[:], ACT.Exp).then_inc(soft_out, 1)
                act.wait_ge(diff_in, 1)
                nc.scalar.activation(ed[:], ed[:], ACT.Exp).then_inc(diff_out, 1)

            @block.tensor
            def _(pe):
                pe.wait_ge(const_done, 11)
                pe.wait_ge(picked, 1)
                flat = both[:].rearrange("p t e -> p (t e)")
                for n, m in enumerate((ones, up)):
                    if n:
                        pe.wait_ge(totals_out, 1)
                    for c in range(2):
                        last = nc.tensor.matmul(rk_ps[:, c, 0:ROUTE_CUT], m[:], flat[:, ROUTE_CUT * c:ROUTE_CUT * c + ROUTE_CUT],
                                                start=True, stop=True)
                    last.then_inc(totals_done if n == 0 else ranked, 1)

            @block.vector
            def _(dve):
                v = Chain(dve, v_own)
                V = nc.vector
                tt, ts, stt, red = V.tensor_tensor, V.tensor_scalar, V.scalar_tensor_tensor, V.tensor_reduce
                dve.wait_ge(const_done, 11)
                v.hold(V.memset(ones_row[:], 1.0))
                for dst, src in ((pri, pri_i), (first, first_i), (steps, steps_i), (blocks, blocks_i)):
                    v.hold(V.tensor_copy(dst[:], src[:]))
                v.wait()

                def wide(x, n=8):
                    return x.unsqueeze(2).to_broadcast([P, TT, n])

                def row8(x):
                    return x.unsqueeze(1).to_broadcast([P, TT, 8])

                def first_max(values, best, hot):
                    v(red(best, values, AX.X, ALU.max))
                    v(tt(cand[:], values, wide(best), ALU.is_equal))
                    v(tt(cand[:], cand[:], row8(pri[:]), ALU.mult))
                    v(red(m8[:], cand[:], AX.X, ALU.max))
                    v(tt(hot, cand[:], wide(m8[:]), ALU.is_equal))

                groups = lg[:, :, 0:GROUPS]
                first_max(groups, pg[:], ohg[:])
                v(tt(gexp[:], groups, wide(pg[:]), ALU.subtract))
                dve.sem_inc(soft_in, 1)
                el = lg[:, :, GROUPS:].rearrange("p t (g e) -> p t g e", g=GROUPS)
                bg = big[:].rearrange("p t (g e) -> p t g e", g=GROUPS)
                for t in range(TT):
                    v.hold(tt(bg[:, t], el[:, t], ohg[:, t].unsqueeze(2).to_broadcast([P, GROUPS, 8]), ALU.mult))
                v.wait()
                v(red(ein[:], bg.rearrange("p t g e -> p t e g"), AX.X, ALU.add))
                first_max(ein[:], top[:, 0], oh[:, 0])
                v(stt(out=ein[:], in0=oh[:, 0], scalar=-BIG, in1=ein[:], op0=ALU.mult, op1=ALU.add))
                first_max(ein[:], top[:, 1], oh[:, 1])
                v(tt(ed[:], top[:, 1], top[:, 0], ALU.subtract))
                dve.sem_inc(diff_in, 1)
                dve.wait_ge(soft_out, 1)
                v(red(pg[:], gexp[:], AX.X, ALU.add))
                v(V.reciprocal(pg[:], pg[:]))
                dve.wait_ge(diff_out, 1)
                v(ts(m8[:], ed[:], 1.0, None, ALU.add))
                v(V.reciprocal(m8[:], m8[:]))
                v(tt(gate[:, :, 0], pg[:], m8[:], ALU.mult))
                v(tt(gate[:, :, 1], gate[:, :, 0], ed[:], ALU.mult))
                v(tt(ohg[:], ohg[:], wide(valid[:]), ALU.mult))
                for c in range(2):
                    for t in range(TT):
                        v.hold(tt(chosen[:, c, t].rearrange("p (g e) -> p g e", g=GROUPS),
                                  ohg[:, t].unsqueeze(2).to_broadcast([P, GROUPS, 8]),
                                  oh[:, c, t].unsqueeze(1).to_broadcast([P, GROUPS, 8]), ALU.mult))
                v.wait()
                v(tt(both[:], chosen[:, 0], chosen[:, 1], ALU.add))
                dve.sem_inc(picked, 1)
                dve.wait_ge(totals_done, 1)
                cut = lambda x, c: x.rearrange("p t e -> p (t e)")[:, ROUTE_CUT * c:ROUTE_CUT * c + ROUTE_CUT]
                for c in range(2):
                    v.hold(V.tensor_copy(cut(big[:], c), rk_ps[:, c, 0:ROUTE_CUT]))
                v(V.memset(base[:, 0], 0.0))
                dve.sem_inc(totals_out, 1)
                for t in range(TT):
                    v(tt(base[:, t + 1], base[:, t], big[:, t], ALU.add))
                dve.wait_ge(ranked, 1)
                for c in range(2):
                    v.hold(tt(cut(rank[:], c), rk_ps[:, c, 0:ROUTE_CUT], cut(base[:, 0:TT], c), ALU.add))
                v.wait()
                v(tt(over[:], base[:, TT].unsqueeze(2).to_broadcast([P, EXPERTS, PER_EXPERT_SPILL]),
                     steps[:].unsqueeze(1).to_broadcast([P, EXPERTS, PER_EXPERT_SPILL]), ALU.is_gt))
                v(red(nspill[:], over[:], AX.X, ALU.add))
                v(V.tensor_tensor_scan(send[:], ones_row[:], nspill[:], 0.0, ALU.mult, ALU.add))
                v(tt(jump[:], send[:], nspill[:], ALU.subtract))
                v(ts(jump[:], jump[:], float(CAP), float(MAIN_SLOTS - CAP), ALU.mult, ALU.add))
                v(tt(jump[:], jump[:], first[:], ALU.subtract))
                v(ts(big[:], rank[:], float(CAP), None, ALU.is_ge))
                for x, op in ((jump, ALU.mult), (first, ALU.add)):
                    v(tt(big[:], big[:], x[:].unsqueeze(1).to_broadcast([P, TT, EXPERTS]), op))
                v(tt(rank[:], rank[:], big[:], ALU.add))
                for c in range(2):
                    v(tt(big[:], rank[:], chosen[:, c], ALU.mult))
                    v(red(slot_f[:, :, c], big[:], AX.X, ALU.add))
                v(V.tensor_copy(dest[:], slot_f[:]))
                dve.sem_inc(slots_ready, 1)
                v(tt(owner[:], send[0:1].unsqueeze(1).to_broadcast([1, SPILL_BLOCKS, EXPERTS]),
                     blocks[0:1].unsqueeze(2).to_broadcast([1, SPILL_BLOCKS, EXPERTS]), ALU.is_le))
                v(red(owners[:, 0:SPILL_BLOCKS], owner[:], AX.X, ALU.add))
                v(ts(owners[:, 0:SPILL_BLOCKS], owners[:, 0:SPILL_BLOCKS], float(EXPERTS - 1), None, ALU.min))
                v(V.tensor_copy(owners[:, SPILL_BLOCKS:], send[0:1, EXPERTS - 1:]))
                v(V.tensor_copy(spill[:], owners[:]))
                dve.wait_ge(queue_loaded, 16)
                v(ts(queue[:, 0], queue[:, 1], 1, None, ALU.arith_shift_right))


def expert_loads(nc, D, layer, wgu, wd):
    wg_d, wu_d, wd_d = D["w_gate_2"][layer], D["w_up_2"][layer], D["w_down_2"][layer]

    def gate_up(sp, b, loaded, pair):
        for n, e in enumerate(pair):
            for c, src in enumerate((wg_d, wu_d)):
                sp.dma_start(wgu[:, b, n, c], src[bass.ds(e, 1)].rearrange("a (p k) f -> (a p) k f", k=KT)
                             ).then_inc(loaded, 16)

    def down(sp, b, loaded, pair):
        for n, e in enumerate(pair):
            sp.dma_start(wd[:, b, n], wd_d[bass.ds(e, 1)].rearrange("a (p k) f -> (a p) k f", k=2)
                         ).then_inc(loaded, 16)

    return gate_up, down


def experts(nc, D, layer, queue, spill, wgu, wd, gu_loaded, d_loaded):
    gate_up_loads, down_loads = expert_loads(nc, D, layer, wgu, wd)
    with Phase(nc, "ex") as ph:
        ib = ph.sb("ib", [P, 2, 2], I32)
        xe = ph.sb("xe", [P, 2, DM])
        xT = ph.sb("xT", [P, 2, KT, P])
        sg = ph.sb("sg", [P, 2, DE])
        hs = ph.sb("hs", [P, 2, DE])
        hT = ph.sb("hT", [P, 2, 2, P])
        ysb = ph.sb("ysb", [P, 2, DM])
        ident = ph.sb("ident", [P, P])
        x_ps = ph.ps("x_ps", [P, 2, 512])
        h_ps = ph.ps("h_ps", [P, 2, 512])
        ht_ps = ph.ps("ht_ps", [P, 2, 512])
        y_ps = ph.ps("y_ps", [P, 2, 512])
        id_done = ph.sem("id_done")
        xe_clear = ph.sem("xe_clear")
        names = ["in_ready", "out_ready", "x_loaded", "x_turned", "xT_out",
                 "h_done", "silu_done", "h_out", "h_turned", "hT_out", "y_done", "y_out", "y_stored"]
        S = [{n: ph.sem(f"{n}{b}") for n in names} for b in range(3)]
        for b in range(2):
            S[b]["gu_loaded"], S[b]["d_loaded"] = gu_loaded[b], d_loaded[b]
        for n in ("gu_loaded", "d_loaded", "w_used", "x_used", "seen"):
            S[2][n] = ph.sem(f"{n}2")
        hn_dram, y_rows = D["hn"], D["ys"].rearrange("t (c d) -> (t c) d", c=2)

        def gather(pool, b, s, pair):
            pool.sem_inc(s["in_ready"], 1)
            nc.gpsimd.tensor_copy(ib[:, b, 0:1], queue[:, 0, bass.ds(pair, 1)]).then_inc(s["in_ready"], 1)
            pool.wait_ge(s["in_ready"], 2)
            nc.gpsimd.indirect_dma_start(xe[:, b], None, hn_dram[:, :], bass.IndirectOffsetOnAxis(ap=ib[:, b, 0:1], axis=0),
                                         bounds_check=T - 1, oob_is_err=False).then_inc(s["x_loaded"], 16)
            pool.sem_clear(s["in_ready"])

        def scatter(pool, b, s, pair):
            pool.sem_inc(s["out_ready"], 1)
            nc.gpsimd.tensor_copy(ib[:, b, 1:2], queue[:, 1, bass.ds(pair, 1)]).then_inc(s["out_ready"], 1)
            pool.wait_ge(s["out_ready"], 2)
            nc.gpsimd.indirect_dma_start(y_rows[:, :], bass.IndirectOffsetOnAxis(ap=ib[:, b, 1:2], axis=0), ysb[:, b], None,
                                         bounds_check=2 * T - 1, oob_is_err=False).then_inc(s["y_stored"], 16)
            pool.sem_clear(s["out_ready"])

        def products(pe, b, s, count):
            pe.wait_ge(s["x_loaded"], 16 * count)
            for k in range(KT):
                last = nc.tensor.transpose(x_ps[:, k // 4, P * (k % 4):P * (k % 4) + P], xe[:, b, k::KT], ident[:])
            last.then_inc(s["x_turned"], 1)
            pe.wait_ge(s["xT_out"], 2 * count)
            pe.wait_ge(s["gu_loaded"], 64 * count)
            for k in range(KT):
                for n in range(2):
                    half = slice(CAP * n, CAP * n + CAP)
                    last = nc.tensor.matmul(h_ps[half, b].rearrange("p (a b) -> p a b", a=2), xT[:, b, k, half],
                                            wgu[:, b, n, :, k], start=(k == 0), stop=(k == KT - 1))
            last.then_inc(s["h_done"], 1)
            pe.wait_ge(s["h_out"], count)
            for k in range(2):
                last = nc.tensor.transpose(ht_ps[:, b, P * k:P * k + P], hs[:, b, k::2], ident[:])
            last.then_inc(s["h_turned"], 1)
            pe.wait_ge(s["hT_out"], count)
            pe.wait_ge(s["d_loaded"], 32 * count)
            for c in range(2):
                for k in range(2):
                    for n in range(2):
                        half = slice(CAP * n, CAP * n + CAP)
                        last = nc.tensor.matmul(y_ps[half, c], hT[:, b, k, half], wd[:, b, n, k, 512 * c:512 * c + 512],
                                                start=(k == 0), stop=(k == 1))
            last.then_inc(s["y_done"], 1)
            pe.wait_ge(s["y_out"], 2 * count)

        def scalar_part(act, b, s, count, stored):
            act.wait_ge(s["x_turned"], count)
            nc.scalar.copy(xT[:, b, 0:4].rearrange("p k q -> p (k q)"), x_ps[:, 0]).then_inc(s["xT_out"], 1)
            act.wait_ge(s["h_done"], count)
            nc.scalar.activation(sg[:, b], h_ps[:, b, 0:DE], ACT.Silu).then_inc(s["silu_done"], 1)
            act.wait_ge(s["h_turned"], count)
            nc.scalar.copy(hT[:, b].rearrange("p k q -> p (k q)"), ht_ps[:, b, 0:2 * P]).then_inc(s["hT_out"], 1)
            stored()
            act.wait_ge(s["y_done"], count)
            nc.scalar.copy(ysb[:, b, 0:512], y_ps[:, 0]).then_inc(s["y_out"], 1)

        def vector_part(dve, b, s, count, stored):
            dve.wait_ge(s["x_turned"], count)
            nc.vector.tensor_copy(xT[:, b, 4:8].rearrange("p k q -> p (k q)"), x_ps[:, 1]).then_inc(s["xT_out"], 1)
            dve.wait_ge(s["silu_done"], count)
            nc.vector.tensor_tensor(hs[:, b], sg[:, b], h_ps[:, b, DE:], ALU.mult).then_inc(s["h_out"], 1)
            stored()
            dve.wait_ge(s["y_done"], count)
            nc.vector.tensor_copy(ysb[:, b, 512:], y_ps[:, 1]).then_inc(s["y_out"], 1)

        MAIN = PAIRS_M // 2
        with nc.Block() as block:

            @block.sync
            def _(sp):
                with sp.Fori(0, MAIN - 1) as i:
                    for b in range(2):
                        s = S[b]
                        pair = [4 * (i + 1) + 2 * b, 4 * (i + 1) + 2 * b + 1]
                        sp.wait_ge(s["h_done"], i + 1)
                        gate_up_loads(sp, b, s["gu_loaded"], pair)
                        sp.wait_ge(s["y_done"], i + 1)
                        down_loads(sp, b, s["d_loaded"], pair)

            @block.gpsimd
            def _(pool):
                make_identity(nc, pool, ident, id_done)
                pool.wait_ge(xe_clear, 1)
                for b in range(2):
                    gather(pool, b, S[b], b)
                with pool.Fori(0, MAIN - 1) as i:
                    for b in range(2):
                        s = S[b]
                        pool.wait_ge(s["x_turned"], i + 1)
                        gather(pool, b, s, 2 * (i + 1) + b)
                        pool.wait_ge(s["y_out"], 2 * i + 2)
                        scatter(pool, b, s, 2 * i + b)
                for b in range(2):
                    pool.wait_ge(S[b]["y_out"], 2 * MAIN)
                    scatter(pool, b, S[b], PAIRS_M - 2 + b)
                for b in range(2):
                    pool.wait_ge(S[b]["y_stored"], 16 * MAIN)

            @block.tensor
            def _(pe):
                pe.wait_ge(id_done, 2)
                with pe.Fori(0, MAIN) as i:
                    for b in range(2):
                        products(pe, b, S[b], i + 1)

            @block.scalar
            def _(act):
                for b in range(2):
                    scalar_part(act, b, S[b], 1, lambda: None)
                with act.Fori(1, MAIN) as i:
                    for b in range(2):
                        scalar_part(act, b, S[b], i + 1, lambda: act.wait_ge(S[b]["y_stored"], 16 * i))

            @block.vector
            def _(dve):
                nc.vector.memset(xe[:], 0.0).then_inc(xe_clear, 1)
                for b in range(2):
                    vector_part(dve, b, S[b], 1, lambda: None)
                with dve.Fori(1, MAIN) as i:
                    for b in range(2):
                        vector_part(dve, b, S[b], i + 1, lambda: dve.wait_ge(S[b]["y_stored"], 16 * i))

        s = S[2]
        with nc.Block() as block:

            def spilled(eng):
                return eng.value_load(spill[0:1, SPILL_BLOCKS:], min_val=0, max_val=SPILL_BLOCKS)

            @block.sync
            def _(sp):
                total = spilled(sp)
                with sp.Fori(0, SPILL_PAIRS) as i:
                    with sp.If(2 * i < total):
                        sp.wait_ge(s["w_used"], i + 1)
                        pair = [sp.value_load(spill[0:1, bass.ds(2 * i + n, 1)], min_val=0, max_val=EXPERTS - 1)
                                for n in range(2)]
                        gate_up_loads(sp, 0, s["gu_loaded"], pair)
                        down_loads(sp, 0, s["d_loaded"], pair)

            @block.gpsimd
            def _(pool):
                total = spilled(pool)
                with pool.Fori(0, SPILL_PAIRS) as i:
                    with pool.If(2 * i < total):
                        pool.wait_ge(s["x_used"], i + 1)
                        gather(pool, 0, s, PAIRS_M + i)
                        pool.wait_ge(s["y_out"], 2 * i + 2)
                        scatter(pool, 0, s, PAIRS_M + i)
                        pool.wait_ge(s["y_stored"], 16 * i + 16)
                        pool.sem_inc(s["seen"], 1)

            @block.tensor
            def _(pe):
                for n in ("w_used", "x_used", "seen"):
                    pe.sem_inc(s[n], 1)
                total = spilled(pe)
                with pe.Fori(0, SPILL_PAIRS) as i:
                    with pe.If(2 * i < total):
                        products(pe, 0, s, i + 1)
                        for n in ("w_used", "x_used"):
                            pe.sem_inc(s[n], 1)

            @block.scalar
            def _(act):
                total = spilled(act)
                with act.Fori(0, SPILL_PAIRS) as i:
                    with act.If(2 * i < total):
                        scalar_part(act, 0, s, i + 1, lambda: act.wait_ge(s["seen"], i + 1))

            @block.vector
            def _(dve):
                total = spilled(dve)
                with dve.Fori(0, SPILL_PAIRS) as i:
                    with dve.If(2 * i < total):
                        vector_part(dve, 0, s, i + 1, lambda: dve.wait_ge(s["seen"], i + 1))


def gathered_sum(nc, v, y, gate, h, out, t):
    v(nc.vector.scalar_tensor_tensor(out=out, in0=y[:, 0:DM], scalar=gate[:, t, 0:1], in1=h, op0=ALU.mult, op1=ALU.add))
    v(nc.vector.scalar_tensor_tensor(out=out, in0=y[:, DM:], scalar=gate[:, t, 1:2], in1=out, op0=ALU.mult, op1=ALU.add))


def combine_for_latents(nc, D, gate, h_in, h_out, hq, hk):
    with Phase(nc, "cl") as ph:
        NBUF = 3
        hb = ph.sb("hb", [P, NBUF, DM])
        yb = ph.sb("yb", [P, NBUF, 2 * DM])
        ho = ph.sb("ho", [P, 2, DM])
        yb_clear, v_own, made = ph.sem("yb_clear"), ph.sem("v_own"), ph.sem("made")
        loaded = [ph.sem(f"h{n}_loaded") for n in range(NBUF)]
        stored = [ph.sem(f"h{n}_stored") for n in range(2)]
        norm = NormTurn(nc, ph, [hq, hk], [D["norm_mix_g_t"][1], D["kv_norm_g_t"]], [(P * t, P) for t in range(TT)],
                        lambda n: ho[:, n % 2], made)
        with nc.Block() as block:

            @block.sync
            def _(sp):
                norm.load(sp)
                sp.wait_ge(yb_clear, 1)
                for t in range(TT):
                    if t >= NBUF:
                        sp.wait_ge(made, t - NBUF + 1)
                    b, r = t % NBUF, rows_of(t)
                    sp.dma_start(hb[:, b], h_in[P * t:P * t + P]).then_inc(loaded[b], 16)
                    sp.dma_start(yb[0:r, b], D["ys"][P * t:P * t + r]).then_inc(loaded[b], 16)

            @block.gpsimd
            def _(pool):
                norm.constants(pool)
                for t in range(TT):
                    pool.wait_ge(made, t + 1)
                    pool.dma_start(h_out[P * t:P * t + P], ho[:, t % 2]).then_inc(stored[t % 2], 16)
                for b in range(2):
                    pool.wait_ge(stored[b], 16 * ((TT + 1 - b) // 2))

            @block.tensor
            def _(pe):
                for t in range(TT):
                    norm.turn(pe, t)

            @block.scalar
            def _(act):
                for t in range(TT):
                    norm.square(act, t)

            @block.vector
            def _(dve):
                v = Chain(dve, v_own)
                nc.vector.memset(yb[:], 0.0).then_inc(yb_clear, 1)
                for t in range(TT):
                    dve.wait_ge(loaded[t % NBUF], 32 * (t // NBUF + 1))
                    if t >= 2:
                        dve.wait_ge(norm.scaled, t - 1)
                        dve.wait_ge(stored[t % 2], 16 * (t // 2))
                    gathered_sum(nc, v, yb[:, t % NBUF], gate, hb[:, t % NBUF], ho[:, t % 2], t)
                    dve.sem_inc(made, 1)
                    if t >= 1:
                        norm.scale(dve, v, t - 1)
                    if t >= 2:
                        norm.out(dve, t - 2)
                norm.out(dve, TT - 2)
                norm.scale(dve, v, TT - 1)
                norm.out(dve, TT - 1)


def combine_out(nc, D, gate, h_in):
    with Phase(nc, "co") as ph:
        NBUF = 3
        hb = ph.sb("hb", [P, NBUF, DM])
        yb = ph.sb("yb", [P, NBUF, 2 * DM])
        ho = ph.sb("ho", [P, 2, DM])
        gb = ph.sb("gb", [P, DM])
        sq = ph.sb("sq", [P, DM], mybir.dt.bfloat16)
        ss, rt, rs = (ph.sb(n, [P, 2]) for n in ("ss", "rt", "rs"))
        eps = ph.sb("eps", [P, 1])
        g_loaded, cleared, made, squared, rooted, scaled, v_own = (
            ph.sem(n) for n in ("g_loaded", "cleared", "made", "squared", "rooted", "scaled", "v_own"))
        loaded = [ph.sem(f"h{n}_loaded") for n in range(NBUF)]
        stored = [ph.sem(f"o{n}_stored") for n in range(2)]
        with nc.Block() as block:

            @block.sync
            def _(sp):
                sp.dma_start(gb[:], D["final_norm_g_2"].partition_broadcast(P)).then_inc(g_loaded, 16)
                sp.wait_ge(cleared, 2)
                for t in range(TT):
                    if t >= NBUF:
                        sp.wait_ge(made, t - NBUF + 1)
                    b, r = t % NBUF, rows_of(t)
                    sp.dma_start(hb[:, b], h_in[P * t:P * t + P]).then_inc(loaded[b], 16)
                    sp.dma_start(yb[0:r, b], D["ys"][P * t:P * t + r]).then_inc(loaded[b], 16)

            @block.gpsimd
            def _(pool):
                for t in range(TT):
                    pool.wait_ge(scaled, t + 1)
                    skip = 0 if t else META
                    pool.dma_start(D["out"][P * t - META + skip:min(P * t - META + P, SEQ)], ho[skip:rows_of(t), t % 2]
                                   ).then_inc(stored[t % 2], 16)
                for b in range(2):
                    pool.wait_ge(stored[b], 16 * ((TT + 1 - b) // 2))

            @block.scalar
            def _(act):
                act.wait_ge(cleared, 2)
                for t in range(TT):
                    b = t % 2
                    act.wait_ge(made, t + 1)
                    if t >= 2:
                        act.wait_ge(scaled, t - 1)
                    nc.scalar.activation(sq[:], ho[:, b], ACT.Square, accum_out=ss[:, b:b + 1]).then_inc(squared, 1)
                    act.wait_ge(squared, t + 1)
                    nc.scalar.activation(rt[:, b:b + 1], ss[:, b:b + 1], ACT.Sqrt, scale=1.0 / DM,
                                         bias=eps[:]).then_inc(rooted, 1)

            @block.vector
            def _(dve):
                v = Chain(dve, v_own)
                nc.vector.memset(yb[:], 0.0).then_inc(cleared, 1)
                nc.vector.memset(eps[:], NORM_EPS).then_inc(cleared, 1)
                dve.wait_ge(g_loaded, 16)

                def scale(t):
                    b = t % 2
                    dve.wait_ge(rooted, t + 1)
                    v(nc.vector.reciprocal(rs[:, b:b + 1], rt[:, b:b + 1]))
                    v(nc.vector.scalar_tensor_tensor(out=ho[:, b], in0=ho[:, b], scalar=rs[:, b:b + 1], in1=gb[:],
                                                     op0=ALU.mult, op1=ALU.mult))
                    dve.sem_inc(scaled, 1)

                for t in range(TT):
                    dve.wait_ge(loaded[t % NBUF], 32 * (t // NBUF + 1))
                    if t >= 2:
                        dve.wait_ge(stored[t % 2], 16 * (t // 2))
                    gathered_sum(nc, v, yb[:, t % NBUF], gate, hb[:, t % NBUF], ho[:, t % 2], t)
                    dve.sem_inc(made, 1)
                    if t >= 1:
                        scale(t - 1)
                scale(TT - 1)


def scratch(nc, D):
    for name, shape, dt in (("h0", (TP, DM), F32), ("h1", (TP, DM), F32), ("h2", (TP, DM), F32), ("h3", (TP, DM), F32),
                            ("hn", (TP, DM), F32), ("ys", (T, 2 * DM), F32), ("table", (SLOTS, 1), I32)):
        if name not in D:
            D[name] = nc.dram_tensor(f"s_{name}", shape, dt, kind="Internal").ap()


def moe(nc, D, layer, lg, gate, wgu):
    with Phase(nc, "mo") as ph:
        wd = ph.sb("wd", [P, 2, 2, 2, DM])
        queue = ph.sb("queue", [P, 2, QUEUE_ROWS], I32)
        spill = ph.sb("spill", [1, SPILL_BLOCKS + 1], I32)
        gu_loaded = [ph.sem(f"gu{b}_loaded") for b in range(2)]
        d_loaded = [ph.sem(f"d{b}_loaded") for b in range(2)]
        gate_up, down = expert_loads(nc, D, layer, wgu, wd)

        def start_weights(sp):
            for b in range(2):
                gate_up(sp, b, gu_loaded[b], [2 * b, 2 * b + 1])
                down(sp, b, d_loaded[b], [2 * b, 2 * b + 1])

        route(nc, D, lg, gate, queue, spill, start_weights)
        experts(nc, D, layer, queue, spill, wgu, wd, gu_loaded, d_loaded)


def program_parts(nc, D, arena, gate):
    def part(first_tile, *shape):
        n = int(np.prod(shape))
        flat = arena[:, SEQ * first_tile:SEQ * first_tile + n]
        names = "abcde"[:len(shape)]
        return flat.rearrange(f"p ({' '.join(names)}) -> p {' '.join(names)}", **dict(zip(names, shape)))

    proj = part(0, PROJ_TILES, SEQ)
    zT, hnT = part(0, KT, TP), part(9, KT, TP)
    wgu = part(0, 2, 2, 2, KT, DE)
    lg = part(PROJ_TILES - 1, TT, LG)
    hq, hk = part(0, KT, TP), part(9, KT, TP)
    oT = part(0, HEADS, TP)
    first(nc, D, proj)
    first_out(nc, D, proj, hnT)
    conv_mixer(nc, D, hnT, zT)
    back_and_route(nc, D, 0, zT, D["conv_w_out_2"], D["h0"], D["h1"], lg)
    moe(nc, D, 0, lg, gate, wgu)
    with Phase(nc, "lt") as ph:
        cq = ph.sb("cq", [P, QR // P, TP])
        ckv = ph.sb("ckv", [P, KVR // P, TP])
        kr = ph.sb("kr", [P, 2, T])
        combine_for_latents(nc, D, gate, D["h1"], D["h2"], hq, hk)
        latents(nc, D, hq, hk, cq, ckv, kr)
        heads(nc, D, cq, ckv, kr, oT)
    back_and_route(nc, D, 1, oT, D["w_o_2"], D["h2"], D["h3"], lg)
    moe(nc, D, 1, lg, gate, wgu)
    combine_out(nc, D, gate, D["h3"])


def program(nc, D):
    Phase.seen.clear()
    scratch(nc, D)
    with Phase(nc, "all") as ph:
        arena = ph.sb("arena", [P, PROJ_TILES * SEQ])
        gate = ph.sb("gate", [P, TT, 2])
        program_parts(nc, D, arena, gate)


def by_partition(a, *order):
    return np.ascontiguousarray(a.reshape(-1, P, *a.shape[1:]).swapaxes(0, 1))


def lay_out(inputs):
    a = {k: np.ascontiguousarray(np.asarray(v)) for k, v in inputs.items()}
    o = {n: a[n] for n in ("meta_tokens_2", "norm_ffn_g_2", "w_gate_2", "w_up_2", "w_down_2", "final_norm_g_2")}
    for n in ("x", "attn_sinks", "lru_wa", "lru_wx", "rwkv_w2", "rwkv_a2", "w_out", "ln_g", "ln_b", "conv_w_out_2", "w_o_2"):
        o[n] = a[n][0]
    o["xT"] = by_partition(a["x"][0].T)
    w = a["w_in"][0]
    q, k, v, ga, xb, gb, c, gc = np.split(w, np.cumsum([512, 128, 128, 512, 256, 256, 832, 256])[:-1], axis=1)
    swapped = np.concatenate([k[:, HALF:], k[:, :HALF]], 1)
    tiles = np.concatenate([ga, gb, gc, q, k, swapped, xb, c, np.zeros((DM, HALF + P), w.dtype)], 1)
    o["w_in_t"] = np.ascontiguousarray(tiles.reshape(KT, P, PROJ_TILES + 1, P).transpose(2, 1, 0, 3))
    o["w_v_t"] = by_partition(v)

    def vectors(rows):
        return np.ascontiguousarray(np.stack(rows).reshape(-1, 2, P).transpose(2, 1, 0))

    o["lru_vec"] = vectors([*a["conv_w"][0], a["conv_b"][0], a["lru_ba"][0], a["lru_bx"][0], a["lru_lambda"][0]])
    mu = a["rwkv_mu"][0]
    o["rwkv_vec"] = vectors([mu[0:256], mu[256:512], mu[512:768], a["rwkv_w0"][0], a["rwkv_a0"][0], a["rwkv_kk"][0],
                             a["rwkv_ka"][0], a["rwkv_rk"][0].reshape(-1), a["rwkv_gn_w"][0], a["rwkv_gn_b"][0]])
    o["rwkv_mu_lo"] = np.ascontiguousarray(mu[768:].reshape(HALF, 1))
    o["norm_mix_g_t"] = np.stack([by_partition(g) for g in a["norm_mix_g_2"]])
    o["kv_norm_g_t"] = by_partition(a["kv_norm_g_2"])
    o["conv_w_in_t"] = np.ascontiguousarray(a["conv_w_in_2"][0].reshape(KT, P, 3, KT, P).transpose(3, 1, 2, 0, 4))
    o["conv_w_2_t"] = np.ascontiguousarray(a["conv_w_2"][0].reshape(3, KT, P).transpose(2, 1, 0))
    o["w_dq_t"] = by_partition(a["w_dq_2"][0])
    dkv = a["w_dkv_2"]
    o["w_dkv_t"] = by_partition(dkv[:, :KVR])
    rope = dkv[:, KVR:]
    turned = np.concatenate([rope[:, ROPE // 2:], rope[:, :ROPE // 2]], 1)
    o["w_rope_t"] = by_partition(np.stack([np.concatenate([rope, rope], 1), np.concatenate([turned, turned], 1)], 1))
    o["cq_g_t"] = by_partition(a["cq_norm_g_2"][0])
    o["ckv_g_t"] = by_partition(a["ckv_norm_g_2"])
    inv = np.float32(10000.0) ** (-np.arange(0, ROPE, 2, dtype=np.float32) / np.float32(ROPE))
    angle = np.arange(T, dtype=np.float32)[:, None] * inv[None, :]
    cos, sin = np.cos(angle).T, np.sin(angle).T
    o["cos_t"] = np.ascontiguousarray(np.concatenate([cos] * 4, 0))
    o["sin_t"] = np.ascontiguousarray(np.concatenate([-sin, sin] * 2, 0))
    uq = a["w_uq_2"][0].reshape(QR // P, P, HEADS // 2, 2, NOPE + ROPE)
    nope, rq = uq[..., :NOPE], uq[..., NOPE:]
    rs = np.concatenate([rq[..., ROPE // 2:], rq[..., :ROPE // 2]], -1)
    o["w_uq_t"] = np.ascontiguousarray(np.stack(
        [nope[:, :, :, 0], nope[:, :, :, 1], rq.reshape(QR // P, P, HEADS // 2, P), rs.reshape(QR // P, P, HEADS // 2, P)],
        3).transpose(2, 1, 0, 3, 4))
    ukv = a["w_ukv_2"].reshape(KVR // P, P, HEADS // 2, 2, 2, P)
    o["w_ukv_t"] = np.ascontiguousarray(ukv.transpose(2, 1, 0, 4, 3, 5).reshape(HEADS // 2, P, KVR // P, 4, P))
    o["w_route_t"] = np.stack([by_partition(np.concatenate([g, e], 1)) for g, e in zip(a["w_grp_2"], a["w_exp_2"])])
    return o


def kernel(**inputs):
    import concourse.bacc as bacc
    from concourse.bass_utils import run_bass_kernel_spmd

    nc = bacc.Bacc("TRN2", target_bir_lowering=False, num_devices=1)
    arrays = {f"in_{n}": x for n, x in lay_out(inputs).items()}
    D = {n[3:]: nc.dram_tensor(n, x.shape, mybir.dt.from_np(x.dtype), kind="ExternalInput").ap() for n, x in arrays.items()}
    D["out"] = nc.dram_tensor("out_0", (SEQ, DM), F32, kind="ExternalOutput").ap()
    program(nc, D)
    r = run_bass_kernel_spmd(nc, [arrays], core_ids=[0])
    return r.results[0]["out_0"].reshape(1, SEQ, DM)
```

```python
import numpy as np
import concourse.bass as bass
from concourse import mybir
from contextlib import ExitStack

F32 = mybir.dt.float32
I32 = mybir.dt.int32
U32 = mybir.dt.uint32
ALU = mybir.AluOpType
ACT = mybir.ActivationFunctionType
AX = mybir.AxisListType
P = 128
HALF = 64

SEQ = 1024
DM = 1024
KT = DM // P
NB = SEQ // P
PAIRS = 4
KV = 2
G_T, Q_T, K_T, KS_T, XB_T, R_T, CK_T, CV_T, WA_T = 0, 8, 12, 13, 14, 16, 18, 20, 22
PROJ_TILES = 23
GATE_TILES = 8
HEAD_SCALE = 64.0 ** -0.5
MASKED = -1.0e30
CHUNK = 64
NCH = SEQ // CHUNK
LN_EPS = 1e-5
GN_EPS = 64e-5
ALPHA = 2.0 ** 0.25
DECAY_HALF = float(np.exp(-0.5))
RANK = 32


class Chain:

    def __init__(self, eng, sem):
        self.eng, self.sem, self.n = eng, sem, 0

    def __call__(self, ins):
        self.n += 1
        ins.then_inc(self.sem, 1)
        self.eng.wait_ge(self.sem, self.n)

    def hold(self, ins):
        self.n += 1
        ins.then_inc(self.sem, 1)

    def wait(self):
        self.eng.wait_ge(self.sem, self.n)

    def restart(self):
        if self.n:
            self.eng.sem_clear(self.sem)
        self.n = 0


class Phase:

    seen = {}

    def __init__(self, nc, name):
        again = Phase.seen[name] = Phase.seen.get(name, -1) + 1
        self.nc, self.name, self.ctx, self.sems = nc, f"{name}{again}", ExitStack(), []

    def __enter__(self):
        return self

    def __exit__(self, kind, *rest):
        self.ctx.close()
        if kind is None and self.sems:
            self.nc.clear_and_free_semaphores(self.sems)
            self.nc.all_engine_barrier()

    def sb(self, name, shape, dt=F32):
        return self.ctx.enter_context(self.nc.sbuf_tensor(f"{self.name}__{name}", shape, dt))

    def ps(self, name, shape, dt=F32):
        return self.ctx.enter_context(self.nc.psum_tensor(f"{self.name}__{name}", shape, dt))

    def sem(self, name):
        self.sems.append(self.nc.alloc_semaphore(f"{self.name}__{name}"))
        return self.sems[-1]


def col(v):
    return v.rearrange("(p a) -> p a", a=1)


TL = 2
ORDER = [XB_T, XB_T + 1, WA_T, R_T, R_T + 1, CK_T, CK_T + 1, CV_T, CV_T + 1, G_T + 4, G_T + 5,
         Q_T, Q_T + 1, Q_T + 2, Q_T + 3, K_T, KS_T, G_T, G_T + 1, G_T + 2, G_T + 3, G_T + 6, G_T + 7]
GATE_AT = ORDER.index(G_T + 5) + 1


def front(nc, D, proj, vpad, kkb, bb, dlt, wc, vec):
    with Phase(nc, "fr") as ph:
        xT = ph.sb("xT", [P, KT, SEQ])
        wbuf = ph.sb("w", [P, 2, KT, P])
        wv = ph.sb("wv", [P, KT, P])
        cum = ph.sb("cum", [P, TL, SEQ])
        aa = ph.sb("aa", [P, TL, SEQ])
        lw = ph.sb("lw", [P, TL, SEQ])
        keep = ph.sb("keep", [P, SEQ], mybir.dt.bfloat16)
        ones2 = ph.sb("ones2", [P, P])
        w2a2 = ph.sb("w2a2", [HALF, TL * P])
        muwa = ph.sb("muwa", [HALF, 1])
        eps = ph.sb("eps", [P, 1])
        lvec = ph.sb("lvec", [P, TL, 8])
        sp8 = ph.sb("sp8", [P, TL, 2])
        wa = ph.sb("wa", [P, TL, P])
        wx = ph.sb("wx", [P, TL, P])
        acc = ph.ps("acc", [P, 2, 2, 512])
        aux = ph.ps("aux", [P, TL, 2, 512])
        xc, rg, ig, uv, av = cum, aa, lw, dlt, proj[:, XB_T:XB_T + TL]
        lo = proj[0:HALF, WA_T]
        rr, kx, vv = (proj[:, m:m + TL] for m in (R_T, CK_T, CV_T))
        wv_loaded, loaded, vec_loaded = ph.sem("wv_loaded"), ph.sem("loaded"), ph.sem("vec_loaded")
        x_loaded = [ph.sem(f"x{k}_loaded") for k in range(KT)]
        w_loaded = [ph.sem("w0_loaded"), ph.sem("w1_loaded")]
        (done, evac, aux_done, aux_free, v_own, a_own, zeroed, conv_done, low_ready, tanh_low, sig_done, decay_done,
         tanh_done, root_in, root_done, logs_done, sq_ready, norm_done, cum_done, bonus_in, exp_done) = (ph.sem(n) for n in (
             "done", "evac", "aux_done", "aux_free", "v_own", "a_own", "zeroed", "conv_done", "low_ready", "tanh_low",
             "sig_done", "decay_done", "tanh_done", "root_in", "root_done", "logs_done", "sq_ready", "norm_done",
             "cum_done", "bonus_in", "exp_done"))
        w_dram = D["w_in_t"]

        def flat(x):
            return x.rearrange("p a b -> p (a b)")

        with nc.Block() as block:

            @block.sync
            def _(sp):
                sp.dma_start(wbuf[:, 0], w_dram[ORDER[0]]).then_inc(w_loaded[0], 16)
                for k in range(KT):
                    sp.dma_start(xT[:, k], D["xT"][:, k]).then_inc(x_loaded[k], 16)
                sp.dma_start(wbuf[:, 1], w_dram[ORDER[1]]).then_inc(w_loaded[1], 16)
                for m in range(2, PROJ_TILES):
                    sp.wait_ge(done, m - 1)
                    sp.dma_start(wbuf[:, m % 2], w_dram[ORDER[m]]).then_inc(w_loaded[m % 2], 16)

            @block.gpsimd
            def _(pool):
                pool.dma_start(lvec[:], D["lru_vec"]).then_inc(vec_loaded, 16)
                pool.dma_start(vec[:], D["rwkv_vec"]).then_inc(loaded, 16)
                pool.dma_start(muwa[:], D["rwkv_mu_lo"]).then_inc(loaded, 16)
                pool.dma_start(w2a2[0:RANK], D["rwkv_w2"]).then_inc(loaded, 16)
                pool.dma_start(w2a2[RANK:2 * RANK], D["rwkv_a2"]).then_inc(loaded, 16)
                pool.wait_ge(zeroed, 1)
                for w, name in ((wa, "lru_wa"), (wx, "lru_wx")):
                    for n in range(4):
                        h = n % 2
                        pool.dma_start(w[HALF * h:HALF * h + HALF, n // 2, HALF * h:HALF * h + HALF],
                                       D[name][n]).then_inc(loaded, 16)
                pool.dma_start(wv[:], D["w_v_t"]).then_inc(wv_loaded, 16)

            @block.tensor
            def _(pe):
                mm = nc.tensor.matmul
                def small(n, weights, moving, *waits):
                    if n:
                        pe.wait_ge(aux_free, n)
                    for s, value in waits:
                        pe.wait_ge(s, value)
                    for t in range(TL):
                        for c in range(2):
                            last = mm(aux[:, t, c], weights(t), moving(t)[:, 512 * c:512 * c + 512], start=True, stop=True)
                    last.then_inc(aux_done, 1)

                def smalls(m):
                    if m == 4:
                        small(0, lambda t: wa[:, t], lambda t: xc[:, t], (conv_done, 1), (loaded, 16 * 12))
                    if m == 5:
                        small(1, lambda t: wx[:, t], lambda t: xc[:, t])
                    if m == 10:
                        small(2, lambda t: w2a2[0:RANK, P * t:P * t + P], lambda t: lo[0:RANK], (tanh_low, 1))
                    if m == 11:
                        small(3, lambda t: w2a2[RANK:2 * RANK, P * t:P * t + P], lambda t: lo[RANK:2 * RANK])
                    if m == 14:
                        small(4, lambda t: ones2[:], lambda t: dlt[:, t], (sq_ready, 1))
                    if m == 18:
                        small(5, lambda t: ones2[:], lambda t: dlt[:, t], (bonus_in, 1))

                for m in range(PROJ_TILES):
                    b = m % 2
                    pe.wait_ge(w_loaded[b], 16 * (m // 2 + 1))
                    if m >= 2:
                        pe.wait_ge(evac, m - 1)
                    for c in range(2):
                        for k in range(KT):
                            if m == 0 and c == 0:
                                pe.wait_ge(x_loaded[k], 16)
                            last = mm(acc[:, b, c], wbuf[:, b, k], xT[:, k, 512 * c:512 * c + 512],
                                      start=(k == 0), stop=(k == KT - 1))
                    last.then_inc(done, 1)
                    smalls(m)
                pe.wait_ge(wv_loaded, 16)
                pe.wait_ge(aux_free, 6)
                for t in range(NB):
                    for k in range(KT):
                        last = mm(aux[:, 0, t // 4, P * (t % 4):P * (t % 4) + P], xT[:, k, P * t:P * t + P], wv[:, k],
                                  start=(k == 0), stop=(k == KT - 1))
                last.then_inc(aux_done, 1)

            @block.scalar
            def _(act):
                a = Chain(act, a_own)

                def evacuate(m):
                    act.wait_ge(done, m + 1)
                    gate = ORDER[m] < GATE_TILES
                    nc.scalar.activation(proj[:, ORDER[m]], flat(acc[:, m % 2]),
                                         ACT.Silu if gate else ACT.Copy).then_inc(evac, 1)

                act.wait_ge(vec_loaded, 16)
                a(nc.scalar.activation(sp8[:, :, 0:1], lvec[:, :, 7:8], ACT.Exp, scale=-1.0))
                a(nc.scalar.activation(sp8[:, :, 1:2], sp8[:, :, 0:1], ACT.Ln, bias=1.0))
                for m in range(5):
                    evacuate(m)
                for n, (out, bias) in enumerate(((rg, 5), (ig, 6))):
                    act.wait_ge(aux_done, n + 1)
                    for t in range(TL):
                        a.hold(nc.scalar.activation(out[:, t], flat(aux[:, t]), ACT.Sigmoid, bias=lvec[:, t, bias:bias + 1]))
                    a.wait()
                    act.sem_inc(aux_free, 1)
                    evacuate(5 + n)
                act.sem_inc(sig_done, 1)
                act.wait_ge(low_ready, 1)
                a(nc.scalar.activation(lo[0:RANK], lo[0:RANK], ACT.Tanh))
                act.sem_inc(tanh_low, 1)
                act.wait_ge(decay_done, 1)
                a.hold(nc.scalar.activation(av, rg[:], ACT.Exp))
                a.hold(nc.scalar.activation(uv[:], rg[:], ACT.Tanh))
                a.wait()
                act.sem_inc(tanh_done, 1)
                evacuate(7)
                act.wait_ge(root_in, 1)
                a(nc.scalar.activation(uv[:], uv[:], ACT.Sqrt))
                act.sem_inc(root_done, 1)
                for m in range(8, 11):
                    evacuate(m)
                for n, (out, bias) in enumerate(((lw, 3), (aa, 4))):
                    act.wait_ge(logs_done, 1)
                    act.wait_ge(aux_done, n + 3)
                    for t in range(TL):
                        a.hold(nc.scalar.activation(out[:, t], flat(aux[:, t]), ACT.Sigmoid, bias=vec[:, t, bias:bias + 1]))
                    a.wait()
                    act.sem_inc(aux_free, 1)
                    evacuate(11 + n)
                act.sem_inc(sig_done, 1)
                for m in range(13, 15):
                    evacuate(m)
                act.wait_ge(aux_done, 5)
                a(nc.scalar.activation(dlt[:], aux[:].rearrange("p t a b -> p t (a b)"), ACT.Sqrt, bias=eps[:]))
                act.sem_inc(aux_free, 1)
                act.sem_inc(norm_done, 1)
                for m in range(15, 19):
                    evacuate(m)
                act.wait_ge(cum_done, 1)
                act.wait_ge(bonus_in, 1)
                a.hold(nc.scalar.activation(aa[:], cum[:], ACT.Exp))
                a.hold(nc.scalar.activation(lw[:], lw[:], ACT.Exp))
                a.wait()
                a(nc.scalar.activation(cum[:], cum[:], ACT.Exp, scale=-1.0))
                act.sem_inc(exp_done, 1)
                for m in range(19, PROJ_TILES):
                    evacuate(m)

            @block.vector
            def _(dve):
                v = Chain(dve, v_own)
                V = nc.vector
                v.hold(V.memset(wa[:], 0.0))
                v(V.memset(wx[:], 0.0))
                dve.sem_inc(zeroed, 1)
                v.hold(V.memset(eps[:], 1e-12))
                v.hold(V.memset(vpad[:], 0.0))
                v.hold(V.memset(ones2[:], 0.0))
                v(V.memset(keep[:], 1.0))
                v.hold(V.memset(keep[:].rearrange("p (n c) -> p n c", c=CHUNK)[:, :, 0:1], 0.0))
                for h in range(2):
                    v.hold(V.memset(ones2[HALF * h:HALF * h + HALF, HALF * h:HALF * h + HALF], 1.0))
                v.wait()
                dve.wait_ge(vec_loaded, 16)
                for t in range(TL):
                    dve.wait_ge(evac, t + 1)
                    v.hold(V.tensor_scalar(xc[:, t], proj[:, XB_T + t], lvec[:, t, 3:4], lvec[:, t, 4:5], ALU.mult, ALU.add))
                v.wait()
                for back in range(1, 4):
                    for t in range(TL):
                        v.hold(V.scalar_tensor_tensor(out=xc[:, t, back:], in0=proj[:, XB_T + t, 0:SEQ - back],
                                                      scalar=lvec[:, t, 3 - back:4 - back], in1=xc[:, t, back:],
                                                      op0=ALU.mult, op1=ALU.add))
                    v.wait()
                dve.sem_inc(conv_done, 1)

                def shift(x, delta, mu):
                    v.hold(V.tensor_scalar(delta[:, 0:1], x[:, 0:1], -1.0, None, ALU.mult))
                    v(V.tensor_tensor(delta[:, 1:SEQ], x[:, 0:SEQ - 1], x[:, 1:SEQ], ALU.subtract))
                    v(V.scalar_tensor_tensor(out=x, in0=delta, scalar=mu, in1=x, op0=ALU.mult, op1=ALU.add))

                dve.wait_ge(loaded, 16 * 12)
                dve.wait_ge(evac, 3)
                shift(lo, bb[0:HALF, 0], muwa[:, 0:1])
                dve.sem_inc(low_ready, 1)
                for t in range(TL):
                    dve.wait_ge(evac, 4 + t)
                    shift(rr[:, t], bb[:, t], vec[:, t, 0:1])
                dve.wait_ge(sig_done, 1)
                for t in range(TL):
                    v.hold(V.tensor_scalar(rg[:, t], rg[:, t], sp8[:, t, 1:2], -8.0, ALU.mult, ALU.mult))
                v.wait()
                dve.sem_inc(decay_done, 1)
                v(V.tensor_tensor(ig[:], ig[:], xc[:], ALU.mult))
                dve.wait_ge(tanh_done, 1)
                v(V.tensor_tensor(xc[:], av, av, ALU.mult))
                v(V.tensor_scalar(xc[:], xc[:], 1.0, -1.0, ALU.add, ALU.mult))
                v(V.tensor_tensor(uv[:], uv[:], xc[:], ALU.mult))
                dve.sem_inc(root_in, 1)
                for t in range(TL):
                    dve.wait_ge(evac, 6 + t)
                    shift(kx[:, t], bb[:, t], vec[:, t, 1:2])
                dve.wait_ge(root_done, 1)
                v(V.tensor_tensor(uv[:], uv[:], ig[:], ALU.mult))
                dve.sem_inc(logs_done, 1)
                for t in range(TL):
                    v.hold(V.tensor_tensor_scan(xc[:, t], av[:, t], uv[:, t], 0.0, ALU.mult, ALU.add))
                v.wait()
                for t in range(TL):
                    dve.wait_ge(evac, 8 + t)
                    shift(vv[:, t], bb[:, t], vec[:, t, 2:3])
                for t in range(TL):
                    v.hold(V.tensor_scalar(kkb[:, t], kx[:, t], vec[:, t, 5:6], None, ALU.mult))
                v.wait()
                v(V.tensor_tensor(dlt[:], kkb[:], kkb[:], ALU.mult))
                dve.sem_inc(sq_ready, 1)
                dve.wait_ge(evac, GATE_AT)
                v(V.tensor_tensor(proj[:, G_T + 4:G_T + 6], proj[:, G_T + 4:G_T + 6], xc[:], ALU.mult))
                dve.wait_ge(sig_done, 2)
                for t in range(TL):
                    v(V.tensor_scalar(bb[:, t], aa[:, t], -1.0, vec[:, t, 6:7], ALU.add, ALU.mult))
                    v(V.scalar_tensor_tensor(out=kx[:, t], in0=bb[:, t], scalar=1.0, in1=kx[:, t],
                                             op0=ALU.add, op1=ALU.mult))
                v(V.tensor_scalar(lw[:], lw[:], -DECAY_HALF, None, ALU.mult))
                for t in range(TL):
                    v.hold(V.tensor_tensor_scan(cum[:, t], keep[:], lw[:, t], 0.0, ALU.mult, ALU.add))
                v.wait()
                v(V.tensor_tensor(lw[:], cum[:], lw[:], ALU.subtract))
                dve.sem_inc(cum_done, 1)
                dve.wait_ge(norm_done, 1)
                v(V.reciprocal(dlt[:], dlt[:]))
                v(V.tensor_tensor(kkb[:], kkb[:], dlt[:], ALU.mult))
                v(V.tensor_tensor(bb[:], kkb[:], aa[:], ALU.mult))
                for t in range(TL):
                    v.hold(V.scalar_tensor_tensor(out=dlt[:, t], in0=rr[:, t], scalar=vec[:, t, 7:8],
                                                  in1=kx[:, t], op0=ALU.mult, op1=ALU.mult))
                v.wait()
                dve.sem_inc(bonus_in, 1)
                dve.wait_ge(aux_done, 6)
                v(V.tensor_tensor(dlt[:], aux[:].rearrange("p t a b -> p t (a b)"), vv, ALU.mult))
                dve.sem_inc(aux_free, 1)
                dve.wait_ge(exp_done, 1)
                V.tensor_copy(wc[:], aa[:].rearrange("p t (n c) -> p t n c", c=CHUNK)[:, :, :, CHUNK - 1])
                V.tensor_tensor(rr, rr, aa[:], ALU.mult)
                V.scalar_tensor_tensor(out=kkb[:], in0=kkb[:], scalar=-1.0, in1=lw[:], op0=ALU.mult, op1=ALU.mult)
                V.tensor_tensor(bb[:], bb[:], cum[:], ALU.mult)
                v(V.tensor_tensor(kx, kx, cum[:], ALU.mult))
                dve.wait_ge(aux_done, 7)
                for g in range(KV):
                    V.tensor_copy(vpad[:, 1:NB + 1, g, HALF:2 * HALF],
                                  aux[:, 0].rearrange("p a (b c) -> p (a b) c", c=P)[:, :, HALF * g:HALF * g + HALF])


def window_attention(nc, D, proj, vpad):
    with Phase(nc, "swa") as ph:
        kd = ph.sb("kd", [P, KV, 2, SEQ + P])
        mask = ph.sb("mask", [P, NB, 2 * P])
        ident = ph.sb("ident", [P, P])
        qs = ph.sb("qs", [P, PAIRS, P])
        vs = ph.sb("vs", [P, 2, 2, KV, 3 * HALF])
        sinks = ph.sb("sinks", [P, 2 * PAIRS])
        nsinks = ph.sb("nsinks", [P, 2 * PAIRS])
        sc = ph.sb("sc", [P, 2, PAIRS, 2, 2 * P])
        mx = ph.sb("mx", [P, PAIRS, 2])
        nm = ph.sb("nm", [P, PAIRS, 2])
        ls = ph.sb("ls", [P, PAIRS, 2])
        es = ph.sb("es", [P, PAIRS, 2])
        den = ph.sb("den", [P, PAIRS, 2])
        rd = ph.sb("rd", [P, PAIRS, 2])
        pT = ph.sb("pT", [P, 2, 4, P])
        s_ps = ph.ps("s", [P, PAIRS, 512])
        t_ps = ph.ps("t", [P, 2, 512])
        o_ps = ph.ps("o", [P, 2, 512])
        sinks_loaded, mask_done, v_own = ph.sem("sinks_loaded"), ph.sem("mask_done"), ph.sem("v_own")
        staged = ph.sem("staged")
        values = ph.sem("values")
        scored = ph.sem("scored")
        maxed = ph.sem("maxed")
        exped = ph.sem("exped")
        normed = ph.sem("normed")
        turned = ph.sem("turned")
        turned_out = ph.sem("turned_out")
        mixed = ph.sem("mixed")
        gated = ph.sem("gated")
        with nc.Block() as block:

            @block.sync
            def _(sp):
                sp.dma_start(sinks[:], D["attn_sinks"].partition_broadcast(P)).then_inc(sinks_loaded, 16)

            @block.gpsimd
            def _(pool):
                nc.gpsimd.memset(mask[:], 0.0).then_inc(mask_done, 1)
                nc.gpsimd.memset(ident[:], 0.0).then_inc(mask_done, 1)
                pool.wait_ge(mask_done, 2)
                nc.gpsimd.affine_select(out=mask[:, :, 0:P], in_=mask[:, :, 0:P], compare_op=ALU.is_gt,
                                        fill=MASKED, base=0, pattern=[[0, NB], [1, P]],
                                        channel_multiplier=-1).then_inc(mask_done, 1)
                nc.gpsimd.affine_select(out=mask[:, :, P:2 * P], in_=mask[:, :, P:2 * P], compare_op=ALU.is_ge,
                                        fill=MASKED, base=0, pattern=[[0, NB], [-1, P]],
                                        channel_multiplier=1).then_inc(mask_done, 1)
                nc.gpsimd.affine_select(out=ident[:], in_=ident[:], compare_op=ALU.not_equal, fill=1.0,
                                        base=0, pattern=[[-1, P]], channel_multiplier=1).then_inc(mask_done, 1)
                pool.wait_ge(mask_done, 5)
                nc.gpsimd.memset(mask[:, 0, 0:P], MASKED).then_inc(mask_done, 1)

            @block.tensor
            def _(pe):
                pe.wait_ge(mask_done, 6)

                def scores(n):
                    pe.wait_ge(staged, n + 1)
                    for j in range(PAIRS):
                        nc.tensor.matmul(s_ps[:, j].rearrange("p (a b) -> p a b", a=2), qs[:, j],
                                         kd[:, j // 2, :, bass.ds(n * P, 2 * P)],
                                         start=True, stop=True).then_inc(scored, 1)

                def turn(n, p, j):
                    pe.wait_ge(normed, n * PAIRS + j + 1)
                    pe.wait_ge(turned_out, n * PAIRS + j + 1)
                    for c in range(4):
                        last = nc.tensor.transpose(t_ps[:, j % 2, P * c:P * c + P],
                                                   sc[:, p, j, c // 2, P * (c % 2):P * (c % 2) + P], ident[:])
                    last.then_inc(turned, 1)

                def mix(n, p, j):
                    if j == 0:
                        pe.wait_ge(values, n + 1)
                    pe.wait_ge(turned_out, n * PAIRS + j + 3)
                    pe.wait_ge(gated, n * PAIRS + j + 1)
                    for c in range(4):
                        h, b = c // 2, c % 2
                        last = nc.tensor.matmul(o_ps[:, j % 2, 0:P], vs[:, p, b, j // 2, HALF - HALF * h:3 * HALF - HALF * h],
                                                pT[:, j % 2, c], start=(c == 0), stop=(c == 3))
                    last.then_inc(mixed, 1)

                def output(n, p):
                    turn(n, p, 0)
                    for j in range(PAIRS):
                        if j + 1 < PAIRS:
                            turn(n, p, j + 1)
                        mix(n, p, j)

                scores(0)
                with pe.Fori(0, NB // 2 - 1) as i:
                    for p in range(2):
                        scores(2 * i + p + 1)
                        output(2 * i + p, p)
                scores(NB - 1)
                output(NB - 2, 0)
                output(NB - 1, 1)

            @block.scalar
            def _(act):
                act.sem_inc(turned_out, 2)
                act.sem_inc(mixed, 2)
                act.wait_ge(sinks_loaded, 16)

                def exponentials(n, p, j):
                    act.wait_ge(maxed, n * PAIRS + j + 1)
                    for h in range(2):
                        nc.scalar.activation(sc[:, p, j, h], sc[:, p, j, h], ACT.Exp, bias=nm[:, j, h:h + 1],
                                             accum_out=ls[:, j, h:h + 1])
                    for h in range(2):
                        last = nc.scalar.activation(es[:, j, h:h + 1], sinks[:, 2 * j + h:2 * j + h + 1], ACT.Exp,
                                                    bias=nm[:, j, h:h + 1])
                    last.then_inc(exped, 1)

                def evacuate(n, j):
                    act.wait_ge(turned, n * PAIRS + j + 1)
                    act.wait_ge(mixed, n * PAIRS + j + 1)
                    nc.scalar.copy(pT[:, j % 2], t_ps[:, j % 2].rearrange("p (c q) -> p c q", c=4)).then_inc(turned_out, 1)

                def step(n, p):
                    for j in range(PAIRS):
                        exponentials(n + 1, 1 - p, j)
                        evacuate(n, j)

                for j in range(PAIRS):
                    exponentials(0, 0, j)
                with act.Fori(0, NB // 2 - 1) as i:
                    for p in range(2):
                        step(2 * i + p, p)
                step(NB - 2, 0)
                for j in range(PAIRS):
                    evacuate(NB - 1, j)

            @block.vector
            def _(dve):
                v = Chain(dve, v_own)
                dve.sem_inc(gated, 2)
                v.hold(nc.vector.memset(kd[:], 0.0))
                dve.wait_ge(sinks_loaded, 16)
                v(nc.vector.tensor_scalar(nsinks[:], sinks[:], -1.0, None, ALU.mult))
                for src in range(2):
                    for h in range(2):
                        g = h if src == 0 else 1 - h
                        v.hold(nc.vector.tensor_copy(kd[HALF * h:HALF * h + HALF, g, h, P:],
                                                     proj[HALF * h:HALF * h + HALF, K_T + src]))
                v.wait()
                dve.wait_ge(mask_done, 6)

                def queries(n):
                    v(nc.vector.tensor_copy(qs[:], proj[:, Q_T:Q_T + PAIRS, bass.ds(n * P, P)]))
                    dve.sem_inc(staged, 1)

                def block_values(n, p):
                    v(nc.vector.tensor_copy(vs[:, p], vpad[:, bass.ds(n, 2)]))
                    dve.sem_inc(values, 1)

                def biggest(n, p, j):
                    dve.wait_ge(scored, n * PAIRS + j + 1)
                    v(nc.vector.scalar_tensor_tensor(
                        out=sc[:, p, j], in0=s_ps[:, j].rearrange("p (a b) -> p a b", a=2), scalar=HEAD_SCALE,
                        in1=mask[:, bass.ds(n, 1)].to_broadcast([P, 2, 2 * P]), op0=ALU.mult, op1=ALU.add))
                    v(nc.vector.tensor_reduce(mx[:, j], sc[:, p, j], AX.X, ALU.max))
                    nc.vector.scalar_tensor_tensor(out=nm[:, j], in0=mx[:, j], scalar=-1.0,
                                                   in1=nsinks[:, 2 * j:2 * j + 2], op0=ALU.mult,
                                                   op1=ALU.min).then_inc(maxed, 1)

                def norm(n, p, j):
                    dve.wait_ge(exped, n * PAIRS + j + 1)
                    v(nc.vector.tensor_tensor(den[:, j], ls[:, j], es[:, j], ALU.add))
                    v(nc.vector.reciprocal(rd[:, j], den[:, j]))
                    nc.vector.tensor_tensor(sc[:, p, j], sc[:, p, j],
                                            rd[:, j].unsqueeze(2).to_broadcast([P, 2, 2 * P]),
                                            ALU.mult).then_inc(normed, 1)

                def gate(n, j):
                    dve.wait_ge(mixed, n * PAIRS + j + 3)
                    out = proj[:, G_T + j, bass.ds(n * P, P)]
                    nc.vector.tensor_tensor(out, out, o_ps[:, j % 2, 0:P], ALU.mult).then_inc(gated, 1)

                def step(n, p, more=True):
                    block_values(n, p)
                    for j in range(PAIRS):
                        biggest(n + 1, 1 - p, j)
                        if j == PAIRS - 1 and more:
                            queries(n + 2)
                        if j:
                            norm(n + 1, 1 - p, j - 1)
                            gate(n, j - 1)
                    norm(n + 1, 1 - p, PAIRS - 1)
                    gate(n, PAIRS - 1)

                queries(0)
                for j in range(PAIRS):
                    biggest(0, 0, j)
                queries(1)
                for j in range(PAIRS):
                    norm(0, 0, j)
                with dve.Fori(0, NB // 2 - 1) as i:
                    v.restart()
                    for p in range(2):
                        step(2 * i + p, p)
                v.restart()
                step(NB - 2, 0, more=False)
                block_values(NB - 1, 1)
                for j in range(PAIRS):
                    gate(NB - 1, j)
                dve.wait_ge(gated, NB * PAIRS + 2)


def chunks(nc, D, proj, kkb, bb, bonus, wc, vec):
    U = 4
    rr, k2, vv = (proj[:, m:m + TL] for m in (R_T, CK_T, CV_T))
    N1, LT, N2, MT = 3, 4, 5, 6
    V_, K_, B_ = 0, 1, 2
    SQ = 5
    with Phase(nc, "rwc") as ph:
        dg = ph.sb("dg", [P, TL, 2, 6, P])
        big = ph.sb("big", [P, U, 7, P])
        pw = ph.sb("pw", [P, U, 2, P])
        inv = ph.sb("inv", [P, U, P])
        vt = ph.sb("vt", [P, U, HALF])
        am = ph.sb("am", [P, U, P + HALF])
        tav = ph.sb("tav", [P, U, P + HALF])
        gr = ph.sb("gr", [P, U, 2, P])
        hz = ph.sb("hz", [P, U, HALF])
        z = ph.sb("z", [P, TL, 2, HALF])
        wcs = ph.sb("wcs", [P, TL, 2])
        masks = ph.sb("masks", [P, 4, P])
        lowm = ph.sb("lowm", [P, P])
        ident = ph.sb("ident", [P, P])
        idh = ph.sb("idh", [P, HALF])
        st = ph.sb("st", [P, U, 6])
        mv = ph.sb("mv", [P, U, 2])
        rs = ph.sb("rs", [P, U])
        eps = ph.sb("eps", [P, 1])
        ydg = ph.sb("ydg", [P, U, P])
        yo = ph.sb("yo", [P, TL, 2, CHUNK])
        X = [ph.ps(f"x{u}", [P, 512]) for u in range(U)]
        Y = [ph.ps(f"y{u}", [P, 512]) for u in range(U)]
        (const_done, v_own, zeroed, staged_p, staged_a, x_free, passed, crossed, masked, tok_out, inv_init, sq_done, pw_out, am_done, am_out, inv_done, inv_out,
         tav_done, tav_out, gr_done, gr_out, z_done, z_out, var_ready, rooted, y_in, y_turned) = (ph.sem(n) for n in (
             "const_done", "v_own", "zeroed", "staged_p", "staged_a", "x_free", "passed", "crossed", "masked", "tok_out", "inv_init", "sq_done", "pw_out", "am_done",
             "am_out", "inv_done", "inv_out", "tav_done", "tav_out", "gr_done", "gr_out", "z_done", "z_out", "var_ready",
             "rooted", "y_in", "y_turned"))

        def feature(u, n):
            return dg[:, u // 2, u % 2, n]

        def stage(copy, h, n):
            hp = slice(HALF * h, HALF * h + HALF)
            for m, src in ((1, rr), (2, kkb), (3, bb), (4, k2), (5, vv)):
                last = copy(dg[hp, :, :, m, hp], src[hp, :, bass.ds(n * 2 * CHUNK, 2 * CHUNK)].rearrange(
                    "p t (c k) -> p t c k", c=2))
            return last

        with nc.Block() as block:

            @block.gpsimd
            def _(pool):
                g = nc.gpsimd

                def select(m, op, mult, step, fill=0.0, base=0):
                    g.affine_select(out=m, in_=m, compare_op=op, fill=fill, base=base,
                                    pattern=[[step, m.shape[1]]], channel_multiplier=mult).then_inc(const_done, 1)

                g.memset(masks[:], 1.0).then_inc(const_done, 1)
                g.memset(lowm[:], 1.0).then_inc(const_done, 1)
                g.memset(ident[:], 0.0).then_inc(const_done, 1)
                g.memset(idh[:], 0.0).then_inc(const_done, 1)
                pool.wait_ge(const_done, 4)
                for n in range(4):
                    select(masks[:, n], ALU.is_ge if n % 2 == 0 else ALU.is_gt, -1, 1)
                select(lowm[:], ALU.is_gt, 1, -1)
                select(ident[:], ALU.not_equal, 1, -1, 1.0)
                select(idh[:], ALU.not_equal, 1, -1, 1.0)
                pool.wait_ge(const_done, 11)
                select(idh[:], ALU.not_equal, 1, -1, 1.0, -HALF)
                pool.wait_ge(zeroed, 1)
                stage(g.tensor_copy, 0, 0).then_inc(staged_p, 1)

                def body(i, more=True):
                    for u in range(U):
                        pool.wait_ge(masked, i * U + u + 1)
                        g.tensor_tensor(inv[:, u], big[:, u, LT], ident[:], ALU.add)
                        pool.wait_ge(tok_out, i * U + u + 1)
                        g.tensor_tensor(vt[:, u], big[:, u, V_, 0:HALF], big[:, u, V_, HALF:P],
                                        ALU.add).then_inc(inv_init, 1)
                    if more:
                        pool.wait_ge(gr_out, i * U + U)
                        pool.sem_inc(passed, 1)
                        stage(g.tensor_copy, 0, i + 1).then_inc(staged_p, 1)

                with pool.Fori(0, NCH // 2 - 1) as i:
                    body(i)
                body(NCH // 2 - 1, more=False)

            @block.vector
            def _(dve):
                v = Chain(dve, v_own)
                V = nc.vector
                for b in (dg, z, ydg):
                    v.hold(V.memset(b[:], 0.0))
                v(V.memset(eps[:], GN_EPS))
                dve.wait_ge(const_done, 12)
                for u in range(U):
                    v.hold(V.tensor_copy(feature(u, 0), ident[:]))
                v.wait()
                dve.sem_inc(zeroed, 1)

                def body(i):
                    v.restart()
                    now = bass.ds(i * 2 * CHUNK, 2 * CHUNK)
                    V.tensor_copy(wcs[:], wc[:, :, bass.ds(2 * i, 2)])
                    for u in range(U):
                        dve.wait_ge(crossed, i * U + u + 1)
                        V.tensor_tensor(big[:, u, N1:], X[u][:].rearrange("p (a b) -> p a b", a=4), masks[:], ALU.mult)
                        V.tensor_tensor(pw[:, u, 0], Y[u][:, 0:P], lowm[:], ALU.mult).then_inc(masked, 1)
                    for n in range(SQ):
                        for u in range(U):
                            dve.wait_ge(inv_done, i * U * SQ + U * n + u + 1)
                            if n == 0:
                                dve.wait_ge(inv_init, i * U + u + 1)
                            V.tensor_tensor(inv[:, u], inv[:, u], Y[u][:, 2 * P:3 * P], ALU.add).then_inc(inv_out, 1)
                    for u in range(U):
                        dve.wait_ge(gr_done, i * U + u + 1)
                        V.tensor_tensor(gr[:, u], Y[u][:, 0:2 * P].rearrange("p (a b) -> p a b", a=2),
                                        dg[:, u // 2, u % 2, 0:2], ALU.add)
                        V.tensor_scalar(hz[:, u], Y[u][:, 2 * P:2 * P + HALF], wcs[:, u // 2, u % 2:u % 2 + 1], None,
                                        ALU.mult).then_inc(gr_out, 1)
                    dve.wait_ge(gr_out, i * U + U)
                    for c in range(2):
                        for t in range(TL):
                            u = 2 * t + c
                            dve.wait_ge(z_done, i * U + 2 * c + t + 1)
                            V.scalar_tensor_tensor(out=z[:, t, 1 - c], in0=X[u][:, 3 * P:3 * P + HALF],
                                                   scalar=wcs[:, t, c:c + 1], in1=hz[:, u], op0=ALU.mult,
                                                   op1=ALU.add).then_inc(z_out, 1)
                    for u in range(U):
                        v.hold(V.bn_stats(st[:, u], Y[u][:, 2 * P + HALF:3 * P]))
                    v.wait()
                    for u in range(U):
                        last = V.bn_aggr(mv[:, u], st[:, u])
                    last.then_inc(var_ready, 1)
                    dve.wait_ge(rooted, i + 1)
                    v(V.reciprocal(rs[:], rs[:]))
                    for u in range(U):
                        for h in range(2):
                            hp = slice(HALF * h, HALF * h + HALF)
                            last = V.tensor_scalar(ydg[hp, u, hp], Y[u][hp, 2 * P + HALF:3 * P], mv[hp, u, 0:1],
                                                   rs[hp, u:u + 1], ALU.subtract, ALU.mult)
                        last.then_inc(y_in, 1)
                    for u in range(U):
                        t = u // 2
                        dve.wait_ge(y_turned, i * U + u + 1)
                        V.tensor_scalar(yo[:, t, u % 2], X[u][:, 3 * P + HALF:4 * P], vec[:, t, 8:9],
                                        vec[:, t, 9:10], ALU.mult, ALU.add).then_inc(x_free, 1)
                    dve.wait_ge(x_free, i * U + U)
                    yf = yo[:].rearrange("p t c k -> p t (c k)")
                    v(V.tensor_tensor(yf, yf, bonus[:, :, now], ALU.add))
                    out = proj[:, G_T + 6:G_T + 8, now]
                    v(V.tensor_tensor(out, out, yf, ALU.mult))

                with dve.Fori(0, NCH // 2 - 1) as i:
                    body(i)
                body(NCH // 2 - 1)

            @block.scalar
            def _(act):
                act.wait_ge(zeroed, 1)
                stage(nc.scalar.copy, 1, 0).then_inc(staged_a, 1)

                def body(i, more=True):
                    for u in range(U):
                        act.wait_ge(masked, i * U + u + 1)
                        nc.scalar.copy(big[:, u, 0:3].rearrange("p a b -> p (a b)"), Y[u][:, P:4 * P]).then_inc(tok_out, 1)
                    for n in range(SQ):
                        for u in range(U):
                            act.wait_ge(sq_done, i * U * SQ + U * n + u + 1)
                            nc.scalar.copy(pw[:, u].rearrange("p a b -> p (a b)"), X[u][:, 0:2 * P]).then_inc(pw_out, 1)
                        if n == 0:
                            for u in range(U):
                                act.wait_ge(am_done, i * U + u + 1)
                                nc.scalar.copy(am[:, u], Y[u][:, 0:P + HALF]).then_inc(am_out, 1)
                    for u in range(U):
                        act.wait_ge(tav_done, i * U + u + 1)
                        nc.scalar.copy(tav[:, u], X[u][:, 0:P + HALF]).then_inc(tav_out, 1)
                    if more:
                        act.wait_ge(gr_out, i * U + U)
                        stage(nc.scalar.copy, 1, i + 1).then_inc(staged_a, 1)
                    act.wait_ge(var_ready, i + 1)
                    nc.scalar.activation(rs[:], mv[:, :, 1], ACT.Sqrt, bias=eps[:]).then_inc(rooted, 1)

                with act.Fori(0, NCH // 2 - 1) as i:
                    body(i)
                body(NCH // 2 - 1, more=False)

            @block.tensor
            def _(pe):
                mm = nc.tensor.matmul

                def body(i, start=False):
                    pe.wait_ge(staged_p, i + 1)
                    pe.wait_ge(staged_a, i + 1)
                    for u in range(U):
                        if not start:
                            pe.wait_ge(x_free, (i - 1) * U + u + 1)
                        ra = dg[:, u // 2, u % 2, 1:3].rearrange("p a b -> p (a b)")
                        mm(X[u][:, 0:2 * P], feature(u, 3), ra, start=True, stop=True)
                        mm(X[u][:, 2 * P:4 * P], feature(u, 4), ra, start=True, stop=True)
                        mm(Y[u][:, 0:P], feature(u, 2), feature(u, 3), start=True, stop=True)
                        for n, src in enumerate((5, 4, 3)):
                            last = nc.tensor.transpose(Y[u][:, P + P * n:2 * P + P * n], feature(u, src), ident[:])
                        last.then_inc(crossed, 1)
                    for u in range(U):
                        pe.wait_ge(masked, i * U + u + 1)
                        mm(X[u][:, 0:P], big[:, u, LT], pw[:, u, 0], start=True, stop=True)
                        mm(X[u][:, P:2 * P], pw[:, u, 0], big[:, u, LT], start=True, stop=True).then_inc(sq_done, 1)
                    for u in range(U):
                        pe.wait_ge(tok_out, i * U + u + 1)
                        nc.tensor.transpose(Y[u][:, 0:P], feature(u, 2), ident[:])
                        pe.wait_ge(inv_init, i * U + u + 1)
                        mm(Y[u][:, P:P + HALF], big[:, u, MT], vt[:, u], start=True, stop=True).then_inc(am_done, 1)
                    for n in range(SQ):
                        for u in range(U):
                            pe.wait_ge(pw_out, i * U * SQ + U * n + u + 1)
                            if n:
                                pe.wait_ge(inv_out, i * U * SQ + U * (n - 1) + u + 1)
                            else:
                                pe.wait_ge(am_out, i * U + u + 1)
                            mm(Y[u][:, 2 * P:3 * P], pw[:, u, 0], inv[:, u], start=True, stop=True).then_inc(inv_done, 1)
                            if n < SQ - 1:
                                mm(X[u][:, 0:P], pw[:, u, 1], pw[:, u, 0], start=True, stop=True)
                                mm(X[u][:, P:2 * P], pw[:, u, 0], pw[:, u, 1], start=True, stop=True).then_inc(sq_done, 1)
                    for u in range(U):
                        pe.wait_ge(inv_out, i * U * SQ + U * (SQ - 1) + u + 1)
                        mm(X[u][:, 0:P + HALF], inv[:, u], am[:, u], start=True, stop=True).then_inc(tav_done, 1)
                    for u in range(U):
                        pe.wait_ge(tav_out, i * U + u + 1)
                        tmv = tav[:, u, P:P + HALF]
                        mm(Y[u][:, 0:2 * P], tav[:, u, 0:P], big[:, u, B_:N1 + 1].rearrange("p a b -> p (a b)"),
                           start=True, stop=True)
                        h = Y[u][:, 2 * P:2 * P + HALF]
                        mm(h, big[:, u, B_], tmv, start=True, stop=False)
                        mm(h, big[:, u, K_], vt[:, u], start=False, stop=True)
                        y = Y[u][:, 2 * P + HALF:3 * P]
                        mm(y, big[:, u, N1], tmv, start=True, stop=False)
                        mm(y, big[:, u, N2], vt[:, u], start=False, stop=False).then_inc(gr_done, 1)
                    for c in range(2):
                        for t in range(TL):
                            u = 2 * t + c
                            pe.wait_ge(gr_out, i * U + u + 1)
                            if c:
                                pe.wait_ge(z_out, i * U + t + 1)
                            mm(X[u][:, 3 * P:3 * P + HALF], gr[:, u, 0], z[:, t, c], start=True, stop=True)
                            mm(Y[u][:, 2 * P + HALF:3 * P], gr[:, u, 1], z[:, t, c], start=False,
                               stop=True).then_inc(z_done, 1)
                    for u in range(U):
                        pe.wait_ge(y_in, i * U + u + 1)
                        mm(X[u][:, 3 * P + HALF:4 * P], ydg[:, u], idh[:], start=True, stop=True).then_inc(y_turned, 1)
                    pe.wait_ge(z_out, i * U + U)

                body(0, start=True)
                with pe.Fori(1, NCH // 2) as i:
                    body(i)



META = 16
T = META + SEQ
NORM_EPS = 1e-6


def make_identity(nc, pool, ident, sem):
    nc.gpsimd.memset(ident[:], 0.0).then_inc(sem, 1)
    pool.wait_ge(sem, 1)
    nc.gpsimd.affine_select(out=ident[:], in_=ident[:], compare_op=ALU.not_equal, fill=1.0,
                            base=0, pattern=[[-1, P]], channel_multiplier=1).then_inc(sem, 1)


class NormTurn:

    def __init__(self, nc, ph, outs, gains, spans, tile, made):
        self.nc, self.outs, self.gains, self.spans, self.tile, self.made = nc, outs, gains, spans, tile, made
        self.xh = ph.sb("xh", [P, 2, DM])
        self.sq = ph.sb("sq", [P, DM], mybir.dt.bfloat16)
        self.ss, self.rt, self.rs = (ph.sb(n, [P, 2]) for n in ("ss", "rt", "rs"))
        self.eps = ph.sb("neps", [P, 1])
        self.gain = ph.sb("gain", [P, len(gains), KT])
        self.ident = ph.sb("ident", [P, P])
        self.tp = ph.ps("tp", [P, 2, 2, 512])
        self.g_loaded, self.id_done, self.rooted, self.scaled, self.turned, self.out_done, self.own = (
            ph.sem(n) for n in ("g_loaded", "id_done", "nrooted", "scaled", "turned", "out_done", "n_own"))

    def load(self, sp):
        for n, g in enumerate(self.gains):
            sp.dma_start(self.gain[:, n], g).then_inc(self.g_loaded, 16)

    def constants(self, pool):
        make_identity(self.nc, pool, self.ident, self.id_done)
        self.nc.gpsimd.memset(self.eps[:], NORM_EPS).then_inc(self.id_done, 1)

    def square(self, act, n):
        r, b = self.spans[n][1], n % 2
        act.wait_ge(self.id_done, 3)
        act.wait_ge(self.made, n + 1)
        if n >= 2:
            act.wait_ge(self.scaled, n - 1)
        self.nc.scalar.activation(self.sq[0:r], self.tile(n), ACT.Square,
                                  accum_out=self.ss[0:r, b:b + 1]).then_inc(self.own, 1)
        act.wait_ge(self.own, n + 1)
        self.nc.scalar.activation(self.rt[0:r, b:b + 1], self.ss[0:r, b:b + 1], ACT.Sqrt, scale=1.0 / DM,
                                  bias=self.eps[0:r]).then_inc(self.rooted, 1)

    def scale(self, dve, v, n):
        r, b = self.spans[n][1], n % 2
        dve.wait_ge(self.rooted, n + 1)
        v(self.nc.vector.reciprocal(self.rs[0:r, b:b + 1], self.rt[0:r, b:b + 1]))
        if n >= 2:
            dve.wait_ge(self.turned, n - 1)
        self.nc.vector.tensor_scalar(self.xh[0:r, b], self.tile(n), self.rs[0:r, b:b + 1], None,
                                     ALU.mult).then_inc(self.scaled, 1)

    def turn(self, pe, n):
        r, b = self.spans[n][1], n % 2
        pe.wait_ge(self.scaled, n + 1)
        pe.wait_ge(self.id_done, 3)
        if n >= 2:
            pe.wait_ge(self.out_done, n - 1)
        for k in range(KT):
            last = self.nc.tensor.transpose(self.tp[:, b, k // 4, P * (k % 4):P * (k % 4) + r],
                                            self.xh[0:r, b, P * k:P * k + P], self.ident[0:r, 0:r])
        last.then_inc(self.turned, 1)

    def out(self, dve, n):
        (at, r), b = self.spans[n], n % 2
        dve.wait_ge(self.g_loaded, 16 * len(self.gains))
        dve.wait_ge(self.turned, n + 1)
        for i, out in enumerate(self.outs):
            for c in range(2):
                last = self.nc.vector.tensor_tensor(
                    out[:, 4 * c:4 * c + 4, at:at + r],
                    self.tp[:, b, c].rearrange("p (k q) -> p k q", k=4)[:, :, 0:r],
                    self.gain[:, i, 4 * c:4 * c + 4].unsqueeze(2).to_broadcast([P, 4, r]), ALU.mult)
        last.then_inc(self.out_done, 1)


def first_out(nc, D, proj, hnT):
    with Phase(nc, "fo") as ph:
        wo = ph.sb("wo", [P, KT, DM])
        xb = ph.sb("xb", [P, 2, DM])
        hb = ph.sb("hb", [P, 2, DM])
        gb = ph.sb("gb", [P, 2, DM])
        st = ph.sb("st", [P, 2, 6])
        mv = ph.sb("mv", [P, 2])
        rs = ph.sb("lrs", [P, 1])
        eps = ph.sb("eps", [P, 1])
        acc = ph.ps("acc", [P, 2, 2, 512])
        w_loaded = [ph.sem(f"w{k}_loaded") for k in range(KT)]
        gb_loaded, v_own, made, meta_in, pad_ready, padded = (
            ph.sem(n) for n in ("gb_loaded", "v_own", "made", "meta_in", "pad_ready", "padded"))
        stored = [ph.sem("h0_stored"), ph.sem("h1_stored")]
        x_loaded = [ph.sem("x0_loaded"), ph.sem("x1_loaded")]
        done, var_ready, rooted, summed = ph.sem("done"), ph.sem("var_ready"), ph.sem("rooted"), ph.sem("summed")
        h = D["h0"]
        spans = [(0, META)] + [(META + P * t, P) for t in range(NB)]
        norm = NormTurn(nc, ph, [hnT], [D["norm_mix_g_t"][0]], spans,
                        lambda n: hb[:, (n - 1) % 2] if n else hb[0:META, 1], made)
        with nc.Block() as block:

            @block.sync
            def _(sp):
                sp.dma_start(hb[0:META, 1], D["meta_tokens_2"]).then_inc(meta_in, 16)
                for k in range(KT):
                    sp.dma_start(wo[:, k], D["w_out"][P * k:P * k + P]).then_inc(w_loaded[k], 16)
                for t in range(2):
                    sp.dma_start(xb[:, t], D["x"][P * t:P * t + P]).then_inc(x_loaded[t], 16)
                sp.dma_start(gb[:, 0], D["ln_g"].partition_broadcast(P)).then_inc(gb_loaded, 16)
                sp.dma_start(gb[:, 1], D["ln_b"].partition_broadcast(P)).then_inc(gb_loaded, 16)
                norm.load(sp)
                sp.wait_ge(meta_in, 16)
                sp.dma_start(h[0:META], hb[0:META, 1]).then_inc(padded, 16)
                for t in range(NB):
                    sp.wait_ge(made, t + 2)
                    sp.dma_start(h[META + P * t:META + P * t + P], hb[:, t % 2]).then_inc(stored[t % 2], 16)
                    if t + 2 < NB:
                        sp.dma_start(xb[:, t % 2], D["x"][P * (t + 2):P * (t + 3)]).then_inc(x_loaded[t % 2], 16)
                sp.wait_ge(padded, 16)
                sp.wait_ge(summed, NB)
                sp.dma_start(h[META + SEQ:], xb[0:P - META, 0]).then_inc(padded, 16)
                sp.wait_ge(padded, 32)
                for b in range(2):
                    sp.wait_ge(stored[b], 16 * (NB // 2))

            @block.gpsimd
            def _(pool):
                norm.constants(pool)

            @block.tensor
            def _(pe):
                for t in range(NB):
                    if t >= 2:
                        pe.wait_ge(var_ready, t - 1)
                    for c in range(2):
                        for k in range(KT):
                            if t == 0 and c == 0:
                                pe.wait_ge(w_loaded[k], 16)
                            last = nc.tensor.matmul(acc[:, t % 2, c], proj[:, G_T + k, P * t:P * t + P],
                                                    wo[:, k, 512 * c:512 * c + 512], start=(k == 0), stop=(k == KT - 1))
                    last.then_inc(done, 1)
                    if t >= 1:
                        norm.turn(pe, t - 1)
                for n in (NB - 1, NB):
                    norm.turn(pe, n)

            @block.vector
            def _(dve):
                v = Chain(dve, v_own)
                nc.vector.memset(hnT[:, :, T:], 0.0).then_inc(pad_ready, 1)
                v(nc.vector.memset(eps[:], LN_EPS))
                dve.wait_ge(meta_in, 16)
                dve.sem_inc(made, 1)
                norm.scale(dve, v, 0)
                dve.wait_ge(gb_loaded, 32)
                dve.wait_ge(padded, 16)
                for t in range(NB):
                    b = t % 2
                    dve.wait_ge(done, t + 1)
                    dve.wait_ge(x_loaded[b], 16 * (t // 2 + 1))
                    if t >= 2:
                        dve.wait_ge(stored[b], 16 * (t // 2))
                    v(nc.vector.scalar_tensor_tensor(out=hb[:, b], in0=xb[:, b], scalar=ALPHA,
                                                     in1=acc[:, b].rearrange("p a b -> p (a b)"),
                                                     op0=ALU.mult, op1=ALU.add))
                    for c in range(2):
                        v.hold(nc.vector.bn_stats(st[:, c], hb[:, b, 512 * c:512 * c + 512]))
                    v.wait()
                    v(nc.vector.bn_aggr(mv[:], st[:].rearrange("p a b -> p (a b)")))
                    dve.sem_inc(var_ready, 1)
                    if t >= 1:
                        norm.scale(dve, v, t)
                    dve.wait_ge(rooted, t + 1)
                    v(nc.vector.reciprocal(rs[:], rs[:]))
                    v(nc.vector.tensor_scalar(hb[:, b], hb[:, b], mv[:, 0:1], rs[:], ALU.subtract, ALU.mult))
                    v(nc.vector.tensor_tensor(hb[:, b], hb[:, b], gb[:, 0], ALU.mult))
                    v(nc.vector.tensor_tensor(hb[:, b], hb[:, b], gb[:, 1], ALU.add))
                    dve.sem_inc(made, 1)
                    if t == NB - 1:
                        v(nc.vector.memset(xb[:, 0], 0.0))
                        dve.sem_inc(summed, NB)
                    if t >= 1:
                        norm.out(dve, t - 1)
                norm.scale(dve, v, NB)
                norm.out(dve, NB - 1)
                norm.out(dve, NB)

            @block.scalar
            def _(act):
                norm.square(act, 0)
                for t in range(NB):
                    act.wait_ge(var_ready, t + 1)
                    nc.scalar.activation(rs[:], mv[:, 1:2], ACT.Sqrt, bias=eps[:]).then_inc(rooted, 1)
                    norm.square(act, t + 1)


def first(nc, D, proj):
    with Phase(nc, "V") as pv:
        vpad = pv.sb("vpad", [P, NB + 1, KV, 3 * HALF])
        kkb = pv.sb("kkb", [P, TL, SEQ])
        bb = pv.sb("bb", [P, TL, SEQ])
        bonus = pv.sb("bonus", [P, TL, SEQ])
        wc = pv.sb("wc", [P, TL, NCH])
        vec = pv.sb("vec", [P, TL, 10])
        front(nc, D, proj, vpad, kkb, bb, bonus, wc, vec)
        window_attention(nc, D, proj, vpad)
        chunks(nc, D, proj, kkb, bb, bonus, wc, vec)

TT = -(-T // P)
TP = TT * P
LAST = T - (TT - 1) * P
CUTS = [(0, 352), (352, 352), (704, T - 704)]
GROUPS = 8
LG = GROUPS + 64
PER_GROUP = 8
EXPERTS = GROUPS * PER_GROUP
DE = 256
CAP = 64
MAIN_SLOTS = EXPERTS * CAP
SPILL_BLOCKS = 2 * T // CAP
SPILL_BLOCKS += SPILL_BLOCKS % 2
PER_EXPERT_SPILL = (T - 1) // CAP
SLOTS = MAIN_SLOTS + SPILL_BLOCKS * CAP
PAIRS_M = EXPERTS // 2
HEADS = 8
NOPE = 128
ROPE = 64
QR = 384
KVR = 256
VD = 128
ATT_SCALE = float(NOPE + ROPE) ** -0.5


def rows_of(t):
    return P if t < TT - 1 else LAST


def back_and_route(nc, D, layer, src, w_dram, h_in, h_out, lg):
    with Phase(nc, "pb") as ph:
        NBUF = 2
        w = ph.sb("w", [P, KT, DM])
        hb = ph.sb("hb", [P, NBUF, DM])
        ho = ph.sb("ho", [P, 2, DM])
        hn = ph.sb("hn", [P, 2, DM])
        hnT = ph.sb("hnT", [P, 2, KT, P])
        gb = ph.sb("gb", [P, DM])
        wr = ph.sb("wr", [P, KT, LG])
        sq = ph.sb("sq", [P, DM], mybir.dt.bfloat16)
        ss, rt, rs = (ph.sb(n, [P, 2]) for n in ("ss", "rt", "rs"))
        eps = ph.sb("eps", [P, 1])
        ident = ph.sb("ident", [P, P])
        acc = ph.ps("acc", [P, 2, 2, 512])
        tp = ph.ps("tp", [P, 2, 512])
        lg_ps = ph.ps("lg_ps", [P, 2, 512])
        w_loaded = [ph.sem(f"w{k}_loaded") for k in range(KT)]
        (r_loaded, done, summed, id_done, squared, rooted, scaled, turned, evac, lg_done, lg_out, v_own) = (
            ph.sem(n) for n in ("r_loaded", "done", "summed", "id_done", "squared", "rooted", "scaled", "turned",
                                "evac", "lg_done", "lg_out", "v_own"))
        loaded = [ph.sem(f"h{n}_loaded") for n in range(NBUF)]
        stored = [ph.sem(f"h{n}_stored") for n in range(2)]
        hn_stored = [ph.sem(f"hn{n}_stored") for n in range(2)]
        with nc.Block() as block:

            @block.sync
            def _(sp):
                for k in range(KT):
                    sp.dma_start(w[:, k], w_dram[P * k:P * k + P]).then_inc(w_loaded[k], 16)
                sp.dma_start(wr[:], D["w_route_t"][layer]).then_inc(r_loaded, 16)
                sp.dma_start(gb[:], D["norm_ffn_g_2"][layer].partition_broadcast(P)).then_inc(r_loaded, 16)
                for t in range(TT):
                    if t >= NBUF:
                        sp.wait_ge(summed, t - NBUF + 1)
                    sp.dma_start(hb[:, t % NBUF], h_in[P * t:P * t + P]).then_inc(loaded[t % NBUF], 16)

            @block.gpsimd
            def _(pool):
                make_identity(nc, pool, ident, id_done)
                nc.gpsimd.memset(eps[:], NORM_EPS).then_inc(id_done, 1)

            @block.scalar
            def _(act):
                act.wait_ge(id_done, 3)

                def logits_out(t):
                    act.wait_ge(lg_done, t + 1)
                    nc.scalar.copy(lg[:, t], lg_ps[:, t % 2, 0:LG]).then_inc(lg_out, 1)

                for t in range(TT):
                    b = t % 2
                    act.wait_ge(summed, t + 1)
                    act.dma_start(h_out[P * t:P * t + P], ho[:, b]).then_inc(stored[b], 16)
                    if t >= 2:
                        act.wait_ge(scaled, t - 1)
                    nc.scalar.activation(sq[:], ho[:, b], ACT.Square, accum_out=ss[:, b:b + 1]).then_inc(squared, 1)
                    act.wait_ge(squared, t + 1)
                    nc.scalar.activation(rt[:, b:b + 1], ss[:, b:b + 1], ACT.Sqrt, scale=1.0 / DM,
                                         bias=eps[:]).then_inc(rooted, 1)
                    act.wait_ge(scaled, t + 1)
                    act.dma_start(D["hn"][P * t:P * t + P], hn[:, b]).then_inc(hn_stored[b], 16)
                    if t >= 2:
                        logits_out(t - 2)
                logits_out(TT - 2)
                logits_out(TT - 1)
                for b in range(2):
                    act.wait_ge(stored[b], 16 * ((TT + 1 - b) // 2))
                    act.wait_ge(hn_stored[b], 16 * ((TT + 1 - b) // 2))

            @block.tensor
            def _(pe):
                pe.wait_ge(id_done, 3)

                def turn(t):
                    pe.wait_ge(scaled, t + 1)
                    if t >= 1:
                        pe.wait_ge(evac, t)
                    for k in range(KT):
                        last = nc.tensor.transpose(tp[:, k // 4, P * (k % 4):P * (k % 4) + P],
                                                   hn[:, t % 2, P * k:P * k + P], ident[:])
                    last.then_inc(turned, 1)

                def logits(t):
                    pe.wait_ge(evac, t + 1)
                    pe.wait_ge(r_loaded, 32)
                    if t >= 2:
                        pe.wait_ge(lg_out, t - 1)
                    for k in range(KT):
                        last = nc.tensor.matmul(lg_ps[:, t % 2, 0:LG], hnT[:, t % 2, k], wr[:, k],
                                                start=(k == 0), stop=(k == KT - 1))
                    last.then_inc(lg_done, 1)

                for t in range(TT):
                    if t >= 2:
                        pe.wait_ge(summed, t - 1)
                    for c in range(2):
                        for k in range(KT):
                            if t == 0 and c == 0:
                                pe.wait_ge(w_loaded[k], 16)
                            last = nc.tensor.matmul(acc[:, t % 2, c], src[:, k, P * t:P * t + P],
                                                    w[:, k, 512 * c:512 * c + 512], start=(k == 0), stop=(k == KT - 1))
                    last.then_inc(done, 1)
                    if t >= 1:
                        turn(t - 1)
                    if t >= 2:
                        logits(t - 2)
                logits(TT - 2)
                turn(TT - 1)
                logits(TT - 1)

            @block.vector
            def _(dve):
                v = Chain(dve, v_own)
                dve.wait_ge(r_loaded, 32)

                def scale(t):
                    b = t % 2
                    dve.wait_ge(rooted, t + 1)
                    v(nc.vector.reciprocal(rs[:, b:b + 1], rt[:, b:b + 1]))
                    if t >= 2:
                        dve.wait_ge(turned, t - 1)
                        dve.wait_ge(hn_stored[b], 16 * (t // 2))
                    nc.vector.scalar_tensor_tensor(out=hn[:, b], in0=ho[:, b], scalar=rs[:, b:b + 1], in1=gb[:],
                                                   op0=ALU.mult, op1=ALU.mult).then_inc(scaled, 1)

                def evacuate(t):
                    dve.wait_ge(turned, t + 1)
                    if t >= 2:
                        dve.wait_ge(lg_done, t - 1)
                    nc.vector.tensor_copy(hnT[:, t % 2].rearrange("p k q -> p (k q)"),
                                          tp[:].rearrange("p a b -> p (a b)")).then_inc(evac, 1)

                for t in range(TT):
                    dve.wait_ge(done, t + 1)
                    dve.wait_ge(loaded[t % NBUF], 16 * (t // NBUF + 1))
                    if t >= 2:
                        dve.wait_ge(stored[t % 2], 16 * (t // 2))
                    nc.vector.tensor_tensor(ho[:, t % 2], acc[:, t % 2].rearrange("p a b -> p (a b)"),
                                            hb[:, t % NBUF], ALU.add).then_inc(summed, 1)
                    scale(t)
                    if t >= 1:
                        evacuate(t - 1)
                evacuate(TT - 1)


def conv_mixer(nc, D, hnT, zT):
    with Phase(nc, "cm") as ph:
        w = ph.sb("w", [P, 2, 3, KT, P])
        taps = ph.sb("taps", [P, KT, 3])
        bT = ph.sb("bT", [P, 2, T])
        cT = ph.sb("cT", [P, 2, 352])
        z = ph.sb("z", [P, 2, T + 2])
        acc = ph.ps("acc", [P, 2, 3, 512])
        w_loaded = [ph.sem(f"w{n}_loaded") for n in range(2)]
        part_loaded = [ph.sem(f"part{s}_loaded") for s in range(3)]
        taps_loaded, done, copied, z_made, conv_done, v_own = (
            ph.sem(n) for n in ("taps_loaded", "done", "copied", "z_made", "conv_done", "v_own"))
        NC = len(CUTS)
        with nc.Block() as block:

            @block.sync
            def _(sp):
                for s in range(3):
                    sp.dma_start(w[:, 0, s], D["conv_w_in_t"][0, :, s]).then_inc(part_loaded[s], 16)
                sp.dma_start(taps[:], D["conv_w_2_t"]).then_inc(taps_loaded, 16)
                for j in range(1, KT):
                    if j >= 2:
                        sp.wait_ge(done, NC * (j - 1))
                    sp.dma_start(w[:, j % 2], D["conv_w_in_t"][j]).then_inc(w_loaded[j % 2], 16)

            @block.tensor
            def _(pe):
                for j in range(KT):
                    if j:
                        pe.wait_ge(w_loaded[j % 2], 16 * ((j + 1) // 2))
                    for n, (at, cols) in enumerate(CUTS):
                        u = NC * j + n
                        if u >= 2:
                            pe.wait_ge(z_made, u - 1)
                            pe.wait_ge(copied, u - 1)
                        for s in range(3):
                            if u == 0:
                                pe.wait_ge(part_loaded[s], 16)
                            for k in range(KT):
                                last = nc.tensor.matmul(acc[:, u % 2, s, 0:cols], w[:, j % 2, s, k],
                                                        hnT[:, k, at:at + cols], start=(k == 0), stop=(k == KT - 1))
                        last.then_inc(done, 1)

            @block.scalar
            def _(act):
                for j in range(KT):
                    if j >= 2:
                        act.wait_ge(conv_done, j - 1)
                    for n, (at, cols) in enumerate(CUTS):
                        u = NC * j + n
                        act.wait_ge(done, u + 1)
                        if u >= 2:
                            act.wait_ge(z_made, u - 1)
                        nc.scalar.copy(bT[:, j % 2, at:at + cols], acc[:, u % 2, 0, 0:cols])
                        nc.scalar.copy(cT[:, u % 2, 0:cols], acc[:, u % 2, 1, 0:cols]).then_inc(copied, 1)

            @block.vector
            def _(dve):
                v = Chain(dve, v_own)
                v.hold(nc.vector.memset(zT[:, :, T:TP], 0.0))
                v(nc.vector.memset(z[:, :, 0:2], 0.0))
                dve.wait_ge(taps_loaded, 16)
                for j in range(KT):
                    for n, (at, cols) in enumerate(CUTS):
                        u = NC * j + n
                        dve.wait_ge(copied, u + 1)
                        nc.vector.tensor_tensor(z[:, j % 2, 2 + at:2 + at + cols], cT[:, u % 2, 0:cols],
                                                acc[:, u % 2, 2, 0:cols], ALU.mult).then_inc(z_made, 1)
                    dve.wait_ge(z_made, NC * (j + 1))
                    v(nc.vector.tensor_scalar(zT[:, j, 0:T], z[:, j % 2, 0:T], taps[:, j, 0:1], None, ALU.mult))
                    for s in (1, 2):
                        v(nc.vector.scalar_tensor_tensor(out=zT[:, j, 0:T], in0=z[:, j % 2, s:s + T],
                                                         scalar=taps[:, j, s:s + 1], in1=zT[:, j, 0:T],
                                                         op0=ALU.mult, op1=ALU.add))
                    v(nc.vector.tensor_tensor(zT[:, j, 0:T], zT[:, j, 0:T], bT[:, j % 2], ALU.mult))
                    dve.sem_inc(conv_done, 1)


def latents(nc, D, hq, hk, cq, ckv, kr):
    QT, CT = QR // P, KVR // P
    with Phase(nc, "la") as ph:
        wq = ph.sb("wq", [P, KT, QR])
        wk = ph.sb("wk", [P, KT, KVR])
        wr = ph.sb("wr", [P, KT, 2, P])
        gq = ph.sb("gq", [P, QT])
        gk = ph.sb("gk", [P, CT])
        cosT = ph.sb("cosT", [P, T])
        sinT = ph.sb("sinT", [P, T])
        ident = ph.sb("ident", [P, P])
        lat = ph.sb("lat", [P, 2, QR + KVR])
        sq = ph.sb("sq", [P, QR])
        ss = ph.sb("ss", [P, 2, 2])
        rs = ph.sb("rs", [P, 2, 2])
        eps = ph.sb("eps", [P, 1])
        rot = ph.sb("rot", [P, 2, 352])
        acc = ph.ps("acc", [P, 2, 2, 512])
        tp = ph.ps("tp", [P, 2, 512])
        tk = ph.ps("tk", [P, 2, 512])
        q_loaded, k_loaded, loaded, id_done, eps_done, done, squared, rooted, scaled, turned, out_done, v_own, a_own, rope_done, rope_out = (
            ph.sem(n) for n in ("q_loaded", "k_loaded", "loaded", "id_done", "eps_done", "done", "squared", "rooted", "scaled", "turned", "out_done",
                                "v_own", "a_own", "rope_done", "rope_out"))
        with nc.Block() as block:

            @block.sync
            def _(sp):
                sp.dma_start(wq[:], D["w_dq_t"]).then_inc(q_loaded, 16)
                sp.dma_start(wk[:], D["w_dkv_t"]).then_inc(k_loaded, 16)
                for dst, src in ((wr, "w_rope_t"), (gq, "cq_g_t"), (gk, "ckv_g_t"),
                                 (cosT, "cos_t"), (sinT, "sin_t")):
                    sp.dma_start(dst[:], D[src]).then_inc(loaded, 16)

            @block.gpsimd
            def _(pool):
                make_identity(nc, pool, ident, id_done)

            @block.tensor
            def _(pe):
                pe.wait_ge(q_loaded, 16)
                pe.wait_ge(id_done, 2)

                def turn(t):
                    pe.wait_ge(scaled, t + 1)
                    if t >= 2:
                        pe.wait_ge(out_done, t - 1)
                    for n in range(QT + CT):
                        dst = tp[:, t % 2, P * n:P * n + P] if n < QT else tk[:, t % 2, P * (n - QT):P * (n - QT) + P]
                        last = nc.tensor.transpose(dst, lat[:, t % 2, P * n:P * n + P], ident[:])
                    last.then_inc(turned, 1)

                for t in range(TT):
                    if t >= 2:
                        pe.wait_ge(scaled, t - 1)
                    for w, src, cols, c in ((wq, hq, QR, 0), (wk, hk, KVR, 1)):
                        if c and t == 0:
                            pe.wait_ge(k_loaded, 16)
                        for k in range(KT):
                            last = nc.tensor.matmul(acc[:, t % 2, c, 0:cols], src[:, k, P * t:P * t + P], w[:, k],
                                                    start=(k == 0), stop=(k == KT - 1))
                    last.then_inc(done, 1)
                    if t >= 1:
                        turn(t - 1)
                turn(TT - 1)
                pe.wait_ge(out_done, TT)
                pe.wait_ge(loaded, 16 * 5)
                for n, (at, cols) in enumerate(CUTS):
                    if n >= 2:
                        pe.wait_ge(rope_out, n - 1)
                    for s in range(2):
                        for k in range(KT):
                            last = nc.tensor.matmul(acc[:, n % 2, s, 0:cols], wr[:, k, s], hk[:, k, at:at + cols],
                                                    start=(k == 0), stop=(k == KT - 1))
                    last.then_inc(rope_done, 1)

            @block.scalar
            def _(act):
                a = Chain(act, a_own)
                act.wait_ge(eps_done, 1)
                for t in range(TT):
                    b = t % 2
                    act.wait_ge(done, t + 1)
                    if t >= 2:
                        act.wait_ge(scaled, t - 1)
                    a(nc.scalar.activation(sq[:], acc[:, b, 0, 0:QR], ACT.Square, accum_out=ss[:, b, 0:1]))
                    a(nc.scalar.activation(sq[:, 0:KVR], acc[:, b, 1, 0:KVR], ACT.Square, accum_out=ss[:, b, 1:2]))
                    nc.scalar.activation(ss[:, b, 0:1], ss[:, b, 0:1], ACT.Sqrt, scale=1.0 / QR, bias=eps[:])
                    nc.scalar.activation(ss[:, b, 1:2], ss[:, b, 1:2], ACT.Sqrt, scale=1.0 / KVR,
                                         bias=eps[:]).then_inc(rooted, 1)

            @block.vector
            def _(dve):
                v = Chain(dve, v_own)
                nc.vector.memset(eps[:], NORM_EPS).then_inc(eps_done, 1)
                v(nc.vector.memset(kr[:], 0.0))
                dve.wait_ge(loaded, 16 * 5)

                def evacuate(t):
                    dve.wait_ge(turned, t + 1)
                    nc.vector.tensor_tensor(cq[:, :, P * t:P * t + P],
                                            tp[:, t % 2, 0:QR].rearrange("p (k q) -> p k q", k=QT),
                                            gq[:].unsqueeze(2).to_broadcast([P, QT, P]), ALU.mult)
                    nc.vector.tensor_tensor(ckv[:, :, P * t:P * t + P],
                                            tk[:, t % 2, 0:KVR].rearrange("p (k q) -> p k q", k=CT),
                                            gk[:].unsqueeze(2).to_broadcast([P, CT, P]), ALU.mult).then_inc(out_done, 1)

                for t in range(TT):
                    b = t % 2
                    dve.wait_ge(rooted, t + 1)
                    v(nc.vector.reciprocal(rs[:, b], ss[:, b]))
                    if t >= 2:
                        dve.wait_ge(turned, t - 1)
                    nc.vector.tensor_scalar(lat[:, b, 0:QR], acc[:, b, 0, 0:QR], rs[:, b, 0:1], None, ALU.mult)
                    nc.vector.tensor_scalar(lat[:, b, QR:], acc[:, b, 1, 0:KVR], rs[:, b, 1:2], None,
                                            ALU.mult).then_inc(scaled, 1)
                    if t >= 1:
                        evacuate(t - 1)
                evacuate(TT - 1)
                for n, (at, cols) in enumerate(CUTS):
                    dve.wait_ge(rope_done, n + 1)
                    v.hold(nc.vector.tensor_tensor(rot[:, 0, 0:cols], acc[:, n % 2, 0, 0:cols], cosT[:, at:at + cols], ALU.mult))
                    v(nc.vector.tensor_tensor(rot[:, 1, 0:cols], acc[:, n % 2, 1, 0:cols], sinT[:, at:at + cols], ALU.mult))
                    for h in range(2):
                        hp = slice(HALF * h, HALF * h + HALF)
                        v.hold(nc.vector.tensor_tensor(kr[hp, h, at:at + cols], rot[hp, 0, 0:cols], rot[hp, 1, 0:cols], ALU.add))
                    v.wait()
                    dve.sem_inc(rope_out, 1)


def heads(nc, D, cq, ckv, kr, oT):
    QT, CT = QR // P, KVR // P
    with Phase(nc, "hd") as ph:
        wq = ph.sb("wq", [P, 2, QT, 4, P])
        wkv = ph.sb("wkv", [P, 2, CT, 4, P])
        cosT = ph.sb("cosT", [P, T])
        sinT = ph.sb("sinT", [P, T])
        qn = ph.sb("qn", [P, 2, T])
        qr = ph.sb("qr", [P, T])
        rot = ph.sb("rot", [P, 352])
        kn = ph.sb("kn", [P, 2, TP])
        vv = ph.sb("vv", [P, TT, 2, VD])
        pr = ph.sb("pr", [P, 2, TP])
        pT = ph.sb("pT", [P, 2, TT, P])
        mx = ph.sb("mx", [P, 2])
        nm = ph.sb("nm", [P, 2])
        ls = ph.sb("ls", [P, 2])
        rl = ph.sb("rl", [P, 2])
        dg = ph.sb("dg", [P, 2, P])
        ident = ph.sb("ident", [P, P])
        mask = ph.sb("mask", [P, P])
        SB = 5
        s_ps = ph.ps("s", [P, SB * 512])
        t_ps = ph.ps("t", [P, 2, 512])
        o_ps = ph.ps("o", [P, 512])
        w_loaded = [ph.sem(f"w{n}_loaded") for n in range(2)]
        (tab_loaded, id_done, mask_done, pdone, pout, v_own, ready, scored, maxed, exped, turned, turned_out,
         mixed, diag_done, oout, pads) = (ph.sem(n) for n in (
             "tab_loaded", "id_done", "mask_done", "pdone", "pout", "v_own", "ready", "scored", "maxed",
             "exped", "turned", "turned_out", "mixed", "diag_done", "oout", "pads"))
        NPAIR = HEADS // 2
        jobs = ([("qn", h, c) for h in range(2) for c in range(3)] + [("qa", 0, c) for c in range(3) for _ in (0,)]
                + [("kn", h, c) for h in range(2) for c in range(3)] + [("v", 0, t) for t in range(TT)])
        order = []
        for kind, h, c in jobs:
            order.append((kind, h, c))
            if kind == "qa":
                order.append(("qb", h, c))
        NJ = len(order)
        units = [(TT - 1, 0), (TT - 2, 0), (TT - 1, 1), (TT - 2, 1)] + [(t, h) for t in range(TT - 3, -1, -1) for h in range(2)]
        NU = len(units)

        def quads(t):
            return -(-(t + 1) // 4)
        NQ = sum(quads(t) for t, _ in units)
        qbase = [sum(quads(t) for t, _ in units[:n]) for n in range(NU)]

        def scores(n, cut, cols):
            at = 3 * 512 * (n % 2) + 512 * cut
            return s_ps[0:rows_of(units[n][0]), at:at + cols]

        with nc.Block() as block:

            @block.sync
            def _(sp):
                for j in range(NPAIR):
                    if j >= 2:
                        sp.wait_ge(pdone, NJ * (j - 1))
                    sp.dma_start(wq[:, j % 2], D["w_uq_t"][j]).then_inc(w_loaded[j % 2], 16)
                    sp.dma_start(wkv[:, j % 2], D["w_ukv_t"][j]).then_inc(w_loaded[j % 2], 16)
                    if j == 0:
                        sp.dma_start(cosT[:], D["cos_t"]).then_inc(tab_loaded, 16)
                        sp.dma_start(sinT[:], D["sin_t"]).then_inc(tab_loaded, 16)

            @block.gpsimd
            def _(pool):
                make_identity(nc, pool, ident, id_done)
                nc.gpsimd.memset(mask[:], 0.0).then_inc(mask_done, 1)
                pool.wait_ge(mask_done, 1)
                nc.gpsimd.affine_select(out=mask[:], in_=mask[:], compare_op=ALU.is_ge, fill=MASKED, base=0,
                                        pattern=[[-1, P]], channel_multiplier=1).then_inc(mask_done, 1)

            @block.tensor
            def _(pe):
                mm = nc.tensor.matmul
                pe.wait_ge(id_done, 2)
                for j in range(NPAIR):
                    b = j % 2
                    pe.wait_ge(w_loaded[b], 32 * (j // 2 + 1))
                    for n, (kind, h, c) in enumerate(order):
                        m = NJ * j + n
                        if n < SB:
                            if j:
                                pe.wait_ge(exped, NU * j)
                        else:
                            pe.wait_ge(pout, m - SB + 1)
                        bank = s_ps[:, 512 * (n % SB):512 * (n % SB + 1)]
                        if kind == "v":
                            for k in range(CT):
                                last = mm(bank[:, 0:2 * VD], ckv[:, k, P * c:P * c + P],
                                          wkv[:, b, k, 2:4].rearrange("p a b -> p (a b)"),
                                          start=(k == 0), stop=(k == CT - 1))
                        else:
                            at, cols = CUTS[c]
                            w, src, kt = (wkv, ckv, CT) if kind == "kn" else (wq, cq, QT)
                            which = {"kn": h, "qn": h, "qa": 2, "qb": 3}[kind]
                            for k in range(kt):
                                last = mm(bank[:, 0:cols], w[:, b, k, which], src[:, k, at:at + cols],
                                          start=(k == 0), stop=(k == kt - 1))
                        last.then_inc(pdone, 1)
                    pe.wait_ge(ready, j + 1)

                    def score(n):
                        t, h = units[n]
                        u = NU * j + n
                        if n >= 2:
                            pe.wait_ge(exped, u - 1)
                        rows = slice(P * t, P * t + rows_of(t))
                        for c in range(quads(t)):
                            cols = min(512, min(P * (t + 1), T) - 512 * c)
                            bank = scores(n, c, cols)
                            mm(bank, qn[:, h, rows], kn[:, h, 512 * c:512 * c + cols], start=True, stop=False)
                            last = mm(bank, qr[:, rows], kr[:, h, 512 * c:512 * c + cols], start=False, stop=True)
                        last.then_inc(scored, 1)

                    def mix(n):
                        t, h = units[n]
                        u = NU * j + n
                        pe.wait_ge(turned_out, NQ * j + qbase[n] + quads(t))
                        if u >= 1:
                            pe.wait_ge(oout, u)
                        for s in range(t + 1):
                            k = min(P, T - P * s)
                            last = mm(o_ps[:, 0:rows_of(t)], vv[0:k, s, h], pT[0:k, u % 2, s, 0:rows_of(t)],
                                      start=(s == 0), stop=(s == t))
                        last.then_inc(mixed, 1)

                    def turn(n):
                        t, h = units[n]
                        u, r = NU * j + n, rows_of(t)
                        pe.wait_ge(diag_done, u + 1)
                        for c in range(quads(t)):
                            q = NQ * j + qbase[n] + c
                            if q >= 2:
                                pe.wait_ge(turned_out, q - 1)
                            for s in range(4 * c, min(4 * c + 4, t + 1)):
                                k = min(P, T - P * s)
                                last = mm(t_ps[0:k, q % 2, P * (s % 4):P * (s % 4) + r], pr[0:r, u % 2, P * s:P * s + k],
                                          dg[0:r, u % 2, 0:r], start=True, stop=True)
                            last.then_inc(turned, 1)

                    score(0)
                    for n in range(NU):
                        if n + 1 < NU:
                            score(n + 1)
                        if n >= 1:
                            mix(n - 1)
                        turn(n)
                    mix(NU - 1)

            @block.scalar
            def _(act):

                def exponentials(j, n):
                    t, h = units[n]
                    u, r, b = NU * j + n, rows_of(t), n % 2
                    act.wait_ge(maxed, u + 1)
                    keys = min(P * (t + 1), T)
                    nc.scalar.activation(pr[0:r, b, 0:keys], scores(n, 0, keys), ACT.Exp, scale=ATT_SCALE,
                                         bias=nm[0:r, b:b + 1], accum_out=ls[0:r, b:b + 1]).then_inc(exped, 1)

                def evacuate(j, n):
                    t, h = units[n]
                    u, r = NU * j + n, rows_of(t)
                    if u >= 2:
                        act.wait_ge(mixed, u - 1)
                    for c in range(quads(t)):
                        q = NQ * j + qbase[n] + c
                        act.wait_ge(turned, q + 1)
                        full = [s for s in range(4 * c, min(4 * c + 4, t + 1)) if P * s + P <= T]
                        part = [s for s in range(4 * c, min(4 * c + 4, t + 1)) if P * s + P > T]
                        if full:
                            last = nc.scalar.copy(pT[:, u % 2, full[0]:full[-1] + 1, 0:r],
                                                  t_ps[:, q % 2, 0:P * len(full)].rearrange("p (s q) -> p s q", q=P)[:, :, 0:r])
                        if part:
                            s, k = part[0], T - P * part[0]
                            last = nc.scalar.copy(pT[0:k, u % 2, s, 0:r], t_ps[0:k, q % 2, P * (s % 4):P * (s % 4) + r])
                        last.then_inc(turned_out, 1)

                for j in range(NPAIR):
                    exponentials(j, 0)
                    for n in range(NU):
                        if n + 1 < NU:
                            exponentials(j, n + 1)
                        evacuate(j, n)

            @block.vector
            def _(dve):
                v = Chain(dve, v_own)
                nc.vector.memset(oT[:, :, T:], 0.0).then_inc(pads, 1)
                dve.wait_ge(mask_done, 2)
                dve.wait_ge(id_done, 2)
                for j in range(NPAIR):
                    if j:
                        dve.wait_ge(mixed, NU * j)
                    for n, (kind, h, c) in enumerate(order):
                        m = NJ * j + n
                        dve.wait_ge(pdone, m + 1)
                        bank = s_ps[:, 512 * (n % SB):512 * (n % SB + 1)]
                        if kind == "v":
                            v.hold(nc.vector.tensor_copy(vv[:, c].rearrange("p a b -> p (a b)"), bank[:, 0:2 * VD]))
                        else:
                            at, cols = CUTS[c]
                            if kind == "qn":
                                v.hold(nc.vector.tensor_copy(qn[:, h, at:at + cols], bank[:, 0:cols]))
                            elif kind == "kn":
                                v.hold(nc.vector.tensor_copy(kn[:, h, at:at + cols], bank[:, 0:cols]))
                            elif kind == "qa":
                                if j == 0:
                                    dve.wait_ge(tab_loaded, 32)
                                v(nc.vector.tensor_tensor(qr[:, at:at + cols], bank[:, 0:cols], cosT[:, at:at + cols], ALU.mult))
                            else:
                                v(nc.vector.tensor_tensor(rot[:, 0:cols], bank[:, 0:cols], sinT[:, at:at + cols], ALU.mult))
                                v(nc.vector.tensor_tensor(qr[:, at:at + cols], qr[:, at:at + cols], rot[:, 0:cols], ALU.add))
                        v.wait()
                        dve.sem_inc(pout, 1)
                    dve.sem_inc(ready, 1)

                    def biggest(n):
                        t, h = units[n]
                        r, b = rows_of(t), n % 2
                        dve.wait_ge(scored, NU * j + n + 1)
                        keys = min(P * (t + 1), T)
                        diag = scores(n, 0, keys)[:, P * t:keys]
                        v(nc.vector.tensor_tensor(diag, diag, mask[0:r, 0:keys - P * t], ALU.add))
                        v(nc.vector.tensor_reduce(mx[0:r, b:b + 1], scores(n, 0, keys), AX.X, ALU.max))
                        nc.vector.tensor_scalar(nm[0:r, b:b + 1], mx[0:r, b:b + 1], -ATT_SCALE, None,
                                                ALU.mult).then_inc(maxed, 1)

                    def diagonal(n):
                        u, r, b = NU * j + n, rows_of(units[n][0]), n % 2
                        dve.wait_ge(exped, u + 1)
                        v(nc.vector.reciprocal(rl[0:r, b:b + 1], ls[0:r, b:b + 1]))
                        if n >= 2:
                            dve.wait_ge(turned, NQ * j + qbase[n - 1])
                        nc.vector.tensor_scalar(dg[0:r, b], ident[0:r], rl[0:r, b:b + 1], None, ALU.mult).then_inc(diag_done, 1)

                    def output(n):
                        t, h = units[n]
                        dve.wait_ge(mixed, NU * j + n + 1)
                        nc.vector.tensor_copy(oT[:, 2 * j + h, P * t:P * t + rows_of(t)], o_ps[:, 0:rows_of(t)]).then_inc(oout, 1)

                    biggest(0)
                    for n in range(NU):
                        diagonal(n)
                        if n + 1 < NU:
                            biggest(n + 1)
                        if n >= 1:
                            output(n - 1)
                    output(NU - 1)

QUEUE_ROWS = SLOTS // P
SPILL_PAIRS = SPILL_BLOCKS // 2
EMPTY = 1 << 20
BIG = 1.0e30
ROUTE_CUT = TT * EXPERTS // 2


def route(nc, D, lg, gate, queue, spill, start_weights):
    with Phase(nc, "rt") as ph:
        slot_f = ph.sb("slot_f", [P, TT, 2])
        dest = ph.sb("dest", [P, TT, 2], I32)
        rk_ps = ph.ps("rk_ps", [P, 2, 512])
        zero_q = ph.sb("zero_q", [P, QUEUE_ROWS], I32)
        up = ph.sb("up", [P, P])
        ones = ph.sb("ones", [P, P])
        valid = ph.sb("valid", [P, TT])
        pri = ph.sb("pri", [P, 8])
        pri_i = ph.sb("pri_i", [P, 8], I32)
        first = ph.sb("first", [P, EXPERTS])
        first_i = ph.sb("first_i", [P, EXPERTS], I32)
        steps = ph.sb("steps", [P, PER_EXPERT_SPILL])
        steps_i = ph.sb("steps_i", [P, PER_EXPERT_SPILL], I32)
        blocks = ph.sb("blocks", [P, SPILL_BLOCKS])
        blocks_i = ph.sb("blocks_i", [P, SPILL_BLOCKS], I32)
        choice = ph.sb("choice", [P, TT, 2], I32)
        m8 = ph.sb("m8", [P, TT])
        cand = ph.sb("cand", [P, TT, 8])
        ohg = ph.sb("ohg", [P, TT, 8])
        gexp = ph.sb("gexp", [P, TT, 8])
        pg = ph.sb("pg", [P, TT])
        ein = ph.sb("ein", [P, TT, 8])
        oh = ph.sb("oh", [P, 2, TT, 8])
        top = ph.sb("top", [P, 2, TT])
        ed = ph.sb("ed", [P, TT])
        big = ph.sb("big", [P, TT, EXPERTS])
        chosen = ph.sb("chosen", [P, 2, TT, EXPERTS])
        both = ph.sb("both", [P, TT, EXPERTS])
        base = ph.sb("base", [P, TT + 1, EXPERTS])
        rank = ph.sb("rank", [P, TT, EXPERTS])
        over = ph.sb("over", [P, EXPERTS, PER_EXPERT_SPILL])
        nspill = ph.sb("nspill", [P, EXPERTS])
        send = ph.sb("send", [P, EXPERTS])
        jump = ph.sb("jump", [P, EXPERTS])
        owner = ph.sb("owner", [1, SPILL_BLOCKS, EXPERTS])
        owners = ph.sb("owners", [1, SPILL_BLOCKS + 1])
        ones_row = ph.sb("ones_row", [P, EXPERTS])
        names = ("const_done", "v_own", "soft_in", "soft_out", "diff_in", "diff_out", "picked", "ranked", "totals_out",
                 "totals_done", "slots_ready", "queue_zero", "scattered", "queue_loaded")
        (const_done, v_own, soft_in, soft_out, diff_in, diff_out, picked, ranked, totals_out, totals_done, slots_ready,
         queue_zero, scattered, queue_loaded) = (ph.sem(n) for n in names)
        table = D["table"]
        with nc.Block() as block:

            @block.sync
            def _(sp):
                start_weights(sp)

            @block.gpsimd
            def _(pool):
                g = nc.gpsimd
                for m in (up, ones, valid, zero_q):
                    g.memset(m[:], EMPTY if m is zero_q else 1.0).then_inc(const_done, 1)
                g.iota(pri_i[:], pattern=[[-1, 8]], base=8, channel_multiplier=0).then_inc(const_done, 1)
                g.iota(first_i[:], pattern=[[CAP, EXPERTS]], base=0, channel_multiplier=0).then_inc(const_done, 1)
                g.iota(steps_i[:], pattern=[[CAP, PER_EXPERT_SPILL]], base=CAP, channel_multiplier=0).then_inc(const_done, 1)
                g.iota(blocks_i[:], pattern=[[1, SPILL_BLOCKS]], base=0, channel_multiplier=0).then_inc(const_done, 1)
                g.iota(choice[:], pattern=[[2 * P, TT], [1, 2]], base=0, channel_multiplier=2).then_inc(const_done, 1)
                pool.wait_ge(const_done, 9)
                g.affine_select(out=up[:], in_=up[:], compare_op=ALU.is_gt, fill=0.0, base=0,
                                pattern=[[1, P]], channel_multiplier=-1).then_inc(const_done, 1)
                g.affine_select(out=valid[:], in_=valid[:], compare_op=ALU.is_gt, fill=0.0, base=T,
                                pattern=[[-P, TT]], channel_multiplier=-1).then_inc(const_done, 1)
                pool.dma_start(table.rearrange("(p q) a -> p (q a)", p=P), zero_q[:]).then_inc(queue_zero, 16)
                pool.wait_ge(queue_zero, 16)
                pool.wait_ge(slots_ready, 1)
                for t in range(TT):
                    for c in range(2):
                        g.indirect_dma_start(table[:, :], bass.IndirectOffsetOnAxis(ap=dest[0:rows_of(t), t, c:c + 1], axis=0),
                                             choice[0:rows_of(t), t, c:c + 1], None).then_inc(scattered, 16)
                pool.wait_ge(scattered, 16 * 2 * TT)
                pool.dma_start(queue[:, 1], table.rearrange("(q p) a -> p (q a)", p=P), allow_slow_non_contiguous=True).then_inc(queue_loaded, 16)
                pool.wait_ge(queue_loaded, 16)

            @block.scalar
            def _(act):
                act.wait_ge(soft_in, 1)
                nc.scalar.activation(gexp[:], gexp[:], ACT.Exp).then_inc(soft_out, 1)
                act.wait_ge(diff_in, 1)
                nc.scalar.activation(ed[:], ed[:], ACT.Exp).then_inc(diff_out, 1)

            @block.tensor
            def _(pe):
                pe.wait_ge(const_done, 11)
                pe.wait_ge(picked, 1)
                flat = both[:].rearrange("p t e -> p (t e)")
                for n, m in enumerate((ones, up)):
                    if n:
                        pe.wait_ge(totals_out, 1)
                    for c in range(2):
                        last = nc.tensor.matmul(rk_ps[:, c, 0:ROUTE_CUT], m[:], flat[:, ROUTE_CUT * c:ROUTE_CUT * c + ROUTE_CUT],
                                                start=True, stop=True)
                    last.then_inc(totals_done if n == 0 else ranked, 1)

            @block.vector
            def _(dve):
                v = Chain(dve, v_own)
                V = nc.vector
                tt, ts, stt, red = V.tensor_tensor, V.tensor_scalar, V.scalar_tensor_tensor, V.tensor_reduce
                dve.wait_ge(const_done, 11)
                v.hold(V.memset(ones_row[:], 1.0))
                for dst, src in ((pri, pri_i), (first, first_i), (steps, steps_i), (blocks, blocks_i)):
                    v.hold(V.tensor_copy(dst[:], src[:]))
                v.wait()

                def wide(x, n=8):
                    return x.unsqueeze(2).to_broadcast([P, TT, n])

                def row8(x):
                    return x.unsqueeze(1).to_broadcast([P, TT, 8])

                def first_max(values, best, hot):
                    v(red(best, values, AX.X, ALU.max))
                    v(tt(cand[:], values, wide(best), ALU.is_equal))
                    v(tt(cand[:], cand[:], row8(pri[:]), ALU.mult))
                    v(red(m8[:], cand[:], AX.X, ALU.max))
                    v(tt(hot, cand[:], wide(m8[:]), ALU.is_equal))

                groups = lg[:, :, 0:GROUPS]
                first_max(groups, pg[:], ohg[:])
                v(tt(gexp[:], groups, wide(pg[:]), ALU.subtract))
                dve.sem_inc(soft_in, 1)
                el = lg[:, :, GROUPS:].rearrange("p t (g e) -> p t g e", g=GROUPS)
                bg = big[:].rearrange("p t (g e) -> p t g e", g=GROUPS)
                for t in range(TT):
                    v.hold(tt(bg[:, t], el[:, t], ohg[:, t].unsqueeze(2).to_broadcast([P, GROUPS, 8]), ALU.mult))
                v.wait()
                v(red(ein[:], bg.rearrange("p t g e -> p t e g"), AX.X, ALU.add))
                first_max(ein[:], top[:, 0], oh[:, 0])
                v(stt(out=ein[:], in0=oh[:, 0], scalar=-BIG, in1=ein[:], op0=ALU.mult, op1=ALU.add))
                first_max(ein[:], top[:, 1], oh[:, 1])
                v(tt(ed[:], top[:, 1], top[:, 0], ALU.subtract))
                dve.sem_inc(diff_in, 1)
                dve.wait_ge(soft_out, 1)
                v(red(pg[:], gexp[:], AX.X, ALU.add))
                v(V.reciprocal(pg[:], pg[:]))
                dve.wait_ge(diff_out, 1)
                v(ts(m8[:], ed[:], 1.0, None, ALU.add))
                v(V.reciprocal(m8[:], m8[:]))
                v(tt(gate[:, :, 0], pg[:], m8[:], ALU.mult))
                v(tt(gate[:, :, 1], gate[:, :, 0], ed[:], ALU.mult))
                v(tt(ohg[:], ohg[:], wide(valid[:]), ALU.mult))
                for c in range(2):
                    for t in range(TT):
                        v.hold(tt(chosen[:, c, t].rearrange("p (g e) -> p g e", g=GROUPS),
                                  ohg[:, t].unsqueeze(2).to_broadcast([P, GROUPS, 8]),
                                  oh[:, c, t].unsqueeze(1).to_broadcast([P, GROUPS, 8]), ALU.mult))
                v.wait()
                v(tt(both[:], chosen[:, 0], chosen[:, 1], ALU.add))
                dve.sem_inc(picked, 1)
                dve.wait_ge(totals_done, 1)
                cut = lambda x, c: x.rearrange("p t e -> p (t e)")[:, ROUTE_CUT * c:ROUTE_CUT * c + ROUTE_CUT]
                for c in range(2):
                    v.hold(V.tensor_copy(cut(big[:], c), rk_ps[:, c, 0:ROUTE_CUT]))
                v(V.memset(base[:, 0], 0.0))
                dve.sem_inc(totals_out, 1)
                for t in range(TT):
                    v(tt(base[:, t + 1], base[:, t], big[:, t], ALU.add))
                dve.wait_ge(ranked, 1)
                for c in range(2):
                    v.hold(tt(cut(rank[:], c), rk_ps[:, c, 0:ROUTE_CUT], cut(base[:, 0:TT], c), ALU.add))
                v.wait()
                v(tt(over[:], base[:, TT].unsqueeze(2).to_broadcast([P, EXPERTS, PER_EXPERT_SPILL]),
                     steps[:].unsqueeze(1).to_broadcast([P, EXPERTS, PER_EXPERT_SPILL]), ALU.is_gt))
                v(red(nspill[:], over[:], AX.X, ALU.add))
                v(V.tensor_tensor_scan(send[:], ones_row[:], nspill[:], 0.0, ALU.mult, ALU.add))
                v(tt(jump[:], send[:], nspill[:], ALU.subtract))
                v(ts(jump[:], jump[:], float(CAP), float(MAIN_SLOTS - CAP), ALU.mult, ALU.add))
                v(tt(jump[:], jump[:], first[:], ALU.subtract))
                v(ts(big[:], rank[:], float(CAP), None, ALU.is_ge))
                for x, op in ((jump, ALU.mult), (first, ALU.add)):
                    v(tt(big[:], big[:], x[:].unsqueeze(1).to_broadcast([P, TT, EXPERTS]), op))
                v(tt(rank[:], rank[:], big[:], ALU.add))
                for c in range(2):
                    v(tt(big[:], rank[:], chosen[:, c], ALU.mult))
                    v(red(slot_f[:, :, c], big[:], AX.X, ALU.add))
                v(V.tensor_copy(dest[:], slot_f[:]))
                dve.sem_inc(slots_ready, 1)
                v(tt(owner[:], send[0:1].unsqueeze(1).to_broadcast([1, SPILL_BLOCKS, EXPERTS]),
                     blocks[0:1].unsqueeze(2).to_broadcast([1, SPILL_BLOCKS, EXPERTS]), ALU.is_le))
                v(red(owners[:, 0:SPILL_BLOCKS], owner[:], AX.X, ALU.add))
                v(ts(owners[:, 0:SPILL_BLOCKS], owners[:, 0:SPILL_BLOCKS], float(EXPERTS - 1), None, ALU.min))
                v(V.tensor_copy(owners[:, SPILL_BLOCKS:], send[0:1, EXPERTS - 1:]))
                v(V.tensor_copy(spill[:], owners[:]))
                dve.wait_ge(queue_loaded, 16)
                v(ts(queue[:, 0], queue[:, 1], 1, None, ALU.arith_shift_right))


def expert_loads(nc, D, layer, wgu, wd):
    wg_d, wu_d, wd_d = D["w_gate_2"][layer], D["w_up_2"][layer], D["w_down_2"][layer]

    def gate_up(sp, b, loaded, pair):
        for n, e in enumerate(pair):
            for c, src in enumerate((wg_d, wu_d)):
                sp.dma_start(wgu[:, b, n, c], src[bass.ds(e, 1)].rearrange("a (p k) f -> (a p) k f", k=KT)
                             ).then_inc(loaded, 16)

    def down(sp, b, loaded, pair):
        for n, e in enumerate(pair):
            sp.dma_start(wd[:, b, n], wd_d[bass.ds(e, 1)].rearrange("a (p k) f -> (a p) k f", k=2)
                         ).then_inc(loaded, 16)

    return gate_up, down


def experts(nc, D, layer, queue, spill, wgu, wd, gu_loaded, d_loaded):
    gate_up_loads, down_loads = expert_loads(nc, D, layer, wgu, wd)
    with Phase(nc, "ex") as ph:
        ib = ph.sb("ib", [P, 2, 2], I32)
        xe = ph.sb("xe", [P, 2, DM])
        xT = ph.sb("xT", [P, 2, KT, P])
        sg = ph.sb("sg", [P, 2, DE])
        hs = ph.sb("hs", [P, 2, DE])
        hT = ph.sb("hT", [P, 2, 2, P])
        ysb = ph.sb("ysb", [P, 2, DM])
        ident = ph.sb("ident", [P, P])
        x_ps = ph.ps("x_ps", [P, 2, 512])
        h_ps = ph.ps("h_ps", [P, 2, 512])
        ht_ps = ph.ps("ht_ps", [P, 2, 512])
        y_ps = ph.ps("y_ps", [P, 2, 512])
        id_done = ph.sem("id_done")
        xe_clear = ph.sem("xe_clear")
        names = ["in_ready", "out_ready", "x_loaded", "x_turned", "xT_out",
                 "h_done", "silu_done", "h_out", "h_turned", "hT_out", "y_done", "y_out", "y_stored"]
        S = [{n: ph.sem(f"{n}{b}") for n in names} for b in range(3)]
        for b in range(2):
            S[b]["gu_loaded"], S[b]["d_loaded"] = gu_loaded[b], d_loaded[b]
        for n in ("gu_loaded", "d_loaded", "w_used", "x_used", "seen"):
            S[2][n] = ph.sem(f"{n}2")
        hn_dram, y_rows = D["hn"], D["ys"].rearrange("t (c d) -> (t c) d", c=2)

        def gather(pool, b, s, pair):
            pool.sem_inc(s["in_ready"], 1)
            nc.gpsimd.tensor_copy(ib[:, b, 0:1], queue[:, 0, bass.ds(pair, 1)]).then_inc(s["in_ready"], 1)
            pool.wait_ge(s["in_ready"], 2)
            nc.gpsimd.indirect_dma_start(xe[:, b], None, hn_dram[:, :], bass.IndirectOffsetOnAxis(ap=ib[:, b, 0:1], axis=0),
                                         bounds_check=T - 1, oob_is_err=False).then_inc(s["x_loaded"], 16)
            pool.sem_clear(s["in_ready"])

        def scatter(pool, b, s, pair):
            pool.sem_inc(s["out_ready"], 1)
            nc.gpsimd.tensor_copy(ib[:, b, 1:2], queue[:, 1, bass.ds(pair, 1)]).then_inc(s["out_ready"], 1)
            pool.wait_ge(s["out_ready"], 2)
            nc.gpsimd.indirect_dma_start(y_rows[:, :], bass.IndirectOffsetOnAxis(ap=ib[:, b, 1:2], axis=0), ysb[:, b], None,
                                         bounds_check=2 * T - 1, oob_is_err=False).then_inc(s["y_stored"], 16)
            pool.sem_clear(s["out_ready"])

        def products(pe, b, s, count):
            pe.wait_ge(s["x_loaded"], 16 * count)
            for k in range(KT):
                last = nc.tensor.transpose(x_ps[:, k // 4, P * (k % 4):P * (k % 4) + P], xe[:, b, k::KT], ident[:])
            last.then_inc(s["x_turned"], 1)
            pe.wait_ge(s["xT_out"], 2 * count)
            pe.wait_ge(s["gu_loaded"], 64 * count)
            for k in range(KT):
                for n in range(2):
                    half = slice(CAP * n, CAP * n + CAP)
                    last = nc.tensor.matmul(h_ps[half, b].rearrange("p (a b) -> p a b", a=2), xT[:, b, k, half],
                                            wgu[:, b, n, :, k], start=(k == 0), stop=(k == KT - 1))
            last.then_inc(s["h_done"], 1)
            pe.wait_ge(s["h_out"], count)
            for k in range(2):
                last = nc.tensor.transpose(ht_ps[:, b, P * k:P * k + P], hs[:, b, k::2], ident[:])
            last.then_inc(s["h_turned"], 1)
            pe.wait_ge(s["hT_out"], count)
            pe.wait_ge(s["d_loaded"], 32 * count)
            for c in range(2):
                for k in range(2):
                    for n in range(2):
                        half = slice(CAP * n, CAP * n + CAP)
                        last = nc.tensor.matmul(y_ps[half, c], hT[:, b, k, half], wd[:, b, n, k, 512 * c:512 * c + 512],
                                                start=(k == 0), stop=(k == 1))
            last.then_inc(s["y_done"], 1)
            pe.wait_ge(s["y_out"], 2 * count)

        def scalar_part(act, b, s, count, stored):
            act.wait_ge(s["x_turned"], count)
            nc.scalar.copy(xT[:, b, 0:4].rearrange("p k q -> p (k q)"), x_ps[:, 0]).then_inc(s["xT_out"], 1)
            act.wait_ge(s["h_done"], count)
            nc.scalar.activation(sg[:, b], h_ps[:, b, 0:DE], ACT.Silu).then_inc(s["silu_done"], 1)
            act.wait_ge(s["h_turned"], count)
            nc.scalar.copy(hT[:, b].rearrange("p k q -> p (k q)"), ht_ps[:, b, 0:2 * P]).then_inc(s["hT_out"], 1)
            stored()
            act.wait_ge(s["y_done"], count)
            nc.scalar.copy(ysb[:, b, 0:512], y_ps[:, 0]).then_inc(s["y_out"], 1)

        def vector_part(dve, b, s, count, stored):
            dve.wait_ge(s["x_turned"], count)
            nc.vector.tensor_copy(xT[:, b, 4:8].rearrange("p k q -> p (k q)"), x_ps[:, 1]).then_inc(s["xT_out"], 1)
            dve.wait_ge(s["silu_done"], count)
            nc.vector.tensor_tensor(hs[:, b], sg[:, b], h_ps[:, b, DE:], ALU.mult).then_inc(s["h_out"], 1)
            stored()
            dve.wait_ge(s["y_done"], count)
            nc.vector.tensor_copy(ysb[:, b, 512:], y_ps[:, 1]).then_inc(s["y_out"], 1)

        MAIN = PAIRS_M // 2
        with nc.Block() as block:

            @block.sync
            def _(sp):
                with sp.Fori(0, MAIN - 1) as i:
                    for b in range(2):
                        s = S[b]
                        pair = [4 * (i + 1) + 2 * b, 4 * (i + 1) + 2 * b + 1]
                        sp.wait_ge(s["h_done"], i + 1)
                        gate_up_loads(sp, b, s["gu_loaded"], pair)
                        sp.wait_ge(s["y_done"], i + 1)
                        down_loads(sp, b, s["d_loaded"], pair)

            @block.gpsimd
            def _(pool):
                make_identity(nc, pool, ident, id_done)
                pool.wait_ge(xe_clear, 1)
                for b in range(2):
                    gather(pool, b, S[b], b)
                with pool.Fori(0, MAIN - 1) as i:
                    for b in range(2):
                        s = S[b]
                        pool.wait_ge(s["x_turned"], i + 1)
                        gather(pool, b, s, 2 * (i + 1) + b)
                        pool.wait_ge(s["y_out"], 2 * i + 2)
                        scatter(pool, b, s, 2 * i + b)
                for b in range(2):
                    pool.wait_ge(S[b]["y_out"], 2 * MAIN)
                    scatter(pool, b, S[b], PAIRS_M - 2 + b)
                for b in range(2):
                    pool.wait_ge(S[b]["y_stored"], 16 * MAIN)

            @block.tensor
            def _(pe):
                pe.wait_ge(id_done, 2)
                with pe.Fori(0, MAIN) as i:
                    for b in range(2):
                        products(pe, b, S[b], i + 1)

            @block.scalar
            def _(act):
                for b in range(2):
                    scalar_part(act, b, S[b], 1, lambda: None)
                with act.Fori(1, MAIN) as i:
                    for b in range(2):
                        scalar_part(act, b, S[b], i + 1, lambda: act.wait_ge(S[b]["y_stored"], 16 * i))

            @block.vector
            def _(dve):
                nc.vector.memset(xe[:], 0.0).then_inc(xe_clear, 1)
                for b in range(2):
                    vector_part(dve, b, S[b], 1, lambda: None)
                with dve.Fori(1, MAIN) as i:
                    for b in range(2):
                        vector_part(dve, b, S[b], i + 1, lambda: dve.wait_ge(S[b]["y_stored"], 16 * i))

        s = S[2]
        with nc.Block() as block:

            def spilled(eng):
                return eng.value_load(spill[0:1, SPILL_BLOCKS:], min_val=0, max_val=SPILL_BLOCKS)

            @block.sync
            def _(sp):
                total = spilled(sp)
                with sp.If(0 < total):
                    with sp.Fori(0, SPILL_PAIRS) as i:
                        with sp.If(2 * i < total):
                            sp.wait_ge(s["w_used"], i + 1)
                            pair = [sp.value_load(spill[0:1, bass.ds(2 * i + n, 1)], min_val=0, max_val=EXPERTS - 1)
                                    for n in range(2)]
                            gate_up_loads(sp, 0, s["gu_loaded"], pair)
                            down_loads(sp, 0, s["d_loaded"], pair)

            @block.gpsimd
            def _(pool):
                total = spilled(pool)
                with pool.If(0 < total):
                    with pool.Fori(0, SPILL_PAIRS) as i:
                        with pool.If(2 * i < total):
                            pool.wait_ge(s["x_used"], i + 1)
                            gather(pool, 0, s, PAIRS_M + i)
                            pool.wait_ge(s["y_out"], 2 * i + 2)
                            scatter(pool, 0, s, PAIRS_M + i)
                            pool.wait_ge(s["y_stored"], 16 * i + 16)
                            pool.sem_inc(s["seen"], 1)

            @block.tensor
            def _(pe):
                for n in ("w_used", "x_used", "seen"):
                    pe.sem_inc(s[n], 1)
                total = spilled(pe)
                with pe.If(0 < total):
                    with pe.Fori(0, SPILL_PAIRS) as i:
                        with pe.If(2 * i < total):
                            products(pe, 0, s, i + 1)
                            for n in ("w_used", "x_used"):
                                pe.sem_inc(s[n], 1)

            @block.scalar
            def _(act):
                total = spilled(act)
                with act.If(0 < total):
                    with act.Fori(0, SPILL_PAIRS) as i:
                        with act.If(2 * i < total):
                            scalar_part(act, 0, s, i + 1, lambda: act.wait_ge(s["seen"], i + 1))

            @block.vector
            def _(dve):
                total = spilled(dve)
                with dve.If(0 < total):
                    with dve.Fori(0, SPILL_PAIRS) as i:
                        with dve.If(2 * i < total):
                            vector_part(dve, 0, s, i + 1, lambda: dve.wait_ge(s["seen"], i + 1))


def gathered_sum(nc, v, y, gate, h, out, t):
    v(nc.vector.scalar_tensor_tensor(out=out, in0=y[:, 0:DM], scalar=gate[:, t, 0:1], in1=h, op0=ALU.mult, op1=ALU.add))
    v(nc.vector.scalar_tensor_tensor(out=out, in0=y[:, DM:], scalar=gate[:, t, 1:2], in1=out, op0=ALU.mult, op1=ALU.add))


def combine_for_latents(nc, D, gate, h_in, h_out, hq, hk):
    with Phase(nc, "cl") as ph:
        NBUF, NOUT = 3, 4
        hb = ph.sb("hb", [P, NBUF, DM])
        yb = ph.sb("yb", [P, NBUF, 2 * DM])
        ho = ph.sb("ho", [P, NOUT, DM])
        yb_clear, v_own, made = ph.sem("yb_clear"), ph.sem("v_own"), ph.sem("made")
        loaded = [ph.sem(f"h{n}_loaded") for n in range(NBUF)]
        stored = [ph.sem(f"h{n}_stored") for n in range(NOUT)]
        norm = NormTurn(nc, ph, [hq, hk], [D["norm_mix_g_t"][1], D["kv_norm_g_t"]], [(P * t, P) for t in range(TT)],
                        lambda n: ho[:, n % NOUT], made)
        with nc.Block() as block:

            @block.sync
            def _(sp):
                norm.load(sp)
                for t in range(TT):
                    if t >= NBUF:
                        sp.wait_ge(made, t - NBUF + 1)
                    b, r = t % NBUF, rows_of(t)
                    if b == (TT - 1) % NBUF:
                        sp.wait_ge(yb_clear, 1)
                    sp.dma_start(hb[:, b], h_in[P * t:P * t + P]).then_inc(loaded[b], 16)
                    sp.dma_start(yb[0:r, b], D["ys"][P * t:P * t + r]).then_inc(loaded[b], 16)

            @block.gpsimd
            def _(pool):
                norm.constants(pool)
                for t in range(TT):
                    pool.wait_ge(made, t + 1)
                    pool.dma_start(h_out[P * t:P * t + P], ho[:, t % NOUT]).then_inc(stored[t % NOUT], 16)
                for b in range(NOUT):
                    pool.wait_ge(stored[b], 16 * ((TT + NOUT - 1 - b) // NOUT))

            @block.tensor
            def _(pe):
                for t in range(TT):
                    norm.turn(pe, t)

            @block.scalar
            def _(act):
                for t in range(TT):
                    norm.square(act, t)

            @block.vector
            def _(dve):
                v = Chain(dve, v_own)
                nc.vector.memset(yb[:, (TT - 1) % NBUF], 0.0).then_inc(yb_clear, 1)
                for t in range(TT):
                    dve.wait_ge(loaded[t % NBUF], 32 * (t // NBUF + 1))
                    if t >= NOUT:
                        dve.wait_ge(norm.scaled, t - NOUT + 1)
                        dve.wait_ge(stored[t % NOUT], 16 * (t // NOUT))
                    gathered_sum(nc, v, yb[:, t % NBUF], gate, hb[:, t % NBUF], ho[:, t % NOUT], t)
                    dve.sem_inc(made, 1)
                    if t >= 1:
                        norm.scale(dve, v, t - 1)
                    if t >= 2:
                        norm.out(dve, t - 2)
                norm.out(dve, TT - 2)
                norm.scale(dve, v, TT - 1)
                norm.out(dve, TT - 1)


def combine_out(nc, D, gate, h_in):
    with Phase(nc, "co") as ph:
        NBUF, NOUT = 3, 4
        hb = ph.sb("hb", [P, NBUF, DM])
        yb = ph.sb("yb", [P, NBUF, 2 * DM])
        ho = ph.sb("ho", [P, NOUT, DM])
        gb = ph.sb("gb", [P, DM])
        sq = ph.sb("sq", [P, DM], mybir.dt.bfloat16)
        ss, rt, rs = (ph.sb(n, [P, 2]) for n in ("ss", "rt", "rs"))
        eps = ph.sb("eps", [P, 1])
        g_loaded, eps_done, yb_clear, made, squared, rooted, scaled, v_own = (
            ph.sem(n) for n in ("g_loaded", "eps_done", "yb_clear", "made", "squared", "rooted", "scaled", "v_own"))
        loaded = [ph.sem(f"h{n}_loaded") for n in range(NBUF)]
        stored = [ph.sem(f"o{n}_stored") for n in range(NOUT)]
        with nc.Block() as block:

            @block.sync
            def _(sp):
                sp.dma_start(gb[:], D["final_norm_g_2"].partition_broadcast(P)).then_inc(g_loaded, 16)
                for t in range(TT):
                    if t >= NBUF:
                        sp.wait_ge(made, t - NBUF + 1)
                    b, r = t % NBUF, rows_of(t)
                    if b == (TT - 1) % NBUF:
                        sp.wait_ge(yb_clear, 1)
                    sp.dma_start(hb[:, b], h_in[P * t:P * t + P]).then_inc(loaded[b], 16)
                    sp.dma_start(yb[0:r, b], D["ys"][P * t:P * t + r]).then_inc(loaded[b], 16)

            @block.gpsimd
            def _(pool):
                for t in range(TT):
                    pool.wait_ge(scaled, t + 1)
                    skip = 0 if t else META
                    pool.dma_start(D["out"][P * t - META + skip:min(P * t - META + P, SEQ)], ho[skip:rows_of(t), t % NOUT]
                                   ).then_inc(stored[t % NOUT], 16)
                for b in range(NOUT):
                    pool.wait_ge(stored[b], 16 * ((TT + NOUT - 1 - b) // NOUT))

            @block.scalar
            def _(act):
                act.wait_ge(eps_done, 1)
                for t in range(TT):
                    b = t % 2
                    act.wait_ge(made, t + 1)
                    if t >= 2:
                        act.wait_ge(scaled, t - 1)
                    nc.scalar.activation(sq[:], ho[:, t % NOUT], ACT.Square, accum_out=ss[:, b:b + 1]).then_inc(squared, 1)
                    act.wait_ge(squared, t + 1)
                    nc.scalar.activation(rt[:, b:b + 1], ss[:, b:b + 1], ACT.Sqrt, scale=1.0 / DM,
                                         bias=eps[:]).then_inc(rooted, 1)

            @block.vector
            def _(dve):
                v = Chain(dve, v_own)
                nc.vector.memset(eps[:], NORM_EPS).then_inc(eps_done, 1)
                nc.vector.memset(yb[:, (TT - 1) % NBUF], 0.0).then_inc(yb_clear, 1)
                dve.wait_ge(g_loaded, 16)

                def scale(t):
                    b = t % 2
                    dve.wait_ge(rooted, t + 1)
                    v(nc.vector.reciprocal(rs[:, b:b + 1], rt[:, b:b + 1]))
                    v(nc.vector.scalar_tensor_tensor(out=ho[:, t % NOUT], in0=ho[:, t % NOUT], scalar=rs[:, b:b + 1], in1=gb[:],
                                                     op0=ALU.mult, op1=ALU.mult))
                    dve.sem_inc(scaled, 1)

                for t in range(TT):
                    dve.wait_ge(loaded[t % NBUF], 32 * (t // NBUF + 1))
                    if t >= NOUT:
                        dve.wait_ge(stored[t % NOUT], 16 * (t // NOUT))
                    gathered_sum(nc, v, yb[:, t % NBUF], gate, hb[:, t % NBUF], ho[:, t % NOUT], t)
                    dve.sem_inc(made, 1)
                    if t >= 1:
                        scale(t - 1)
                scale(TT - 1)


def scratch(nc, D):
    for name, shape, dt in (("h0", (TP, DM), F32), ("h1", (TP, DM), F32), ("h2", (TP, DM), F32), ("h3", (TP, DM), F32),
                            ("hn", (TP, DM), F32), ("ys", (T, 2 * DM), F32), ("table", (SLOTS, 1), I32)):
        if name not in D:
            D[name] = nc.dram_tensor(f"s_{name}", shape, dt, kind="Internal").ap()


def moe(nc, D, layer, lg, gate, wgu):
    with Phase(nc, "mo") as ph:
        wd = ph.sb("wd", [P, 2, 2, 2, DM])
        queue = ph.sb("queue", [P, 2, QUEUE_ROWS], I32)
        spill = ph.sb("spill", [1, SPILL_BLOCKS + 1], I32)
        gu_loaded = [ph.sem(f"gu{b}_loaded") for b in range(2)]
        d_loaded = [ph.sem(f"d{b}_loaded") for b in range(2)]
        gate_up, down = expert_loads(nc, D, layer, wgu, wd)

        def start_weights(sp):
            for b in range(2):
                gate_up(sp, b, gu_loaded[b], [2 * b, 2 * b + 1])
                down(sp, b, d_loaded[b], [2 * b, 2 * b + 1])

        route(nc, D, lg, gate, queue, spill, start_weights)
        experts(nc, D, layer, queue, spill, wgu, wd, gu_loaded, d_loaded)


def program_parts(nc, D, arena, gate):
    def part(first_tile, *shape):
        n = int(np.prod(shape))
        flat = arena[:, SEQ * first_tile:SEQ * first_tile + n]
        names = "abcde"[:len(shape)]
        return flat.rearrange(f"p ({' '.join(names)}) -> p {' '.join(names)}", **dict(zip(names, shape)))

    proj = part(0, PROJ_TILES, SEQ)
    zT, hnT = part(0, KT, TP), part(9, KT, TP)
    wgu = part(0, 2, 2, 2, KT, DE)
    lg = part(PROJ_TILES - 1, TT, LG)
    hq, hk = part(0, KT, TP), part(9, KT, TP)
    oT = part(0, HEADS, TP)
    first(nc, D, proj)
    first_out(nc, D, proj, hnT)
    conv_mixer(nc, D, hnT, zT)
    back_and_route(nc, D, 0, zT, D["conv_w_out_2"], D["h0"], D["h1"], lg)
    moe(nc, D, 0, lg, gate, wgu)
    with Phase(nc, "lt") as ph:
        cq = ph.sb("cq", [P, QR // P, TP])
        ckv = ph.sb("ckv", [P, KVR // P, TP])
        kr = ph.sb("kr", [P, 2, T])
        combine_for_latents(nc, D, gate, D["h1"], D["h2"], hq, hk)
        latents(nc, D, hq, hk, cq, ckv, kr)
        heads(nc, D, cq, ckv, kr, oT)
    back_and_route(nc, D, 1, oT, D["w_o_2"], D["h2"], D["h3"], lg)
    moe(nc, D, 1, lg, gate, wgu)
    combine_out(nc, D, gate, D["h3"])


def program(nc, D):
    Phase.seen.clear()
    scratch(nc, D)
    with Phase(nc, "all") as ph:
        arena = ph.sb("arena", [P, PROJ_TILES * SEQ])
        gate = ph.sb("gate", [P, TT, 2])
        program_parts(nc, D, arena, gate)


def by_partition(a, *order):
    return np.ascontiguousarray(a.reshape(-1, P, *a.shape[1:]).swapaxes(0, 1))


def lay_out(inputs):
    a = {k: np.ascontiguousarray(np.asarray(v)) for k, v in inputs.items()}
    o = {n: a[n] for n in ("meta_tokens_2", "norm_ffn_g_2", "w_gate_2", "w_up_2", "w_down_2", "final_norm_g_2")}
    for n in ("x", "attn_sinks", "lru_wa", "lru_wx", "rwkv_w2", "rwkv_a2", "w_out", "ln_g", "ln_b", "conv_w_out_2", "w_o_2"):
        o[n] = a[n][0]
    o["xT"] = by_partition(a["x"][0].T)
    w = a["w_in"][0]
    q, k, v, ga, xb, gb, c, gc = np.split(w, np.cumsum([512, 128, 128, 512, 256, 256, 832, 256])[:-1], axis=1)
    swapped = np.concatenate([k[:, HALF:], k[:, :HALF]], 1)
    tiles = np.concatenate([ga, gb, gc, q, k, swapped, xb, c, np.zeros((DM, HALF + P), w.dtype)], 1)
    o["w_in_t"] = np.ascontiguousarray(tiles.reshape(KT, P, PROJ_TILES + 1, P).transpose(2, 1, 0, 3))
    o["w_v_t"] = by_partition(v)

    def vectors(rows):
        return np.ascontiguousarray(np.stack(rows).reshape(-1, 2, P).transpose(2, 1, 0))

    o["lru_vec"] = vectors([*a["conv_w"][0], a["conv_b"][0], a["lru_ba"][0], a["lru_bx"][0], a["lru_lambda"][0]])
    mu = a["rwkv_mu"][0]
    o["rwkv_vec"] = vectors([mu[0:256], mu[256:512], mu[512:768], a["rwkv_w0"][0], a["rwkv_a0"][0], a["rwkv_kk"][0],
                             a["rwkv_ka"][0], a["rwkv_rk"][0].reshape(-1), a["rwkv_gn_w"][0], a["rwkv_gn_b"][0]])
    o["rwkv_mu_lo"] = np.ascontiguousarray(mu[768:].reshape(HALF, 1))
    o["norm_mix_g_t"] = np.stack([by_partition(g) for g in a["norm_mix_g_2"]])
    o["kv_norm_g_t"] = by_partition(a["kv_norm_g_2"])
    o["conv_w_in_t"] = np.ascontiguousarray(a["conv_w_in_2"][0].reshape(KT, P, 3, KT, P).transpose(3, 1, 2, 0, 4))
    o["conv_w_2_t"] = np.ascontiguousarray(a["conv_w_2"][0].reshape(3, KT, P).transpose(2, 1, 0))
    o["w_dq_t"] = by_partition(a["w_dq_2"][0])
    dkv = a["w_dkv_2"]
    o["w_dkv_t"] = by_partition(dkv[:, :KVR])
    rope = dkv[:, KVR:]
    turned = np.concatenate([rope[:, ROPE // 2:], rope[:, :ROPE // 2]], 1)
    o["w_rope_t"] = by_partition(np.stack([np.concatenate([rope, rope], 1), np.concatenate([turned, turned], 1)], 1))
    o["cq_g_t"] = by_partition(a["cq_norm_g_2"][0])
    o["ckv_g_t"] = by_partition(a["ckv_norm_g_2"])
    inv = np.float32(10000.0) ** (-np.arange(0, ROPE, 2, dtype=np.float32) / np.float32(ROPE))
    angle = np.arange(T, dtype=np.float32)[:, None] * inv[None, :]
    cos, sin = np.cos(angle).T, np.sin(angle).T
    o["cos_t"] = np.ascontiguousarray(np.concatenate([cos] * 4, 0))
    o["sin_t"] = np.ascontiguousarray(np.concatenate([-sin, sin] * 2, 0))
    uq = a["w_uq_2"][0].reshape(QR // P, P, HEADS // 2, 2, NOPE + ROPE)
    nope, rq = uq[..., :NOPE], uq[..., NOPE:]
    rs = np.concatenate([rq[..., ROPE // 2:], rq[..., :ROPE // 2]], -1)
    o["w_uq_t"] = np.ascontiguousarray(np.stack(
        [nope[:, :, :, 0], nope[:, :, :, 1], rq.reshape(QR // P, P, HEADS // 2, P), rs.reshape(QR // P, P, HEADS // 2, P)],
        3).transpose(2, 1, 0, 3, 4))
    ukv = a["w_ukv_2"].reshape(KVR // P, P, HEADS // 2, 2, 2, P)
    o["w_ukv_t"] = np.ascontiguousarray(ukv.transpose(2, 1, 0, 4, 3, 5).reshape(HEADS // 2, P, KVR // P, 4, P))
    o["w_route_t"] = np.stack([by_partition(np.concatenate([g, e], 1)) for g, e in zip(a["w_grp_2"], a["w_exp_2"])])
    return o


def kernel(**inputs):
    import concourse.bacc as bacc
    from concourse.bass_utils import run_bass_kernel_spmd

    nc = bacc.Bacc("TRN2", target_bir_lowering=False, num_devices=1)
    arrays = {f"in_{n}": x for n, x in lay_out(inputs).items()}
    D = {n[3:]: nc.dram_tensor(n, x.shape, mybir.dt.from_np(x.dtype), kind="ExternalInput").ap() for n, x in arrays.items()}
    D["out"] = nc.dram_tensor("out_0", (SEQ, DM), F32, kind="ExternalOutput").ap()
    program(nc, D)
    r = run_bass_kernel_spmd(nc, [arrays], core_ids=[0])
    return r.results[0]["out_0"].reshape(1, SEQ, DM)
```
